# Optimizing a Trainium2 kernel written in Bass

```python
import jax, jax.numpy as jnp
from jax import lax
import numpy as np

D_MODEL = 2048
BATCH = 1
SEQ = 256
DEPTH = 1
DEC_BATCH = 8
DEC_SEQ = 4
PAST_LEN = 2048
PAGE_SIZE = 128

D_RNN = D_MODEL
RG_BLOCKS = 16
RG_BW = D_RNN // RG_BLOCKS
CONV_W = 4
RG_C = 8.0
HEAD = 64
D_ATT = D_MODEL
N_HEADS = D_ATT // HEAD
R_W = 96
R_A = 96
R_G = 256
GN_EPS = 64e-5
D_FF = 4 * D_MODEL
D_PLE = 256
EPS = 1e-6
OFF_RGX = 0
OFF_RGG = OFF_RGX + D_RNN
OFF_RWKV = OFF_RGG + D_RNN
N_RWKV = 3 * D_ATT + R_W + R_A + R_G
OFF_GATE = OFF_RWKV + N_RWKV
N_IN = OFF_GATE + 2 * D_MODEL

kernel_name = "hawk_rwkv7_parallel_gated_step"

def _rmsnorm(x, g):
    xf = x.astype(jnp.float32)
    y = xf * lax.rsqrt(jnp.mean(xf * xf, axis=-1, keepdims=True) + EPS)
    return (y * g.astype(jnp.float32)).astype(x.dtype)

def _causal_conv(u, buf, w, b):
    T = u.shape[1]
    ext = jnp.concatenate([buf, u], axis=1)
    y = b + sum(ext[:, j:j + T] * w[j] for j in range(CONV_W))
    return y, ext[:, -(CONV_W - 1):]

def _rg_lru(xc, h0, first, wa, ba, wx, bx, lam):
    B, T, _ = xc.shape
    f32 = jnp.float32
    xb = xc.reshape(B, T, RG_BLOCKS, RG_BW)
    r = jax.nn.sigmoid(jnp.einsum('btnc,ncd->btnd', xb, wa) + ba).reshape(B, T, D_RNN).astype(f32)
    i = jax.nn.sigmoid(jnp.einsum('btnc,ncd->btnd', xb, wx) + bx).reshape(B, T, D_RNN).astype(f32)
    log_a = -RG_C * r * jax.nn.softplus(-lam.astype(f32))
    a = jnp.exp(log_a)
    mult = jnp.sqrt(-jnp.expm1(2.0 * log_a))
    mult = jnp.where(first[None, :, None], 1.0, mult)
    b = mult * (i * xc.astype(f32))

    def comb(l, rr):
        return (l[0] * rr[0], rr[0] * l[1] + rr[1])

    a_cum, b_cum = lax.associative_scan(comb, (a, b), axis=1)
    h = b_cum + a_cum * h0.astype(f32)[:, None]
    return h, h[:, -1]

def _rwkv7(z, S0, w0, w2, a0, a2, g2, k_kk, k_a, r_k, gn_w, gn_b):
    B, T, _ = z.shape
    f32 = jnp.float32
    z = z.astype(f32)
    r = z[..., :D_ATT]
    k = z[..., D_ATT:2 * D_ATT]
    v = z[..., 2 * D_ATT:3 * D_ATT]
    o = 3 * D_ATT
    wd = z[..., o:o + R_W]
    ad = z[..., o + R_W:o + R_W + R_A]
    gd = z[..., o + R_W + R_A:]
    w = -jax.nn.softplus(-(w0 + jnp.tanh(wd) @ w2)) - 0.5
    decay = jnp.exp(-jnp.exp(w))
    a = jax.nn.sigmoid(a0 + ad @ a2)
    g = jax.nn.sigmoid(gd) @ g2
    hd = lambda t: t.reshape(B, T, N_HEADS, HEAD)
    kk = hd(k * k_kk)
    kk = kk * lax.rsqrt(jnp.maximum(jnp.sum(kk * kk, axis=-1, keepdims=True), 1e-24))
    k = k * (1.0 + (a - 1.0) * k_a)
    r_h, k_h, v_h, w_h, a_h = hd(r), hd(k), hd(v), hd(decay), hd(a)
    b_h = kk * a_h

    def step(S, inp):
        r_t, k_t, v_t, w_t, kk_t, b_t = inp
        sa = jnp.einsum('bhij,bhj->bhi', S, -kk_t)
        S = (S * w_t[:, :, None, :] + sa[..., None] * b_t[:, :, None, :]
             + v_t[..., None] * k_t[:, :, None, :])
        y = jnp.einsum('bhij,bhj->bhi', S, r_t)
        return S, y

    tm = lambda t: jnp.moveaxis(t, 1, 0)
    S_last, y = lax.scan(step, S0.astype(f32), (tm(r_h), tm(k_h), tm(v_h), tm(w_h), tm(kk), tm(b_h)))
    y = jnp.moveaxis(y, 0, 1)
    mu = jnp.mean(y, axis=-1, keepdims=True)
    var = jnp.mean(jnp.square(y - mu), axis=-1, keepdims=True)
    y = ((y - mu) * lax.rsqrt(var + GN_EPS)).reshape(B, T, D_ATT) * gn_w + gn_b
    bonus = jnp.sum(r_h * k_h * r_k, axis=-1, keepdims=True) * v_h
    out = (y + bonus.reshape(B, T, D_ATT)) * g
    return out, S_last

def _layer(x, p_i, cbuf, h0, S0, xprev, first,
           norm_mix, w_in, conv_w, conv_b, rg_wa, rg_ba, rg_wx, rg_bx, rg_lam, w_rg_o,
           mu_shift, rw_w0, rw_w2, rw_a0, rw_a2, rw_g2, rw_kk, rw_ka, rw_rk, rw_gn_w, rw_gn_b,
           w_rw_o, w_o, norm_ffn, w_up, w_down, norm_ple, w_ple_gate, w_ple):
    dt = x.dtype
    xn = _rmsnorm(x, norm_mix)
    P = xn @ w_in
    prw = P[..., OFF_RWKV:OFF_GATE]
    prev_row = (xprev.astype(dt) @ w_in[:, OFF_RWKV:OFF_GATE])[:, None]
    prw_prev = jnp.concatenate([prev_row, prw[:, :-1]], axis=1)
    z = prw + mu_shift * (prw_prev - prw)
    u = P[..., OFF_RGX:OFF_RGX + D_RNN]
    gate = P[..., OFF_RGG:OFF_RGG + D_RNN]
    uc, new_cbuf = _causal_conv(u, cbuf.astype(dt), conv_w, conv_b)
    h, h_last = _rg_lru(uc, h0, first, rg_wa, rg_ba, rg_wx, rg_bx, rg_lam)
    br_a = (h.astype(dt) * jax.nn.gelu(gate)) @ w_rg_o
    o_b, S_last = _rwkv7(z, S0, rw_w0, rw_w2, rw_a0, rw_a2, rw_g2, rw_kk, rw_ka, rw_rk, rw_gn_w, rw_gn_b)
    br_b = o_b.astype(dt) @ w_rw_o
    g_a = jax.nn.sigmoid(P[..., OFF_GATE:OFF_GATE + D_MODEL])
    g_b = jax.nn.sigmoid(P[..., OFF_GATE + D_MODEL:OFF_GATE + 2 * D_MODEL])
    x = x + (g_a * br_a + g_b * br_b) @ w_o
    hf = jax.nn.relu(_rmsnorm(x, norm_ffn) @ w_up)
    x = x + (hf * hf) @ w_down
    x = x + jax.nn.sigmoid(_rmsnorm(x, norm_ple) @ w_ple_gate) * (p_i.astype(dt) @ w_ple)
    return x, h_last.astype(dt), new_cbuf, S_last.astype(dt), xn[:, -1]

def setup_inputs(seed: int = 0) -> dict:
    key = jax.random.key(seed)
    ks = iter(jax.random.split(key, 64))
    nrm = lambda shape, s: jax.random.normal(next(ks), shape, jnp.float32) * s
    uni = lambda shape, lo, hi: jax.random.uniform(next(ks), shape, jnp.float32, lo, hi)
    L = DEPTH
    a_base = uni((L, D_RNN), 0.9, 0.999) ** (1.0 / RG_C)
    return {
        "x_prompt": nrm((BATCH, SEQ, D_MODEL), 1.0),
        "x_sample": nrm((DEC_BATCH, DEC_SEQ, D_MODEL), 1.0),
        "p_prompt": nrm((DEPTH, BATCH, SEQ, D_PLE), 1.0),
        "p_sample": nrm((DEPTH, DEC_BATCH, DEC_SEQ, D_PLE), 1.0),
        "state_rg_h": nrm((L, DEC_BATCH, D_RNN), 0.5),
        "state_rg_conv": nrm((L, DEC_BATCH, CONV_W - 1, D_RNN), 1.0),
        "state_rwkv": nrm((L, DEC_BATCH, N_HEADS, HEAD, HEAD), 0.5),
        "state_shift": nrm((L, DEC_BATCH, D_MODEL), 1.0),
        "norm_mix": 1.0 + nrm((L, D_MODEL), 0.02),
        "w_in": nrm((L, D_MODEL, N_IN), D_MODEL ** -0.5),
        "conv_w": nrm((L, CONV_W, D_RNN), 0.5),
        "conv_b": nrm((L, D_RNN), 0.02),
        "rg_wa": nrm((L, RG_BLOCKS, RG_BW, RG_BW), RG_BW ** -0.5),
        "rg_ba": nrm((L, RG_BLOCKS, RG_BW), 0.02),
        "rg_wx": nrm((L, RG_BLOCKS, RG_BW, RG_BW), RG_BW ** -0.5),
        "rg_bx": nrm((L, RG_BLOCKS, RG_BW), 0.02),
        "rg_lam": jnp.log(a_base / (1.0 - a_base)),
        "w_rg_o": nrm((L, D_RNN, D_MODEL), D_RNN ** -0.5),
        "mu_shift": uni((L, N_RWKV), 0.0, 1.0),
        "rw_w0": uni((L, D_ATT), -6.0, -1.0),
        "rw_w2": nrm((L, R_W, D_ATT), 0.1 * R_W ** -0.5),
        "rw_a0": nrm((L, D_ATT), 0.1),
        "rw_a2": nrm((L, R_A, D_ATT), 0.5 * R_A ** -0.5),
        "rw_g2": nrm((L, R_G, D_ATT), R_G ** -0.5),
        "rw_kk": 0.85 + nrm((L, D_ATT), 0.02),
        "rw_ka": 1.0 + nrm((L, D_ATT), 0.02),
        "rw_rk": nrm((L, N_HEADS, HEAD), 0.1),
        "rw_gn_w": 1.0 + nrm((L, D_ATT), 0.02),
        "rw_gn_b": nrm((L, D_ATT), 0.02),
        "w_rw_o": nrm((L, D_ATT, D_MODEL), D_ATT ** -0.5),
        "w_o": nrm((L, D_MODEL, D_MODEL), D_MODEL ** -0.5),
        "norm_ffn": 1.0 + nrm((L, D_MODEL), 0.02),
        "w_up": nrm((L, D_MODEL, D_FF), D_MODEL ** -0.5),
        "w_down": nrm((L, D_FF, D_MODEL), D_FF ** -0.5),
        "norm_ple": 1.0 + nrm((L, D_MODEL), 0.02),
        "w_ple_gate": nrm((L, D_MODEL, D_MODEL), D_MODEL ** -0.5),
        "w_ple": nrm((L, D_PLE, D_MODEL), D_PLE ** -0.5),
        "norm_f": 1.0 + nrm((D_MODEL,), 0.02),
    }

def reference(x_prompt, x_sample, p_prompt, p_sample, state_rg_h, state_rg_conv, state_rwkv, state_shift,
              norm_mix, w_in, conv_w, conv_b, rg_wa, rg_ba, rg_wx, rg_bx, rg_lam, w_rg_o,
              mu_shift, rw_w0, rw_w2, rw_a0, rw_a2, rw_g2, rw_kk, rw_ka, rw_rk, rw_gn_w, rw_gn_b,
              w_rw_o, w_o, norm_ffn, w_up, w_down, norm_ple, w_ple_gate, w_ple, norm_f):
    dt = x_prompt.dtype
    Bp, Tp = x_prompt.shape[0], x_prompt.shape[1]
    Ts = x_sample.shape[1]
    first_p = jnp.arange(Tp) == 0
    first_s = jnp.zeros((Ts,), dtype=bool)
    zc = jnp.zeros((Bp, CONV_W - 1, D_RNN), dt)
    zh = jnp.zeros((Bp, D_RNN), dt)
    zS = jnp.zeros((Bp, N_HEADS, HEAD, HEAD), dt)
    zx = jnp.zeros((Bp, D_MODEL), dt)
    hp, cp, sp, xp_, hs, cs, ss, xs_ = [], [], [], [], [], [], [], []
    xp, xs = x_prompt, x_sample
    for i in range(DEPTH):
        wts = (norm_mix[i], w_in[i], conv_w[i], conv_b[i], rg_wa[i], rg_ba[i], rg_wx[i], rg_bx[i],
               rg_lam[i], w_rg_o[i], mu_shift[i], rw_w0[i], rw_w2[i], rw_a0[i], rw_a2[i], rw_g2[i],
               rw_kk[i], rw_ka[i], rw_rk[i], rw_gn_w[i], rw_gn_b[i], w_rw_o[i], w_o[i], norm_ffn[i],
               w_up[i], w_down[i], norm_ple[i], w_ple_gate[i], w_ple[i])
        xp, h1, c1, s1, x1 = _layer(xp, p_prompt[i], zc, zh, zS, zx, first_p, *wts)
        xs, h2, c2, s2, x2 = _layer(xs, p_sample[i], state_rg_conv[i], state_rg_h[i], state_rwkv[i],
                                    state_shift[i], first_s, *wts)
        hp.append(h1); cp.append(c1); sp.append(s1); xp_.append(x1)
        hs.append(h2); cs.append(c2); ss.append(s2); xs_.append(x2)
    y_prompt = _rmsnorm(xp, norm_f)
    y_sample = _rmsnorm(xs, norm_f)
    return (y_prompt, y_sample,
            jnp.stack(hp), jnp.stack(cp), jnp.stack(sp), jnp.stack(xp_),
            jnp.stack(hs), jnp.stack(cs), jnp.stack(ss), jnp.stack(xs_))


_drawn_inputs = setup_inputs


def setup_inputs(seed=0):
    import zlib

    import numpy as np

    out = dict(_drawn_inputs(seed))
    spreads = {}
    factors = {'rg_ba': 8.0,
     'rg_bx': 7.973,
     'rw_w2': 8.0,
     'rw_kk': 8.912,
     'rw_gn_w': 8.0,
     'rw_gn_b': 21.962,
     'norm_ffn': 3.45,
     'norm_ple': 64.0,
     'norm_f': 8.15}
    for name, (base, spread) in spreads.items():
        noise = np.random.default_rng([zlib.crc32(name.encode()), seed]).standard_normal(out[name].shape)
        drawn = base * np.exp(spread * noise) if base else spread * noise
        out[name] = __import__('jax').numpy.asarray(drawn.astype(out[name].dtype))
    for name, factor in factors.items():
        out[name] = (out[name] * factor).astype(out[name].dtype)
    return out
```

```python
import math
from contextlib import ExitStack

import numpy as np
import concourse.bass as bass
from concourse import mybir

F32 = mybir.dt.float32
F32R = mybir.dt.float32r
ALU = mybir.AluOpType
ACT = mybir.ActivationFunctionType

P = 128
D = 2048
KT = D // P
SEQ, NB, NS = 256, 8, 4
SAMP = NB * NS
NT = SAMP + SEQ
NX = NB + NT
HEAD = 64
CHUNK = 64
NCH = SEQ // CHUNK
RW, RA, RGL = 96, 96, 256
DFF = 4 * D
DPLE = 256
OFF_R = 2 * D
OFF_K, OFF_V = OFF_R + D, OFF_R + 2 * D
OFF_LOW = OFF_R + 3 * D
OFF_GA = OFF_LOW + RW + RA + RGL
OFF_GB = OFF_GA + D
EPS = 1e-6
GN_EPS = 64e-5

CONV_STATE, H_STATE = 0, 24
(CW, CB, BA, BX, LAM, W0, A0, KK, KA, RK, GNW, GNB, MUR, MUK, MUV, GMIX, GFFN, GPLE, GFIN) = (
    32, 36, 37, 38, 39, 40, 41, 42, 43, 44, 45, 46, 47, 48, 49, 50, 51, 52, 53)
MULOW = 54
NPAR = 58
SP8, NSP8, OMKA = 0, 1, 2
NDER = 3

O_SHIFT, O_H, O_CONV = 0, 9, 18
NOUTF = 45

(C_ID, C_BD, C_ONE, C_AM, C_LM, C_SAM, C_SLM, C_SEQ, C_SQT, C_ID2, C_END) = np.cumsum(
    [0, 128, 128, 128, 512, 6 * 128, 128, 64, 256, 8, 64]).tolist()


def constants():
    c = np.zeros((P, C_END), np.float32)
    i, j = np.arange(P)[:, None], np.arange(P)[None, :]
    c[:, C_ID:C_ID + P] = i == j
    c[:, C_BD:C_BD + P] = i // HEAD == j // HEAD
    c[:, C_ONE:C_ONE + P] = 1 / D

    def half(t, s, m):
        return (t // (2 * m) == s // (2 * m)) & (t % (2 * m) >= m) & (s % (2 * m) < m)

    same = i // CHUNK == j // CHUNK
    c[:, C_AM:C_AM + 512] = np.concatenate([half(j, i, 1), same & (i <= j), same & (i < j), same & (i <= j)], 1)
    for l in range(6):
        c[:, C_LM + l * P:C_LM + (l + 1) * P] = half(i, j, 2 ** l)
    s, t = np.arange(SAMP)[:, None], np.arange(SAMP)[None, :]
    own = s % NB == t % NB
    c[:SAMP, C_SAM:C_SAM + 128] = np.concatenate(
        [own & half(t // NB, s // NB, 1), own & (s <= t), own & (s < t), own & (s <= t)], 1)
    c[:SAMP, C_SLM:C_SLM + 64] = np.concatenate([own & half(s // NB, t // NB, 1), own & half(s // NB, t // NB, 2)], 1)
    c[:, C_SEQ:C_SEQ + 256] = (np.arange(256)[None, :] // SAMP) == (np.arange(256)[None, :] % NB)
    c[:64, C_SQT:C_SQT + NB] = (np.arange(64)[:, None] % NB) == np.arange(NB)[None, :]
    c[:, C_ID2:C_ID2 + HEAD] = (i % HEAD) == np.arange(HEAD)[None, :]
    return c


SLOTS = 24
LOOP_UNITS = 6
U_LOW = 0
U_LOOP = 4
U_GB = U_LOOP + LOOP_UNITS * KT
U_RGO = U_GB + KT
U_RWO = U_RGO + KT
U_WO = U_RWO + KT
U_FFN = U_WO + KT
U_PLE = U_FFN + 8 * KT
U_END = U_PLE + KT

STEPS = {"dve_rg": 18, "dve_ch": 67}
ROW_LOADS = 27
N_INIT = 4
FFN_PLAN = (("up", 0), ("up", 1), ("down", 0), ("up", 2), ("down", 1), ("up", 3), ("down", 2), ("down", 3))


AT = {
    0: ["params", "mix_v", "lowrank"],
    1: ["kk_norm", "rg_gates"],
    2: ["decay"],
    3: ["bonus"],
    4: ["prep"],
    5: ["rg_scan"],
    6: ["turn"],
    7: ["pairwise"],
    9: ["invert1a"],
    10: ["invert1b", "state_in"],
    11: ["invert2a"],
    12: ["invert2b", "samp_pair", "samp_prep"],
    13: ["invert3a"],
    14: ["invert3b", "samp_inv_a"],
    15: ["invert4a", "samp_inv_b"],
    16: ["invert4b", "samp_r"],
    17: ["invert5a", "samp_u"],
    18: ["invert5b"],
    19: ["r0", "samp_out", "u0"],
    20: ["my0", "r1", "u1"],
    21: ["my1", "r2", "u2"],
    22: ["my2", "r3", "u3"],
    23: ["my3", "mean", "var", "small"],
}


def program(nc, a):
    ctx = ExitStack()
    with ctx:
        def sb(name, shape, dt=F32, stack=ctx):
            return stack.enter_context(nc.sbuf_tensor(name, shape, dt))

        def sem(name):
            return ctx.enter_context(nc.semaphore(name))

        bank = [ctx.enter_context(nc.psum_tensor(f"bank{k}", [P, 512], F32)) for k in range(8)]

        xh = sb("xh", [P, KT, NX], F32R)
        xl = sb("xl", [P, KT, NX], F32R)
        rga = sb("rga", [P, KT, NX])
        rwo = sb("rwo", [P, KT, NT])
        raw = [sb(f"raw{s}", [P, KT, P]) for s in range(2)]
        wh = [sb(f"wh{s}", [P, KT, P], F32R) for s in range(2)]
        wl = [sb(f"wl{s}", [P, KT, P], F32R) for s in range(2)]
        cst = sb("cst", [P, C_END])
        par = sb("par", [P, KT, NPAR])
        der = sb("der", [P, KT, NDER])
        der_work = sb("der_work", [P, KT, 4])
        outf = sb("outf", [P, KT, NOUTF])
        sums = sb("sums", [P, NX])

        ident, bd, ones = (cst[:, o:o + P] for o in (C_ID, C_BD, C_ONE))
        samp_all, prompt_all = slice(0, SAMP), slice(SAMP, NT)

        mix = ExitStack()
        with mix:
            def mb(name, shape, dt=F32):
                return sb(name, shape, dt, mix)

            ptu, ptc = mb("ptu", [P, NPAR]), mb("ptc", [P, NPAR])
            dtc = mb("dtc", [P, NDER])
            ex = mb("ex", [P, NX])
            zr, zk, zv = mb("zr", [P, NT]), mb("zk", [P, NT]), mb("zv", [P, NT])
            low = mb("low", [P, 4, NT])
            w2s, a2s, g2s = mb("w2s", [P, P]), mb("a2s", [P, P]), mb("g2s", [P, 2, P])
            was, wxs = mb("was", [P, P]), mb("wxs", [P, P])
            ue, xc, gg, gat = mb("ue", [P, 315]), mb("xc", [P, NT]), mb("gg", [P, NT]), mb("gat", [P, NT])
            rgi, th = mb("rgi", [P, NT]), mb("th", [P, NT])
            siga, sigw, gout, kp = (mb(n, [P, NT]) for n in ("siga", "sigw", "gout", "kp"))
            rn, ksq, kkn, bv = (mb(n, [P, NT]) for n in ("rn", "ksq", "kkn", "bv"))
            cum = mb("cum", [P, 5 * NB + NCH * (CHUNK + 1)])
            zeros = mb("zeros", [P, CHUNK])
            ar, btl, ktl = mb("ar", [P, 2, NT]), mb("btl", [P, NT]), mb("ktl", [P, NT])
            bkh, vv = mb("bkh", [P, 2 * SAMP]), mb("vv", [P, 2 * SAMP])
            tmb, tmv = mb("tmb", [P, 4, P]), mb("tmv", [P, 2, P])
            sbk, svv, suv = mb("sbk", [2 * SAMP, P]), mb("svv", [2 * SAMP, P]), mb("suv", [2 * SAMP, P])
            ams, ab = mb("ams", [P, 4, 512]), mb("ab", [P, 4, P])
            am = [mb(f"am{k}", [P, 4, P]) for k in range(2)]
            tt, tn, yy = mb("tt", [P, 4, P]), mb("tn", [P, 4, P]), mb("yy", [P, 4, P])
            sam, sab = mb("sam", [SAMP, 2, 128]), mb("sab", [SAMP, 2, SAMP])
            sa2, stn, stt_s, syy = (mb(n, [SAMP, 2, SAMP]) for n in ("sa2", "stn", "stt_s", "syy"))
            s0, ms = mb("s0", [P, NB, P]), mb("ms", [P, NB, P])
            aex, bke = mb("aex", [P, NB, SAMP]), mb("bke", [2 * SAMP, 2, 512])
            dg = mb("dg", [P, NB, HEAD])
            so = dg
            rs, us, sr = mb("rs", [P, P]), mb("us", [P, P]), mb("sr", [SAMP, P])
            mp, mtmp = [mb(f"mp{k}", [P, P]) for k in range(2)], mb("mtmp", [P, P])
            sfin = mtmp
            yf, yc, ysq, sd = (mb(n, [P, NT]) for n in ("yf", "yc", "ysq", "sd"))
            dif, rgr, m2 = rn, yf, ysq
            rows = ams[:, :, :].rearrange("p a b -> p (a b)")

        ffn = ExitStack()
        with ffn:
            sbh = [sb(f"sbh{k}", [P, KT, NT], F32R, ffn) for k in range(2)]
            sbl = [sb(f"sbl{k}", [P, KT, NT], F32R, ffn) for k in range(2)]
            tmp = [sb(f"tmp{k}", [P, NT], F32, ffn) for k in range(2)]
            nsq = [sb(f"nsq{k}", [P, 2, NX], F32, ffn) for k in range(2)]
            nrm = [sb(f"nrm{k}", [P, 2, NX], F32, ffn) for k in range(2)]
            gt = [t[:, 0, 0:NT] for t in nsq]
        fin = ExitStack()
        with fin:
            wcol = [sb(f"wcol{k}", [P, 2, P], F32, fin) for k in range(2)]
            ptok, pt = sb("ptok", [P, 3, DPLE], F32, fin), sb("pt", [P, 2, NT], F32, fin)
            small_out = sb("small_out", [NOUTF, D], F32, fin)
            ytok = sb("ytok", [P, 3, D], F32, fin)
        xtok = rwo[:, :, :].rearrange("p k t -> p (k t)")[:, 0:2 * D].rearrange("p (u d) -> p u d", u=2)

        xt_dram = nc.dram_tensor("xt_scratch", [P, KT, NX], F32).ap()
        ga_dram = nc.dram_tensor("ga_scratch", [KT, P, NT], F32).ap()
        gb_dram = nc.dram_tensor("gb_scratch", [KT, P, NT], F32).ap()

        hi_done, lo_done, unit_done = (
            sem(n) for n in ("hi_done", "lo_done", "unit_done"))
        cst_in, rows_zero, rows_in, xs_in, xp_in, xp2_in, xt_mm = (
            sem(n) for n in ("cst_in", "rows_zero", "rows_in", "xs_in", "xp_in", "xp2_in", "xt_mm"))
        par_mm, par_ready, xt_act, xt_dve, xt_saved = (
            sem(n) for n in ("par_mm", "par_ready", "xt_act", "xt_dve", "xt_saved"))
        der_step, init_done, sq_ready, sum_mm, rms_var, rms_std, rms_inv = (
            sem(n) for n in ("der_step", "init_done", "sq_ready", "sum_mm", "rms_var", "rms_std", "rms_inv"))
        nrm_gain, lam_abs, lam_exp, gated, nrm_ready, nrm_hi, nrm_lo = (
            sem(n) for n in ("nrm_gain", "lam_abs", "lam_exp", "gated", "nrm_ready", "nrm_hi", "nrm_lo"))
        nrm_copy = sem("nrm_copy")
        low_ex, low_mix, low_ready, small_in, s0_in, ga_ready, ga_saved = (
            sem(n) for n in ("low_ex", "low_mix", "low_ready", "small_in", "s0_in", "ga_ready", "ga_saved"))
        gb_ready = sem("gb_ready")
        ptc_ready, ex_ready, mixed, ue_ready, conv_ready, gelu_ready = (
            sem(n) for n in ("ptc_ready", "ex_ready", "mixed", "ue_ready", "conv_ready", "gelu_ready"))
        low_mm, low_read, ksq_ready, kk_mm, ss_ready, kk_root, rgr_mm = (
            sem(n) for n in ("low_mm", "low_read", "ksq_ready", "kk_mm", "ss_ready", "kk_root", "rgr_mm"))
        rgr_sig, rgi_mm, rgi_sig, decay_ready, rg_exp, th_ready = (
            sem(n) for n in ("rgr_sig", "rgi_mm", "rgi_sig", "decay_ready", "rg_exp", "th_ready"))
        m2_ready, m_root, bt_ready, bonus_mm, prep_done, turn_mm, turn_read = (
            sem(n) for n in ("m2_ready", "m_root", "bt_ready", "bonus_mm", "prep_done", "turn_mm", "turn_read"))
        pair_mm, ab_read, pair_read, t_start, am_ready = (
            sem(n) for n in ("pair_mm", "ab_read", "pair_read", "t_start", "am_ready"))
        state_mm, state_read, spair_mm, sinv_ready, syy_mm, syy_read, stt_mm = (
            sem(n) for n in ("state_mm", "state_read", "spair_mm", "sinv_ready", "syy_mm", "syy_read", "stt_mm"))
        stt_ready, sr_mm, sr_read, su_mm, su_read = (
            sem(n) for n in ("stt_ready", "sr_mm", "sr_read", "su_mm", "su_read"))
        so_mm, so_ready, so_saved = (
            sem(n) for n in ("so_mm", "so_ready", "so_saved"))
        yy_mm, yy_read, tn_mm, tn_ready, r_mm, u_mm, u_read = (
            sem(n) for n in ("yy_mm", "yy_read", "tn_mm", "tn_ready", "r_mm", "u_mm", "u_read"))
        m_mm, y_mm, m_ready = (
            sem(n) for n in ("m_mm", "y_mm", "m_ready"))
        yf_ready, mean_mm, yc_ready, ysq_ready, var_mm, var_ready, y_root = (
            sem(n) for n in ("yf_ready", "mean_mm", "yc_ready", "ysq_ready", "var_mm", "var_ready", "y_root"))
        rga_ready, rwo_ready = (
            sem(n) for n in ("rga_ready", "rwo_ready"))
        fin_mm, fin_read, fin_saved = (
            sem(n) for n in ("fin_mm", "fin_read", "fin_saved"))
        dve_rg, dve_ch, split_hi, split_lo, x_back = (
            sem(n) for n in ("dve_rg", "dve_ch", "split_hi", "split_lo", "x_back"))
        merged, merged_hi, merged_lo = (
            sem(n) for n in ("merged", "merged_hi", "merged_lo"))
        x_done, h_relu, h_sq, h_hi, h_lo, tmp_ready, ple_in = (
            sem(n) for n in ("x_done", "h_relu", "h_sq", "h_hi", "h_lo", "tmp_ready", "ple_in"))
        pt_mm, pt_ready, sg_ready, embed_mm, sexp_ready, sig_ready, small_mm = (
            sem(n) for n in ("pt_mm", "pt_ready", "sg_ready", "embed_mm", "sexp_ready", "sig_ready", "small_mm"))
        small_read = sem("small_read")
        y_turn, y_read, stored = (
            sem(n) for n in ("y_turn", "y_read", "stored"))
        r_read = [sem(f"r_read{k}") for k in range(4)]
        wcol_in = [sem(f"wcol_in{k}") for k in range(2)]
        gb_saved = [sem(f"gb_saved{k}") for k in range(2)]
        g_in = [sem(f"g_in{k}") for k in range(2)]
        raw_in = [sem(f"raw_in{k}") for k in range(2)]

        block = ctx.enter_context(nc.Block())

        class Count:

            def __init__(self, sem, step, per_step):
                self.sem, self.n = sem, 0
                self.base, self.per_step = step * per_step if per_step else 0, per_step

            def one(self):
                self.n += 1
                return 1

            def so_far(self):
                return self.base + self.n

            def end(self):
                assert self.n == self.per_step, self.n

        def cum_of(which):
            o = 0 if which == "before" else 1
            samples = cum[:, o * NB:o * NB + SAMP]
            prompt = cum[:, 5 * NB:].rearrange("p (c t) -> p c t", c=NCH)[:, :, o:o + CHUNK]
            return samples, prompt

        def last_decay(c):
            col = 5 * NB + c * (CHUNK + 1) + CHUNK
            return cum[:, col:col + 1]

        def chunks(ap):
            return ap[:, SAMP:NT].rearrange("p (c t) -> p c t", c=NCH)

        def unit_columns(u, it):
            return [0, D, OFF_GA, OFF_K, OFF_R, OFF_V][u] + it * P

        @block.sync
        def _(sp):
            def load_unit(src, slot, n=None):
                if n is not None:
                    sp.wait_ge(cst_in, 16)
                    sp.wait_ge(lo_done, n - 1)
                sp.dma_start(raw[slot][:], src.rearrange("(k p) c -> p k c", p=P)).then_inc(raw_in[slot], 16)

            def in_columns(start):
                return a["w_in"][0, :, bass.ds(start, P)]

            sp.dma_start(cst[:], a["const"]).then_inc(cst_in, 16)
            sp.dma_start(xtok[0:NB, 0, :], a["state_shift"][0]).then_inc(xs_in, 16)
            for t in range(NS):
                sp.dma_start(xtok[NB + t * NB:2 * NB + t * NB, 0, :], a["x_sample"][:, t, :]).then_inc(xs_in, 16)
            sp.dma_start(xtok[:, 1, :], a["x_prompt"][0, 0:P, :]).then_inc(xp_in, 16)
            sp.wait_ge(rows_zero, 1)
            n_rows = 0
            for j in range(3):
                sp.dma_start(rows[j * NB:j * NB + NB, :], a["state_rg_conv"][0, :, j, :]).then_inc(rows_in, 16)
            sp.dma_start(rows[H_STATE:H_STATE + NB, :], a["state_rg_h"][0]).then_inc(rows_in, 16)
            sp.dma_start(rows[CW:CW + 4, :], a["conv_w"][0]).then_inc(rows_in, 16)
            n_rows = 5
            mu = a["mu_shift"][0]
            for row, src in ((CB, a["conv_b"][0]), (BA, a["rg_ba"][0]), (BX, a["rg_bx"][0]), (LAM, a["rg_lam"][0]),
                             (W0, a["rw_w0"][0]), (A0, a["rw_a0"][0]), (KK, a["rw_kk"][0]), (KA, a["rw_ka"][0]),
                             (RK, a["rw_rk"][0]), (GNW, a["rw_gn_w"][0]), (GNB, a["rw_gn_b"][0]),
                             (MUR, mu[0:D]), (MUK, mu[D:2 * D]), (MUV, mu[2 * D:3 * D]),
                             (GMIX, a["norm_mix"][0]), (GFFN, a["norm_ffn"][0]), (GPLE, a["norm_ple"][0]),
                             (GFIN, a["norm_f"])):
                width = src.shape[-1]
                src = src.rearrange("a b -> (a b)") if len(src.shape) == 2 else src
                sp.dma_start(rows[row:row + 1, :], src.rearrange("(o d) -> o d", o=1)).then_inc(rows_in, 16)
                n_rows += 1
            o = 3 * D
            for k, (o, w) in enumerate(((3 * D, RW), (3 * D + RW, RA), (3 * D + RW + RA, P), (3 * D + RW + RA + P, P))):
                sp.dma_start(rows[MULOW + k:MULOW + k + 1, 0:w],
                             mu[o:o + w].rearrange("(o d) -> o d", o=1)).then_inc(rows_in, 16)
                n_rows += 1
            assert n_rows == ROW_LOADS
            low_start = (OFF_LOW, OFF_LOW + RW, OFF_LOW + RW + RA, OFF_LOW + RW + RA + P)
            for u in range(2):
                load_unit(in_columns(low_start[u]), u)
            sp.wait_ge(xt_mm, 2)
            sp.dma_start(xtok[:, 0, :], a["x_prompt"][0, P:SEQ, :]).then_inc(xp2_in, 16)
            sp.wait_ge(xt_dve, 6)
            sp.wait_ge(xt_act, 4)
            sp.dma_start(xt_dram, rga[:]).then_inc(xt_saved, 16)

            def small(it, again):
                if again:
                    sp.wait_ge(cst_in, 16)
                    sp.wait_ge(rgi_mm, it)
                cols = bass.ds(it * P, P)
                sp.dma_start(w2s[0:RW, :], a["rw_w2"][0, :, cols]).then_inc(small_in, 16)
                sp.dma_start(a2s[0:RA, :], a["rw_a2"][0, :, cols]).then_inc(small_in, 16)
                sp.dma_start(g2s[:], a["rw_g2"][0, :, cols].rearrange("(k p) c -> p k c", p=P)).then_inc(small_in, 16)
                sp.dma_start(was[:], a["rg_wa"][0, bass.ds(it, 1)].rearrange("o c d -> (o c) d")).then_inc(small_in, 16)
                sp.dma_start(wxs[:], a["rg_wx"][0, bass.ds(it, 1)].rearrange("o c d -> (o c) d")).then_inc(small_in, 16)
                if again:
                    sp.wait_ge(cst_in, 16)
                    sp.wait_ge(state_mm, it)
                else:
                    sp.wait_ge(init_done, N_INIT)
                for h in range(2):
                    sp.dma_start(s0[h * HEAD:(h + 1) * HEAD, :, h * HEAD:(h + 1) * HEAD],
                                 a["state_rwkv"][0, :, bass.ds(2 * it + h, 1)].rearrange("b o i j -> (o i) b j")
                                 ).then_inc(s0_in, 16)

            def states_out(p):
                sp.wait_ge(cst_in, 16)
                sp.wait_ge(so_ready, p + 1)
                sp.dma_start(a["o_rwkv_s"][0, :, bass.ds(2 * p, 2)].rearrange("b h i j -> (h i) b j"), so[:]
                             ).then_inc(so_saved, 16)
                sp.wait_ge(cst_in, 16)
                sp.wait_ge(fin_read, p + 1)
                for h in range(2):
                    sp.dma_start(a["o_rwkv_p"][0, 0, bass.ds(2 * p + h, 1)].rearrange("o i j -> (o i) j"),
                                 sfin[h * HEAD:(h + 1) * HEAD, h * HEAD:(h + 1) * HEAD]).then_inc(fin_saved, 16)

            def step(it, units, chain):
                p = it - 1
                for slot in range(SLOTS):
                    u, q = divmod(slot, 4)
                    if units and q == 0:
                        n = U_LOOP + it * LOOP_UNITS + u + 3
                        if u < 3:
                            load_unit(in_columns(unit_columns(u + 3, it)), (u + 3) % 2, n)
                        elif units == "loop":
                            load_unit(in_columns(unit_columns(u - 3, it + 1)), (u + 3) % 2, n)
                        else:
                            load_unit(in_columns(OFF_GB + (u - 3) * P), (u + 3) % 2, n)
                        if u == 3:
                            sp.wait_ge(cst_in, 16)
                            sp.wait_ge(ga_ready, it + 1)
                            sp.dma_start(ga_dram[bass.ds(it, 1)].rearrange("o p t -> (o p) t"), gat[:]).then_inc(ga_saved, 16)
                    if units and slot == SLOTS - 1:
                        small(it, chain)
                    if chain and slot == SLOTS - 1:
                        states_out(p)

            for u in (2, 3):
                load_unit(in_columns(low_start[u]), u % 2, u)
            for u in range(3):
                load_unit(in_columns(unit_columns(u, 0)), u % 2, U_LOOP + u)
            step(0, "loop", False)
            with sp.Fori(1, KT - 1) as it:
                step(it, "loop", True)
            step(KT - 1, "last", True)
            for slot in range(SLOTS):
                u, q = divmod(slot, 4)
                if q == 0:
                    load_unit(in_columns(OFF_GB + (u + 3) * P), (u + 3) % 2, U_GB + u + 3)
                    if u >= 1:
                        sp.wait_ge(cst_in, 16)
                        sp.wait_ge(gb_ready, u)
                        sp.dma_start(gb_dram[u - 1], gat[:]).then_inc(gb_saved[(u - 1) % 2], 16)
                if slot == SLOTS - 1:
                    states_out(KT - 1)

            def phase(base, src, following, extra=None, start=0, end=None):
                with sp.Fori(start // 2, (KT - 4) // 2) as i:
                    for u in range(2):
                        k = 2 * i + u
                        load_unit(src(k + 3), (u + 1) % 2, base + k + 3)
                        if extra:
                            extra(k, u, i)
                for k in range(KT - 4, KT):
                    if k + 3 < KT:
                        load_unit(src(k + 3), (k + 1) % 2, base + k + 3)
                    elif following:
                        load_unit(following(k + 3 - KT), (k + 1) % 2, base + k + 3)
                    if extra:
                        extra(k, k % 2, k // 2)
                    if end and k == KT - 3:
                        end()

            def columns(name, k0=None):
                w = a[name][0] if k0 is None else a[name][0, k0:k0 + D, :]
                return lambda k: w[:, bass.ds(k * P, P)]

            def up(g):
                return lambda k: a["w_up"][0, :, bass.ds(g * D + k * P, P)]

            sp.wait_ge(gb_ready, 6)
            sp.dma_start(gb_dram[5], gat[:]).then_inc(gb_saved[1], 16)

            def gb_store(k, u, i):
                sp.wait_ge(cst_in, 16)
                sp.wait_ge(gb_ready, k + 1)
                sp.dma_start(gb_dram[bass.ds(k, 1)].rearrange("o p t -> (o p) t"), tmp[u][:]).then_inc(gb_saved[u], 16)

            phase(U_GB, lambda k: in_columns(OFF_GB + k * P), columns("w_rg_o"), gb_store, start=6)

            def gate_load(dram, first):
                def extra(k, u, i):
                    if not (isinstance(i, int) and i == 0):
                        sp.wait_ge(cst_in, 16)
                        sp.wait_ge(merged, first + k - 1)
                    sp.dma_start(gt[u][:], dram[bass.ds(k, 1)].rearrange("o p t -> (o p) t")).then_inc(g_in[u], 16)
                return extra

            sp.wait_ge(ga_saved, 16 * KT)
            sp.wait_ge(gb_saved[0], 8 * KT)
            sp.wait_ge(gb_saved[1], 8 * KT)

            def x_again():
                sp.wait_ge(split_lo, 4)
                sp.dma_start(rga[:], xt_dram).then_inc(x_back, 16)

            for u in range(2):
                load_unit(a["w_rg_o"][0, :, (u + 3) * P:(u + 4) * P], (u + 1) % 2, U_RGO + u + 3)
                gate_load(ga_dram, 0)(u, u, 0)
            phase(U_RGO, columns("w_rg_o"), columns("w_rw_o"), gate_load(ga_dram, 0), start=2, end=x_again)
            phase(U_RWO, columns("w_rw_o"), columns("w_o"), gate_load(gb_dram, KT))
            phase(U_WO, columns("w_o"), up(0))
            plan = [("up", 0), ("up", 1), ("down", 0), ("up", 2), ("down", 1), ("up", 3), ("down", 2), ("down", 3)]
            srcs = [up(g) if kind == "up" else columns("w_down", g * D) for kind, g in plan] + [columns("w_ple_gate")]

            def ple_loads():
                sp.wait_ge(cst_in, 16)
                sp.wait_ge(unit_done, U_FFN + 7 * KT)
                for t in range(NS):
                    sp.dma_start(ptok[t * NB:t * NB + NB, 0, :], a["p_sample"][0, :, t, :]).then_inc(ple_in, 16)
                sp.dma_start(ptok[:, 1:3, :], a["p_prompt"][0, 0].rearrange("(u p) c -> p u c", p=P)).then_inc(ple_in, 16)

            for f in range(8):
                phase(U_FFN + f * KT, srcs[f], srcs[f + 1], end=ple_loads if f == 7 else None)

            def col_load(k, u, i):
                if not (isinstance(i, int) and i == 0):
                    sp.wait_ge(cst_in, 16)
                    sp.wait_ge(embed_mm, k - 1)
                sp.dma_start(wcol[u][:], a["w_ple"][0, :, bass.ds(k * P, P)].rearrange("(k p) c -> p k c", p=P)
                             ).then_inc(wcol_in[u], 16)

            for u in range(2):
                load_unit(srcs[8](u + 3), (u + 1) % 2, U_PLE + u + 3)
                col_load(u, u, 0)
            phase(U_PLE, srcs[8], None, col_load, start=2)

            sp.wait_ge(small_read, 4)
            for dst, row, n in ((a["o_shift_p"][0], O_SHIFT, 1), (a["o_shift_s"][0], O_SHIFT + 1, NB),
                                (a["o_h_p"][0], O_H, 1), (a["o_h_s"][0], O_H + 1, NB),
                                (a["o_conv_p"][0, 0], O_CONV, 3),
                                (a["o_conv_s"][0, :, 0, :], O_CONV + 3, NB), (a["o_conv_s"][0, :, 1, :], O_CONV + 3 + NB, NB),
                                (a["o_conv_s"][0, :, 2, :], O_CONV + 3 + 2 * NB, NB)):
                sp.dma_start(dst, small_out[row:row + n, :]).then_inc(stored, 16)
            sp.wait_ge(y_read, 3 * 8)
            for t in range(NS):
                sp.dma_start(a["o_y_s"][:, t, :], ytok[t * NB:t * NB + NB, 0, :]).then_inc(stored, 16)
            sp.dma_start(a["o_y_p"][0].rearrange("(u p) d -> p u d", p=P), ytok[:, 1:3, :]).then_inc(stored, 16)
            sp.wait_ge(stored, 16 * 13)
            sp.wait_ge(so_saved, 16 * KT)
            sp.wait_ge(fin_saved, 32 * KT)
            sp.wait_ge(xt_saved, 16)

        @block.tensor
        def _(pe):
            def mm(out, lhsT, rhs, start, stop):
                return pe.matmul(out, lhsT, rhs, start=start, stop=stop, skip_group_check=True)

            def apart(value):
                if not isinstance(value, int):
                    value = pe.snap(value)
                    pe.wait_ge(cst_in, 16)
                return value

            def unit_quarter(slot, hi, lo, first, last, q):
                out = bank[slot][:, 0:last - first]
                for kt in range(4 * q, 4 * q + 4):
                    x1, x2 = hi[:, kt, first:last], lo[:, kt, first:last]
                    mm(out, wh[slot][:, kt, :], x1, kt == 0, False)
                    mm(out, wh[slot][:, kt, :], x2, False, False)
                    done = mm(out, wl[slot][:, kt, :], x1, False, kt == KT - 1)
                if q == 3:
                    done.then_inc(unit_done, 1)

            def unit_ready(n, read, count):
                pe.wait_ge(lo_done, n + 1)
                if read:
                    pe.wait_ge(read, count)

            def turn(out, in_):
                return pe.transpose(out, in_, ident)

            pe.wait_ge(cst_in, 16)
            pe.wait_ge(xs_in, 16 * 5)
            for b in range(2):
                for k in range(8):
                    done = pe.transpose(bank[b][:, k * 40:(k + 1) * 40], xtok[0:40, 0, (b * 8 + k) * P:(b * 8 + k + 1) * P], cst[0:40, C_ID:C_ID + 40])
                done.then_inc(xt_mm, 1)
            pe.wait_ge(xp_in, 16)
            for b in range(4):
                for k in range(4):
                    done = turn(bank[2 + b][:, k * P:(k + 1) * P], xtok[:, 1, (b * 4 + k) * P:(b * 4 + k + 1) * P])
                done.then_inc(xt_mm, 1)
            pe.wait_ge(rows_in, 16 * ROW_LOADS)
            for b in range(2):
                for k in range(8):
                    done = pe.transpose(bank[6 + b][:, k * NPAR:(k + 1) * NPAR], rows[0:NPAR, (b * 8 + k) * P:(b * 8 + k + 1) * P], cst[0:NPAR, C_ID:C_ID + NPAR])
                done.then_inc(par_mm, 1)
            pe.wait_ge(xp2_in, 16)
            for b in range(4):
                if b < 2:
                    pe.wait_ge(xt_dve, b + 1)
                else:
                    pe.wait_ge(xt_act, b - 1)
                for k in range(4):
                    done = turn(bank[b][:, k * P:(k + 1) * P], xtok[:, 0, (b * 4 + k) * P:(b * 4 + k + 1) * P])
                done.then_inc(xt_mm, 1)

            def norm(k, width):
                for j in range(8):
                    pe.wait_ge(sq_ready, 8 * k + j + 1)
                    for h in range(2):
                        done = mm(bank[7][:, 0:width], ones, nsq[j % 2][:, h, NX - width:NX], j == 0 and h == 0, j == 7 and h == 1)
                    done.then_inc(sum_mm, 1)

            pe.wait_ge(par_ready, 2)
            norm(0, NX)

            pe.wait_ge(nrm_lo, 8)
            for n in range(4):
                unit_ready(n, low_ex if n > 1 else None, n - 1)
                for q in range(4):
                    unit_quarter(n % 2, xh, xl, 0, NX, q)

            def stage(name, p):
                one = p + 1
                if name == "lowrank":
                    pe.wait_ge(small_in, 80 * one)
                    if isinstance(p, int) and p == 0:
                        pe.wait_ge(low_ready, 4)
                    mm(bank[2][:, 0:NT], w2s[0:RW, :], low[0:RW, 0, :], True, True)
                    mm(bank[3][:, 0:NT], a2s[0:RA, :], low[0:RA, 1, :], True, True)
                    mm(bank[4][:, 0:NT], g2s[:, 0, :], low[:, 2, :], True, False)
                    mm(bank[4][:, 0:NT], g2s[:, 1, :], low[:, 3, :], False, True).then_inc(low_mm, 1)
                elif name == "kk_norm":
                    pe.wait_ge(ksq_ready, one)
                    mm(bank[5][:, 0:NT], bd, ksq[:], True, True).then_inc(kk_mm, 1)
                elif name == "rg_gates":
                    pe.wait_ge(conv_ready, one)
                    mm(bank[7][:, 0:NT], was[:], xc[:], True, True).then_inc(rgr_mm, 1)
                    mm(bank[6][:, 0:NT], wxs[:], xc[:], True, True).then_inc(rgi_mm, 1)
                elif name == "bonus":
                    pe.wait_ge(bt_ready, one)
                    pe.wait_ge(rgi_sig, one)
                    mm(bank[6][:, 0:NT], bd, bv[:], True, True).then_inc(bonus_mm, 1)
                elif name == "turn":
                    pe.wait_ge(prep_done, one)
                    pe.wait_ge(low_read, one)
                    for k, src in enumerate((btl, ktl)):
                        for g in range(2):
                            turn(bank[2][:, (2 * k + g) * P:(2 * k + g + 1) * P], src[:, SAMP + g * P:SAMP + (g + 1) * P])
                    for g in range(2):
                        turn(bank[3][:, g * P:(g + 1) * P], zv[:, SAMP + g * P:SAMP + (g + 1) * P])
                    turn(bank[3][0:2 * SAMP, 256:384], bkh[:])
                    turn(bank[3][0:2 * SAMP, 384:512], vv[:]).then_inc(turn_mm, 1)
                elif name == "pairwise":
                    for g in range(2):
                        cols = slice(SAMP + g * P, SAMP + (g + 1) * P)
                        for h in range(2):
                            rows_h = slice(h * HEAD, (h + 1) * HEAD)
                            out = bank[4 + 2 * g + h]
                            mm(out[:, 0:256], btl[rows_h, cols], ar[rows_h, :, cols], True, True)
                            mm(out[:, 256:512], ktl[rows_h, cols], ar[rows_h, :, cols], True, True).then_inc(pair_mm, 1)
                    pe.wait_ge(turn_read, 5 * one)
                    for g in range(2):
                        cols = slice(SAMP + g * P, SAMP + (g + 1) * P)
                        for h in range(2):
                            rows_h = slice(h * HEAD, (h + 1) * HEAD)
                            done = mm(bank[2 + h][:, g * P:(g + 1) * P], ar[rows_h, 0, cols], btl[rows_h, cols], True, True)
                    done.then_inc(pair_mm, 1)
                elif name[:6] == "invert":
                    l, part = int(name[6]), name[7]
                    if part == "a":
                        if l == 1:
                            pe.wait_ge(t_start, one)
                            pe.wait_ge(pair_read, 4 * one)
                        else:
                            pe.wait_ge(tn_ready, 5 * p + l - 1)
                        pe.wait_ge(am_ready, 5 * p + l)
                        for q in range(4):
                            done = mm(bank[4][:, q * P:(q + 1) * P], am[l % 2][:, q, :], tt[:, q, :], True, True)
                        done.then_inc(yy_mm, 1)
                    else:
                        pe.wait_ge(yy_read, 5 * p + l)
                        for q in range(4):
                            done = mm(bank[5][:, q * P:(q + 1) * P], tn[:, q, :], yy[:, q, :], True, True)
                        if l < 5:
                            for q in range(4):
                                done = mm(bank[6][:, q * P:(q + 1) * P], yy[:, q, :], tn[:, q, :], True, True)
                        done.then_inc(tn_mm, 1)
                elif name == "state_in":
                    pe.wait_ge(s0_in, 32 * one)
                    pe.wait_ge(ab_read, 2 * one)
                    for b in range(NB):
                        done = turn(bank[2 + b // 4][:, (b % 4) * P:(b % 4 + 1) * P], s0[:, b, :])
                    done.then_inc(state_mm, 1)
                elif name == "samp_pair":
                    count = apart(2 * one)
                    pe.wait_ge(state_read, count)
                    for h in range(2):
                        rows_h = slice(h * HEAD, (h + 1) * HEAD)
                        out = bank[2 + h]
                        mm(out[0:SAMP, 0:64], btl[rows_h, 0:SAMP], ar[rows_h, :, 0:SAMP], True, True)
                        mm(out[0:SAMP, 64:128], ktl[rows_h, 0:SAMP], ar[rows_h, :, 0:SAMP], True, True)
                        done = mm(out[0:SAMP, 128:160], ar[rows_h, 0, 0:SAMP], btl[rows_h, 0:SAMP], True, True)
                    done.then_inc(spair_mm, 1)
                elif name == "samp_inv_a":
                    count = apart(one)
                    pe.wait_ge(sinv_ready, count)
                    for h in range(2):
                        done = mm(bank[2][0:SAMP, h * SAMP:(h + 1) * SAMP], sa2[:, h, :], stt_s[:, h, :], True, True)
                    done.then_inc(syy_mm, 1)
                elif name == "samp_inv_b":
                    count = apart(one)
                    pe.wait_ge(syy_read, count)
                    for h in range(2):
                        done = mm(bank[3][0:SAMP, h * SAMP:(h + 1) * SAMP], stn[:, h, :], syy[:, h, :], True, True)
                    done.then_inc(stt_mm, 1)
                elif name == "samp_r":
                    pe.wait_ge(sexp_ready, one)
                    for b in range(NB):
                        mm(bank[2][0:SAMP, 0:P], aex[:, b, :], ms[:, b, :], b == 0, False)
                    for h in range(2):
                        done = mm(bank[2][0:SAMP, h * HEAD:(h + 1) * HEAD], sam[:, h, 64:96], svv[0:SAMP, h * HEAD:(h + 1) * HEAD], False, True)
                    done.then_inc(sr_mm, 1)
                elif name == "samp_u":
                    count = apart(one)
                    pe.wait_ge(sr_read, count)
                    pe.wait_ge(stt_ready, one)
                    for h in range(2):
                        done = mm(bank[3][0:SAMP, h * HEAD:(h + 1) * HEAD], stt_s[:, h, :], sr[:, h * HEAD:(h + 1) * HEAD], True, True)
                    done.then_inc(su_mm, 1)
                elif name == "samp_out":
                    count = apart(one)
                    pe.wait_ge(su_read, count)
                    for b in range(NB):
                        mm(bank[7][:, b:SAMP:NB], ms[:, b, :], ar[:, 1, b:SAMP:NB], b == 0, False)
                    for h in range(2):
                        hc = slice(h * HEAD, (h + 1) * HEAD)
                        mm(bank[7][hc, 0:SAMP], suv[0:SAMP, hc], sam[:, h, 32:64], False, False)
                        mm(bank[7][hc, 0:SAMP], svv[0:SAMP, hc], sam[:, h, 96:128], False, True)
                    for b in range(NB):
                        mm(bank[3][:, b * HEAD:(b + 1) * HEAD], ms[:, b, :], dg[:, b, :], b == 0, False)
                    for h in range(2):
                        hc = slice(h * HEAD, (h + 1) * HEAD)
                        done = mm(bank[3][hc, 0:512], suv[:, hc], bke[:, h, :], False, True)
                    done.then_inc(so_mm, 1)
                elif name[0] == "r" and name[1:].isdigit():
                    c = int(name[1:])
                    g, rc = c // 2, slice((c % 2) * CHUNK, (c % 2 + 1) * CHUNK)
                    cc = (c % 2) * CHUNK
                    if c == 0:
                        count = apart(5 * one)
                        pe.wait_ge(tn_ready, count)
                    else:
                        count = apart(NCH * p + c)
                        pe.wait_ge(m_ready, count)
                        mm(bank[4][rc, 0:P], ar[:, 0, SAMP + c * CHUNK:SAMP + (c + 1) * CHUNK], mp[c % 2][:], True, False)
                    for h in range(2):
                        hc = slice(h * HEAD, (h + 1) * HEAD)
                        done = mm(bank[4][rc, hc], ams[rc, 2 * h + g, 256 + cc:256 + cc + CHUNK], tmv[rc, g, hc], c == 0, True)
                    done.then_inc(r_mm, 1)
                elif name[0] == "u":
                    c = int(name[1:])
                    g, rc = c // 2, slice((c % 2) * CHUNK, (c % 2 + 1) * CHUNK)
                    cc = (c % 2) * CHUNK
                    count = apart(one)
                    pe.wait_ge(r_read[c], count)
                    for h in range(2):
                        hc = slice(h * HEAD, (h + 1) * HEAD)
                        done = mm(bank[5][rc, hc], tt[rc, 2 * h + g, cc:cc + CHUNK], rs[rc, hc], True, True)
                    done.then_inc(u_mm, 1)
                elif name[:2] == "my":
                    c = int(name[2:])
                    g, rc = c // 2, slice((c % 2) * CHUNK, (c % 2 + 1) * CHUNK)
                    cc = (c % 2) * CHUNK
                    ycols = slice(SAMP + c * CHUNK, SAMP + (c + 1) * CHUNK)
                    count = apart(NCH * p + c + 1)
                    pe.wait_ge(u_read, count)
                    mm(bank[6][:, 0:P], tmb[rc, g, :], us[rc, :], True, False)
                    mm(bank[6][:, 0:P], tmb[rc, 2 + g, :], tmv[rc, g, :], False, True).then_inc(m_mm, 1)
                    if c:
                        mm(bank[7][:, ycols], mp[c % 2][:], ar[:, 1, ycols], True, False)
                    for h in range(2):
                        hc = slice(h * HEAD, (h + 1) * HEAD)
                        mm(bank[7][hc, ycols], us[rc, hc], ams[rc, 2 * h + g, 128 + cc:128 + cc + CHUNK], c == 0, False)
                        done = mm(bank[7][hc, ycols], tmv[rc, g, hc], ams[rc, 2 * h + g, 384 + cc:384 + cc + CHUNK], False, True)
                    done.then_inc(y_mm, 1)
                elif name == "mean":
                    pe.wait_ge(m_ready, NCH * one)
                    turn(bank[2][:, 0:P], mp[NCH % 2][:]).then_inc(fin_mm, 1)
                    pe.wait_ge(yf_ready, one)
                    mm(bank[4][:, 0:NT], bd, yf[:], True, True).then_inc(mean_mm, 1)
                elif name == "var":
                    pe.wait_ge(ysq_ready, one)
                    mm(bank[5][:, 0:NT], bd, ysq[:], True, True).then_inc(var_mm, 1)

            def step(it, units, chain):
                for slot in range(SLOTS):
                    u, q = divmod(slot, 4)
                    if units == "loop":
                        first = 0 if u >= 3 else NB
                        if q == 0:
                            read, count = [(ex_ready, 3 * it - 1), (ex_ready, 3 * it), (ue_ready, it + 1),
                                           (gelu_ready, it + 1), (ga_ready, it + 1), (ex_ready, 3 * it + 1)][u]
                            if not chain and u < 2:
                                read, count = low_ex, 3 + u
                            unit_ready(U_LOOP + it * LOOP_UNITS + u, read, count)
                        unit_quarter(u % 2, xh, xl, first, NX, q)
                    else:
                        if q == 0:
                            read, count = (ex_ready, 3 * it - 1 + u) if u < 2 else (gb_ready, u - 1)
                            unit_ready(U_GB + u, read, count)
                        unit_quarter(u % 2, xh, xl, NB, NX, q)
                    if chain:
                        for name in AT.get(slot, []):
                            stage(name, it - 1)

            step(0, "loop", False)
            with pe.Fori(1, KT) as it:
                step(it, "loop", True)
            step(KT, "gb", True)

            def phase(base, hi, lo, first, last, read, before=None, extra=None, start=2):
                def one(k, u):
                    for q in range(4):
                        unit_quarter(u, hi, lo, first, last, q)
                    if extra:
                        extra(k, u)

                if before:
                    for k in range(2):
                        unit_ready(base + k, before[0], before[1] - 1 + k)
                        one(k, k)
                with pe.Fori(start // 2, KT // 2) as i:
                    for u in range(2):
                        unit_ready(base + 2 * i + u, read[0], read[1] + 2 * i + u - 1)
                        one(2 * i + u, u)

            phase(U_GB, xh, xl, NB, NX, (gb_ready, 0), start=6)
            pe.wait_ge(split_lo, 4)
            phase(U_RGO, sbh[0], sbl[0], 0, NT, (merged, 0), (gb_ready, KT))
            pe.wait_ge(split_lo, 8)
            phase(U_RWO, sbh[1], sbl[1], 0, NT, (gated, 0), (merged, KT))
            pe.wait_ge(merged_lo, KT)
            phase(U_WO, sbh[0], sbl[0], 0, NT, (x_done, 0), (gated, KT))
            norm(1, NT)
            pe.wait_ge(nrm_lo, 16)
            f, before = 0, (x_done, KT)
            for kind, g in FFN_PLAN:
                base = U_FFN + f * KT
                if kind == "up":
                    phase(base, xh, xl, NB, NX, (h_relu, KT * g), before)
                    before = (h_relu, KT * (g + 1))
                else:
                    pe.wait_ge(h_lo, KT * (g + 1))
                    phase(base, sbh[g % 2], sbl[g % 2], 0, NT, (x_done, KT * (g + 1)), before)
                    before = (x_done, KT * (g + 2))
                f += 1
            pe.wait_ge(ple_in, 16 * 5)
            for k in range(2):
                pe.transpose(bank[4 + k][:, 0:SAMP], ptok[0:SAMP, 0, k * P:(k + 1) * P], cst[0:SAMP, C_ID:C_ID + SAMP])
                for u in range(2):
                    done = turn(bank[4 + k][:, SAMP + u * P:SAMP + (u + 1) * P], ptok[:, 1 + u, k * P:(k + 1) * P])
            done.then_inc(pt_mm, 1)
            norm(2, NT)
            pe.wait_ge(nrm_lo, 24)
            pe.wait_ge(pt_ready, 2)

            def embed(k, u):
                pe.wait_ge(wcol_in[u], 8 * (k - u) + 16)
                pe.wait_ge(x_done, 5 * KT + k - 1)
                mm(bank[2 + u][:, 0:NT], wcol[u][:, 0, :], pt[:, 0, :], True, False)
                mm(bank[2 + u][:, 0:NT], wcol[u][:, 1, :], pt[:, 1, :], False, True).then_inc(embed_mm, 1)

            phase(U_PLE, xh, xl, NB, NX, (sg_ready, 0), before, embed)
            for b in range(4):
                for k in range(4):
                    done = turn(bank[4 + b % 2][0:NOUTF, k * P:(k + 1) * P], outf[:, b * 4 + k, :])
                    if k == 0 and b >= 2:
                        pass
                done.then_inc(small_mm, 1)
                if b in (1, 2):
                    pe.wait_ge(small_read, b)
            pe.wait_ge(small_read, 4)
            norm(3, NT)
            for j in range(8):
                pe.wait_ge(nrm_ready, 24 + j + 1)
                if j >= 2:
                    pe.wait_ge(y_read, 3 * (j - 1))
                b3 = (2, 3, 4) if j % 2 == 0 else (5, 6, 1)
                for k in range(2):
                    kc = slice(k * P, (k + 1) * P)
                    turn(bank[b3[0]][0:SAMP, kc], nrm[j % 2][:, k, NB:NB + SAMP])
                    for u in range(2):
                        o = NB + SAMP + u * P
                        done = turn(bank[b3[1 + u]][:, kc], nrm[j % 2][:, k, o:o + P])
                done.then_inc(y_turn, 1)

        @block.scalar
        def _(act):
            def hi(n, slot, half):
                act.wait_ge(raw_in[slot], 16 * half + 16)
                if not (isinstance(n, int) and n < 2):
                    act.wait_ge(unit_done, n - 1)
                act.activation(wh[slot][:], raw[slot][:], ACT.Copy).then_inc(hi_done, 1)

            hi(0, 0, 0)
            hi(1, 1, 0)
            for b in range(4):
                act.wait_ge(xt_mm, 3 + b)
                act.activation(rga[:, 4 * b:4 * b + 4, 40:40 + P], bank[2 + b][:].rearrange("p (k t) -> p k t", k=4), ACT.Copy).then_inc(xt_act, 1)

            def norm(k, width):
                for j in range(8):
                    if j >= 2:
                        act.wait_ge(sum_mm, 8 * k + j - 1)
                    act.activation(nsq[j % 2][:, :, NX - width:], rga[:, 2 * j:2 * j + 2, NX - width:], ACT.Square).then_inc(sq_ready, 1)
                act.wait_ge(rms_var, k + 1)
                act.activation(sums[:, NX - width:], sums[:, NX - width:], ACT.Sqrt).then_inc(rms_std, 1)

            def norm_split(k, width, out):
                for j in range(8):
                    act.wait_ge(nrm_ready, 8 * k + j + 1)
                    act.activation(out[:, 2 * j:2 * j + 2, NX - width:], nrm[j % 2][:, :, NX - width:], ACT.Copy).then_inc(nrm_hi, 1)

            act.wait_ge(xt_dve, 6)
            act.wait_ge(xt_act, 4)
            norm(0, NX)
            norm_split(0, NX, xh)

            act.wait_ge(lam_abs, 1)
            act.activation(der_work[:, :, 1], der_work[:, :, 1], ACT.Exp, scale=-1.0).then_inc(lam_exp, 1)

            for n in range(4):
                act.wait_ge(unit_done, n + 1)
                if n:
                    act.wait_ge(low_mix, n)
                act.activation(ex[:], bank[n % 2][:, 0:NX], ACT.Copy).then_inc(low_ex, 1)
                if n < 3:
                    hi(n + 2, n % 2, n // 2 + 1)
            act.wait_ge(low_mix, 4)
            act.activation(low[0:RW, 0, :], low[0:RW, 0, :], ACT.Tanh).then_inc(low_ready, 1)
            act.activation(low[:, 2, :], low[:, 2, :], ACT.Sigmoid).then_inc(low_ready, 1)
            act.activation(low[:, 3, :], low[:, 3, :], ACT.Sigmoid).then_inc(low_ready, 1)

            def scalar(col):
                return ptc[:, col:col + 1]

            def stage(name, p):
                one = p + 1
                if name == "lowrank":
                    act.wait_ge(ptc_ready, one)
                    act.wait_ge(mixed, 3 * p + 1)
                    act.activation(ksq[:], zk[:], ACT.Square, scale=scalar(KK)).then_inc(ksq_ready, 1)
                    act.wait_ge(low_mm, one)
                    act.activation(siga[:], bank[3][:, 0:NT], ACT.Sigmoid, bias=scalar(A0)).then_inc(sig_ready, 1)
                    act.activation(sigw[:], bank[2][:, 0:NT], ACT.Sigmoid, bias=scalar(W0)).then_inc(sig_ready, 1)
                elif name == "rg_gates":
                    act.wait_ge(rgr_mm, one)
                    act.activation(rgr[:], bank[7][:, 0:NT], ACT.Sigmoid, bias=scalar(BA)).then_inc(rgr_sig, 1)
                    act.wait_ge(rgi_mm, one)
                    act.activation(rgi[:], bank[6][:, 0:NT], ACT.Sigmoid, bias=scalar(BX)).then_inc(rgi_sig, 1)
                    act.wait_ge(rgr_sig, one)
                    act.activation(th[:], rgr[:], ACT.Tanh, scale=dtc[:, SP8:SP8 + 1]).then_inc(th_ready, 1)
                elif name == "decay":
                    act.wait_ge(sig_ready, 2 * one)
                    act.activation(sigw[:], sigw[:], ACT.Exp, scale=-math.exp(-0.5)).then_inc(decay_ready, 1)
                    act.wait_ge(th_ready, one)
                    act.activation(rgr[:], rgr[:], ACT.Exp, scale=dtc[:, NSP8:NSP8 + 1]).then_inc(rg_exp, 1)
                elif name == "bonus":
                    act.wait_ge(ss_ready, one)
                    act.activation(rn[:], rn[:], ACT.Sqrt).then_inc(kk_root, 1)
                    act.wait_ge(m2_ready, one)
                    act.activation(m2[:], m2[:], ACT.Sqrt).then_inc(m_root, 1)
                elif name == "prep":
                    if not (isinstance(p, int) and p == 0):
                        act.wait_ge(rwo_ready, p)
                    act.activation(gout[:], bank[4][:, 0:NT], ACT.Copy).then_inc(low_read, 1)
                elif name == "turn":
                    act.wait_ge(turn_mm, one)
                    act.activation(tmb[:].rearrange("p a b -> p (a b)"), bank[2][:], ACT.Copy).then_inc(turn_read, 1)
                    act.activation(tmv[:].rearrange("p a b -> p (a b)"), bank[3][:, 0:256], ACT.Copy).then_inc(turn_read, 1)
                    act.activation(sbk[:], bank[3][0:64, 256:384], ACT.Copy).then_inc(turn_read, 1)
                    act.activation(svv[:], bank[3][0:64, 384:512], ACT.Copy).then_inc(turn_read, 1)
                    act.activation(suv[SAMP:2 * SAMP, :], bank[3][SAMP:2 * SAMP, 384:512], ACT.Copy).then_inc(turn_read, 1)
                elif name == "pairwise":
                    act.wait_ge(pair_mm, 5 * one)
                    for h in range(2):
                        act.activation(ab[:, 2 * h:2 * h + 2, :].rearrange("p a b -> p (a b)"), bank[2 + h][:, 0:256], ACT.Copy).then_inc(ab_read, 1)
                elif name[:6] == "invert" and name[7] == "a":
                    act.wait_ge(yy_mm, 5 * p + int(name[6]))
                    act.activation(yy[:].rearrange("p a b -> p (a b)"), bank[4][:], ACT.Copy).then_inc(yy_read, 1)
                elif name == "state_in":
                    act.wait_ge(state_mm, one)
                    for b in range(2):
                        act.activation(ms[:, 4 * b:4 * b + 4, :].rearrange("p a b -> p (a b)"), bank[2 + b][:], ACT.Copy).then_inc(state_read, 1)
                elif name == "samp_inv_a":
                    act.wait_ge(syy_mm, one)
                    act.activation(syy[:].rearrange("p a b -> p (a b)"), bank[2][0:SAMP, 0:2 * SAMP], ACT.Copy).then_inc(syy_read, 1)
                elif name == "samp_r":
                    act.wait_ge(sr_mm, one)
                    act.activation(sr[:], bank[2][0:SAMP, 0:P], ACT.Copy).then_inc(sr_read, 1)
                elif name == "samp_out":
                    act.wait_ge(so_mm, one)
                    act.activation(so[:].rearrange("p a b -> p (a b)"), bank[3][:], ACT.Copy).then_inc(so_ready, 1)
                elif name[0] == "r" and name[1:].isdigit():
                    c = int(name[1:])
                    rc = slice((c % 2) * CHUNK, (c % 2 + 1) * CHUNK)
                    act.wait_ge(r_mm, NCH * p + c + 1)
                    act.activation(rs[rc, :], bank[4][rc, 0:P], ACT.Copy).then_inc(r_read[c], 1)
                elif name == "mean":
                    act.wait_ge(fin_mm, one)
                    act.activation(sfin[:], bank[2][:, 0:P], ACT.Copy).then_inc(fin_read, 1)
                    act.wait_ge(y_mm, NCH * one)
                    act.activation(yf[:], bank[7][:, 0:NT], ACT.Copy).then_inc(yf_ready, 1)
                    act.wait_ge(yc_ready, one)
                    act.activation(ysq[:], yc[:], ACT.Square).then_inc(ysq_ready, 1)
                elif name == "var":
                    act.wait_ge(var_ready, one)
                    act.activation(sd[:], sd[:], ACT.Sqrt).then_inc(y_root, 1)

            def evict(u, it):
                if u == 0:
                    return
                act.wait_ge(unit_done, U_LOOP + it * LOOP_UNITS + u + 1)
                out = bank[u % 2]
                if u == 1:
                    if not (isinstance(it, int) and it == 0):
                        act.wait_ge(rga_ready, it)
                    act.activation(gg[:], out[:, 0:NT], ACT.Gelu_apprx_tanh).then_inc(gelu_ready, 1)
                elif u == 2:
                    if not (isinstance(it, int) and it == 0):
                        act.wait_ge(ga_saved, 16 * it)
                    act.activation(gat[:], out[:, 0:NT], ACT.Sigmoid).then_inc(ga_ready, 1)
                else:
                    if not (isinstance(it, int) and it == 0 and u == 3):
                        act.wait_ge(mixed, 3 * it + u - 3)
                    act.activation(ex[:], out[:, 0:NX], ACT.Copy).then_inc(ex_ready, 1)

            def gb_evict(u):
                act.wait_ge(unit_done, U_GB + u + 1)
                act.wait_ge(ga_saved, 16 * KT)
                if u:
                    act.wait_ge(gb_saved[(u - 1) % 2], 16 * ((u - 1) // 2 + 1))
                act.activation(gat[:], bank[u % 2][:, 0:NT], ACT.Sigmoid).then_inc(gb_ready, 1)

            def step(it, units, chain):
                for slot in range(SLOTS):
                    u, q = divmod(slot, 4)
                    if q == 0:
                        if units == "loop":
                            if u:
                                evict(u - 1, it)
                            elif chain:
                                evict(5, it - 1)
                            hi(U_LOOP + it * LOOP_UNITS + u + 1, (u + 1) % 2, (U_LOOP + u + 1) // 2 + it * (LOOP_UNITS // 2))
                        else:
                            if u:
                                gb_evict(u - 1)
                            else:
                                evict(5, it - 1)
                            hi(U_GB + u + 1, (u + 1) % 2, (U_GB + u + 1) // 2)
                    if chain:
                        for name in AT.get(slot, []):
                            stage(name, it - 1)

            step(0, "loop", False)
            with act.Fori(1, KT) as it:
                step(it, "loop", True)
            step(KT, "gb", True)
            gb_evict(5)
            hi(U_GB + 7, 1, (U_GB + 7) // 2)

            def phase(base, evict=None, start=0, split=True):
                last = KT // 2 if split else KT // 2 - 1
                with act.Fori(start // 2, last) as i:
                    for u in range(2):
                        if evict:
                            evict(2 * i + u, u, i)
                        hi(base + 2 * i + u + 2, u, base // 2 + i + 1)
                if not split:
                    for u in range(2):
                        evict(KT - 2 + u, u, KT // 2 - 1)

            def gb_evict_rest(k, u, i):
                act.wait_ge(unit_done, U_GB + k + 1)
                act.wait_ge(gb_saved[u], 16 * i)
                act.activation(tmp[u][:], bank[u][:, 0:NT], ACT.Sigmoid).then_inc(gb_ready, 1)

            act.wait_ge(rwo_ready, KT)
            act.wait_ge(y_mm, NCH * KT)
            phase(U_GB, gb_evict_rest, start=6)
            for j in range(4):
                if j == 0:
                    act.wait_ge(rga_ready, KT)
                act.activation(sbh[0][:, 4 * j:4 * j + 4, :], rga[:, 4 * j:4 * j + 4, NB:], ACT.Copy).then_inc(split_hi, 1)
            for j in range(4):
                act.activation(sbh[1][:, 4 * j:4 * j + 4, :], rwo[:, 4 * j:4 * j + 4, :], ACT.Copy).then_inc(split_hi, 1)
            phase(U_RGO)

            def split_merged(k, u, i):
                act.wait_ge(merged, KT + k + 1)
                act.activation(sbh[0][:, bass.ds(k, 1), :].rearrange("p o t -> p (o t)"), rwo[:, bass.ds(k, 1), :].rearrange("p o t -> p (o t)"), ACT.Copy).then_inc(merged_hi, 1)

            phase(U_RWO, split_merged)
            phase(U_WO)
            act.wait_ge(x_done, KT)
            norm(1, NT)
            norm_split(1, NT, xh)
            n = 0
            for kind, g in FFN_PLAN:
                base = U_FFN + n * KT

                def hidden(k, u, i, base=base, g=g):
                    act.wait_ge(unit_done, base + k + 1)
                    if not (g == 0 and isinstance(i, int)):
                        act.wait_ge(h_lo, KT * g + k - 1)
                    act.activation(tmp[u][:], bank[u][:, 0:NT], ACT.Relu).then_inc(h_relu, 1)
                    act.wait_ge(h_relu, KT * g + k + 1)
                    act.activation(tmp[u][:], tmp[u][:], ACT.Square).then_inc(h_sq, 1)
                    act.wait_ge(h_sq, KT * g + k + 1)
                    act.activation(sbh[g % 2][:, bass.ds(k, 1), :].rearrange("p o t -> p (o t)"), tmp[u][:], ACT.Copy).then_inc(h_hi, 1)

                if kind == "up" and g == 0:
                    for u in range(2):
                        hidden(u, u, 0)
                        hi(base + u + 2, u, base // 2 + 1)
                    phase(base, lambda k, u, i, h=hidden: h(k, u, i), start=2)
                else:
                    phase(base, hidden if kind == "up" else None)
                n += 1
            act.wait_ge(x_done, 5 * KT)
            norm(2, NT)
            norm_split(2, NT, xh)

            def ple_gate(k, u, i):
                act.wait_ge(unit_done, U_PLE + k + 1)
                act.wait_ge(x_done, 5 * KT + k - 1)
                act.activation(tmp[u][:], bank[u][:, 0:NT], ACT.Sigmoid).then_inc(sg_ready, 1)

            phase(U_PLE, ple_gate, split=False)
            for b in range(4):
                act.wait_ge(small_mm, b + 1)
                act.activation(small_out[:, b * 512:(b + 1) * 512], bank[4 + b % 2][0:NOUTF, :], ACT.Copy).then_inc(small_read, 1)
            act.wait_ge(x_done, 6 * KT)
            norm(3, NT)
            for j in range(8):
                act.wait_ge(y_turn, j + 1)
                b3 = (2, 3, 4) if j % 2 == 0 else (5, 6, 1)
                cols = slice(j * 256, (j + 1) * 256)
                act.activation(ytok[0:SAMP, 0, cols], bank[b3[0]][0:SAMP, 0:256], ACT.Copy).then_inc(y_read, 1)
                for u in range(2):
                    act.activation(ytok[:, 1 + u, cols], bank[b3[1 + u]][:, 0:256], ACT.Copy).then_inc(y_read, 1)

        @block.vector
        def _(dve):
            def lo(n, slot):
                dve.wait_ge(hi_done, n + 1)
                dve.tensor_tensor(wl[slot][:], raw[slot][:], wh[slot][:].bitcast(F32), ALU.subtract).then_inc(lo_done, 1)

            def tt_(out, x, y, op):
                return dve.tensor_tensor(out, x, y, op)

            def stt(out, x, s, y, op0, op1):
                return dve.scalar_tensor_tensor(out, x, s, y, op0, op1)

            def ts(out, x, s1, s2=None, op0=ALU.mult, op1=ALU.bypass):
                return dve.tensor_scalar(out, x, s1, s2, op0, op1)

            lo(0, 0)
            lo(1, 1)
            for b in range(2):
                dve.wait_ge(xt_mm, b + 1)
                dve.tensor_copy(rga[:, 8 * b:8 * b + 8, 0:40], bank[b][:, 0:320].rearrange("p (k t) -> p k t", k=8)).then_inc(xt_dve, 1)
            for b in range(2):
                dve.wait_ge(par_mm, b + 1)
                dve.tensor_copy(par[:, 8 * b:8 * b + 8, :], bank[6 + b][:, 0:8 * NPAR].rearrange("p (k t) -> p k t", k=8)).then_inc(par_ready, 1)
            for b in range(4):
                dve.wait_ge(xt_mm, 7 + b)
                dve.tensor_copy(rga[:, 4 * b:4 * b + 4, 40 + P:NX], bank[b][:].rearrange("p (k t) -> p k t", k=4)).then_inc(xt_dve, 1)

            def norm(k, width, gain, split):
                first = NX - width
                dve.wait_ge(sum_mm, 8 * k + 8)
                ts(sums[:, first:], bank[7][:, 0:width], EPS, op0=ALU.add).then_inc(rms_var, 1)
                dve.wait_ge(rms_std, k + 1)
                dve.reciprocal(sums[:, first:], sums[:, first:]).then_inc(rms_inv, 1)
                dve.wait_ge(rms_inv, k + 1)

                def low_part(j):
                    dve.wait_ge(nrm_hi, 8 * k + j + 1)
                    tt_(split[1][:, 2 * j:2 * j + 2, first:], nrm[j % 2][:, :, first:], split[0][:, 2 * j:2 * j + 2, first:].bitcast(F32),
                        ALU.subtract).then_inc(nrm_lo, 1)

                for j in range(8):
                    n = nrm[j % 2]
                    if j >= 2:
                        if split:
                            dve.wait_ge(nrm_lo, 8 * k + j - 1)
                        else:
                            dve.wait_ge(y_turn, j - 1)
                    x2, m = rga[:, 2 * j:2 * j + 2, NB:], 8 * k + j + 1
                    if k == 0:
                        dve.wait_ge(nrm_copy, j - 1) if j >= 2 else None
                        dve.tensor_copy(n[:, :, 0:NB], rga[:, 2 * j:2 * j + 2, 0:NB])
                    tt_(n[:, :, NB:], x2, par[:, 2 * j:2 * j + 2, gain:gain + 1].to_broadcast([P, 2, NT]), ALU.mult).then_inc(nrm_gain, 1)
                    dve.wait_ge(nrm_gain, m)
                    tt_(n[:, :, NB:], n[:, :, NB:], sums[:, NB:].unsqueeze(1).to_broadcast([P, 2, NT]), ALU.mult).then_inc(nrm_ready, 1)
                    if k == 0:
                        dve.wait_ge(nrm_ready, m)
                        dve.tensor_copy(outf[:, 2 * j:2 * j + 2, O_SHIFT:O_SHIFT + 1], n[:, :, NX - 1:NX])
                        dve.tensor_copy(outf[:, 2 * j:2 * j + 2, O_SHIFT + 1:O_SHIFT + 1 + NB], n[:, :, NB + SAMP - NB:NB + SAMP]).then_inc(nrm_copy, 1)
                    if split and j:
                        low_part(j - 1)
                if split:
                    low_part(7)

            norm(0, NX, GMIX, (xh, xl))

            head = Count(der_step, 0, 0)
            lam = par[:, :, LAM]
            w1, w2, w3, w4 = (der_work[:, :, k] for k in range(4))
            ts(w1, lam, -1.0).then_inc(head.sem, head.one())
            dve.wait_ge(head.sem, head.so_far())
            tt_(w1, w1, lam, ALU.max).then_inc(head.sem, head.one())
            dve.wait_ge(head.sem, head.so_far())
            dve.tensor_copy(w2, w1).then_inc(lam_abs, 1)
            dve.wait_ge(lam_exp, 1)
            ts(w3, w2, 2.0, op0=ALU.add).then_inc(head.sem, head.one())
            dve.wait_ge(head.sem, head.so_far())
            dve.reciprocal(w3, w3).then_inc(head.sem, head.one())
            dve.wait_ge(head.sem, head.so_far())
            tt_(w2, w2, w3, ALU.mult).then_inc(head.sem, head.one())
            dve.wait_ge(head.sem, head.so_far())
            tt_(w3, w2, w2, ALU.mult).then_inc(head.sem, head.one())
            dve.memset(w4, 1.0 / 19).then_inc(head.sem, head.one())
            dve.wait_ge(head.sem, head.so_far())
            for k in range(8, -1, -1):
                tt_(w4, w4, w3, ALU.mult).then_inc(head.sem, head.one())
                dve.wait_ge(head.sem, head.so_far())
                ts(w4, w4, 1.0 / (2 * k + 1), op0=ALU.add).then_inc(head.sem, head.one())
                dve.wait_ge(head.sem, head.so_far())
            tt_(w4, w4, w2, ALU.mult).then_inc(head.sem, head.one())
            ts(w1, lam, -1.0, 0.0, ALU.mult, ALU.max).then_inc(head.sem, head.one())
            dve.wait_ge(head.sem, head.so_far())
            stt(w4, w4, 2.0, w1, ALU.mult, ALU.add).then_inc(head.sem, head.one())
            dve.wait_ge(head.sem, head.so_far())
            ts(der[:, :, SP8], w4, 8.0).then_inc(head.sem, head.one())
            ts(der[:, :, NSP8], w4, -8.0).then_inc(head.sem, head.one())
            ts(der[:, :, OMKA], par[:, :, KA], -1.0, 1.0, ALU.mult, ALU.add).then_inc(head.sem, head.one())
            dve.wait_ge(head.sem, head.so_far())

            def shift_mix(mu, z, chain, done):
                tt_(dif[:, 0:SAMP], ex[:, 0:SAMP], ex[:, NB:NB + SAMP], ALU.subtract).then_inc(chain.sem, chain.one())
                ts(dif[:, SAMP:SAMP + 1], ex[:, NB + SAMP:NB + SAMP + 1], -1.0).then_inc(chain.sem, chain.one())
                tt_(dif[:, SAMP + 1:NT], ex[:, NB + SAMP:NX - 1], ex[:, NB + SAMP + 1:NX], ALU.subtract).then_inc(chain.sem, chain.one())
                dve.wait_ge(chain.sem, chain.so_far())
                stt(z, dif[:], mu, ex[:, NB:NX], ALU.mult, ALU.add).then_inc(done, 1)

            for n in range(4):
                dve.wait_ge(low_ex, n + 1)
                if n:
                    dve.wait_ge(low_mix, n)
                shift_mix(par[:, 0, MULOW + n:MULOW + n + 1], low[:, n, :], head, low_mix)
                if n < 3:
                    lo(n + 2, n % 2)

            def conv(it, chain):
                dve.wait_ge(unit_done, U_LOOP + it * LOOP_UNITS + 1)
                if isinstance(it, int) and it == 0:
                    dve.wait_ge(init_done, N_INIT)
                else:
                    dve.wait_ge(rgi_mm, it)
                dve.tensor_copy(ue[:, 24:24 + SAMP], bank[0][:, 0:SAMP]).then_inc(chain.sem, chain.one())
                dve.tensor_copy(ue[:, 59:315], bank[0][:, SAMP:NT]).then_inc(ue_ready, 1)
                dve.tensor_copy(ue[:, 0:24], ptu[:, CONV_STATE:CONV_STATE + 24]).then_inc(chain.sem, chain.one())
                dve.wait_ge(chain.sem, chain.so_far())
                dve.wait_ge(ue_ready, it + 1)
                parts = ((0, SAMP, 0, NB), (SAMP, NT, 56, 1))
                for x0, x1, o, by in parts:
                    ts(xc[:, x0:x1], ue[:, o:o + x1 - x0], ptu[:, CW:CW + 1], ptu[:, CB:CB + 1], ALU.mult, ALU.add).then_inc(chain.sem, chain.one())
                for j in range(1, 4):
                    dve.wait_ge(chain.sem, chain.so_far())
                    for x0, x1, o, by in parts:
                        ins = stt(xc[:, x0:x1], ue[:, o + j * by:o + j * by + x1 - x0], ptu[:, CW + j:CW + j + 1], xc[:, x0:x1], ALU.mult, ALU.add)
                        if j == 3 and x0:
                            ins.then_inc(conv_ready, 1)
                        else:
                            ins.then_inc(chain.sem, chain.one())
                dve.tensor_copy(outf[:, bass.ds(it, 1), O_CONV:O_CONV + 3].rearrange("p o t -> p (o t)"), ue[:, 312:315]).then_inc(chain.sem, chain.one())
                dve.tensor_copy(outf[:, bass.ds(it, 1), O_CONV + 3:NOUTF].rearrange("p o t -> p (o t)"), ue[:, 24 + NB:24 + SAMP]).then_inc(chain.sem, chain.one())

            def scalar(col):
                return ptc[:, col:col + 1]

            def stage(name, p, ch):
                one = p + 1
                later = not (isinstance(p, int) and p == 0)
                if name == "params":
                    if later:
                        dve.wait_ge(rwo_ready, p)
                        dve.wait_ge(m_ready, NCH * p)
                        dve.wait_ge(sexp_ready, p)
                    dve.tensor_copy(dtc[:], der[:, bass.ds(p, 1), :].rearrange("p o t -> p (o t)")).then_inc(ch.sem, ch.one())
                    dve.tensor_copy(ptc[:], par[:, bass.ds(p, 1), :].rearrange("p o t -> p (o t)")).then_inc(ptc_ready, 1)
                    dve.wait_ge(ptc_ready, one)
                elif name == "mix_v":
                    dve.wait_ge(ex_ready, 3 * p + 3)
                    dve.wait_ge(mixed, 3 * p + 2)
                    shift_mix(scalar(MUV), zv[:], ch, mixed)
                elif name == "kk_norm":
                    dve.wait_ge(kk_mm, one)
                    dve.wait_ge(mixed, 3 * one)
                    ts(rn[:], bank[5][:, 0:NT], 1e-24, op0=ALU.max).then_inc(ss_ready, 1)
                elif name == "rg_gates":
                    dve.wait_ge(sig_ready, 2 * one)
                    ts(kp[:], siga[:], scalar(KA), dtc[:, OMKA:OMKA + 1], ALU.mult, ALU.add).then_inc(ch.sem, ch.one())
                    stt(bv[:], zr[:], scalar(RK), zk[:], ALU.mult, ALU.mult).then_inc(ch.sem, ch.one())
                    dve.wait_ge(ch.sem, ch.so_far())
                    dve_bt = tt_(bv[:], bv[:], kp[:], ALU.mult)
                    dve_bt.then_inc(bt_ready, 1)
                    dve.wait_ge(bt_ready, one)
                    tt_(kp[:], kp[:], zk[:], ALU.mult).then_inc(ch.sem, ch.one())
                    dve.wait_ge(rgi_sig, one)
                    tt_(rgi[:], rgi[:], xc[:], ALU.mult).then_inc(ch.sem, ch.one())
                elif name == "decay":
                    dve.wait_ge(rg_exp, one)
                    tt_(m2[:], rgr[:], rgr[:], ALU.mult).then_inc(ch.sem, ch.one())
                    dve.wait_ge(ch.sem, ch.so_far())
                    stt(m2[:], m2[:], 1.0, th[:], ALU.add, ALU.mult).then_inc(m2_ready, 1)
                elif name == "bonus":
                    dve.wait_ge(bonus_mm, one)
                    dve.wait_ge(bt_ready, one)
                    tt_(bv[:], bank[6][:, 0:NT], zv[:], ALU.mult).then_inc(ch.sem, ch.one())
                elif name == "prep":
                    dve.wait_ge(kk_root, one)
                    dve.reciprocal(rn[:], rn[:]).then_inc(ch.sem, ch.one())
                    dve.wait_ge(decay_ready, one)
                    for c in range(NCH):
                        o = 5 * NB + c * (CHUNK + 1) + 1
                        dve.tensor_tensor_scan(cum[:, o:o + CHUNK], sigw[:, SAMP + c * CHUNK:SAMP + (c + 1) * CHUNK], zeros[:], 1.0, ALU.mult, ALU.add).then_inc(ch.sem, ch.one())
                    for t in range(NS):
                        dve.wait_ge(ch.sem, ch.so_far())
                        tt_(cum[:, (t + 1) * NB:(t + 2) * NB], cum[:, t * NB:(t + 1) * NB], sigw[:, t * NB:(t + 1) * NB], ALU.mult).then_inc(ch.sem, ch.one())
                    stt(kkn[:], zk[:], scalar(KK), rn[:], ALU.mult, ALU.mult).then_inc(ch.sem, ch.one())
                    dve.wait_ge(ch.sem, ch.so_far())
                    before, at = cum_of("before"), cum_of("at")
                    stt(ar[:, 0, samp_all], kkn[:, samp_all], -1.0, before[0], ALU.mult, ALU.mult).then_inc(ch.sem, ch.one())
                    stt(chunks(ar[:, 0, :]), chunks(kkn[:]), -1.0, before[1], ALU.mult, ALU.mult).then_inc(ch.sem, ch.one())
                    tt_(ar[:, 1, samp_all], zr[:, samp_all], at[0], ALU.mult).then_inc(ch.sem, ch.one())
                    tt_(chunks(ar[:, 1, :]), chunks(zr[:]), at[1], ALU.mult).then_inc(ch.sem, ch.one())
                    dve.reciprocal(rn[:, samp_all], at[0]).then_inc(ch.sem, ch.one())
                    dve.reciprocal(chunks(rn[:]), at[1]).then_inc(ch.sem, ch.one())
                    dve.wait_ge(ch.sem, ch.so_far())
                    tt_(kkn[:], kkn[:], siga[:], ALU.mult).then_inc(ch.sem, ch.one())
                    dve.wait_ge(ch.sem, ch.so_far())
                    tt_(btl[:], kkn[:], rn[:], ALU.mult).then_inc(ch.sem, ch.one())
                    tt_(ktl[:], kp[:], rn[:], ALU.mult).then_inc(ch.sem, ch.one())
                    dve.wait_ge(ch.sem, ch.so_far())
                    last = cum[:, NS * NB:(NS + 1) * NB].unsqueeze(1).to_broadcast([P, NS, NB])
                    for k, src in enumerate((btl, ktl)):
                        tt_(bkh[:, k * SAMP:(k + 1) * SAMP].rearrange("p (t b) -> p t b", b=NB),
                               src[:, samp_all].rearrange("p (t b) -> p t b", b=NB), last, ALU.mult).then_inc(ch.sem, ch.one())
                    dve.tensor_copy(vv[:, 0:SAMP], zv[:, samp_all]).then_inc(ch.sem, ch.one())
                    dve.tensor_copy(vv[:, SAMP:], zv[:, samp_all]).then_inc(prep_done, 1)
                elif name == "rg_scan":
                    dve.wait_ge(m_root, one)
                    dve.memset(m2[:, SAMP:SAMP + 1], 1.0).then_inc(ch.sem, ch.one())
                    dve.wait_ge(ch.sem, ch.so_far())
                    tt_(m2[:], m2[:], rgi[:], ALU.mult).then_inc(ch.sem, ch.one())
                    dve.wait_ge(ch.sem, ch.so_far())
                    dve.tensor_tensor_scan(th[:, SAMP:NT], rgr[:, SAMP:NT], m2[:, SAMP:NT], 0.0, ALU.mult, ALU.add).then_inc(ch.sem, ch.one())
                    for t in range(NS):
                        now = slice(t * NB, (t + 1) * NB)
                        prev = ptc[:, H_STATE:H_STATE + NB] if t == 0 else th[:, (t - 1) * NB:t * NB]
                        tt_(th[:, now], rgr[:, now], prev, ALU.mult).then_inc(ch.sem, ch.one())
                        dve.wait_ge(ch.sem, ch.so_far())
                        tt_(th[:, now], th[:, now], m2[:, now], ALU.add).then_inc(ch.sem, ch.one())
                        dve.wait_ge(ch.sem, ch.so_far())
                    dve.tensor_copy(outf[:, bass.ds(p, 1), O_H:O_H + 1].rearrange("p o t -> p (o t)"), th[:, NT - 1:NT]).then_inc(ch.sem, ch.one())
                    dve.tensor_copy(outf[:, bass.ds(p, 1), O_H + 1:O_H + 1 + NB].rearrange("p o t -> p (o t)"), th[:, SAMP - NB:SAMP]).then_inc(ch.sem, ch.one())
                    dve.wait_ge(gelu_ready, one)
                    if not later:
                        dve.wait_ge(xt_saved, 16)
                    tt_(rga[:, bass.ds(p, 1), NB:].rearrange("p o t -> p (o t)"), th[:], gg[:], ALU.mult).then_inc(rga_ready, 1)
                elif name == "pairwise":
                    masks = cst[:, C_AM:C_AM + 512]
                    for g in range(2):
                        for h in range(2):
                            dve.wait_ge(pair_mm, 5 * p + 2 * g + h + 1)
                            tt_(ams[:, 2 * h + g, :], bank[4 + 2 * g + h][:], masks, ALU.mult).then_inc(pair_read, 1)
                    dve.wait_ge(ab_read, 2 * one)
                    tt_(tn[:], ab[:], cst[:, C_LM:C_LM + P].unsqueeze(1).to_broadcast([P, 4, P]), ALU.mult).then_inc(ch.sem, ch.one())
                    eye = ident.unsqueeze(1).to_broadcast([P, 4, P])
                    dve.wait_ge(pair_read, 4 * one)
                    tt_(tt[:], ams[:, :, 0:P], eye, ALU.add).then_inc(ch.sem, ch.one())
                    dve.wait_ge(ch.sem, ch.so_far())
                    tt_(tn[:], tn[:], eye, ALU.add).then_inc(t_start, 1)
                    dve.wait_ge(t_start, one)
                elif name[:6] == "invert" and name[7] == "b":
                    l = int(name[6])
                    dve.wait_ge(tn_mm, 5 * p + l)
                    if l > 1:
                        dve.wait_ge(tn_ready, 5 * p + l - 1)
                    flat = "p a b -> p (a b)"
                    if l < 5:
                        tt_(tt[:].rearrange(flat), tt[:].rearrange(flat), bank[5][:], ALU.add).then_inc(ch.sem, ch.one())
                        tt_(tn[:].rearrange(flat), tn[:].rearrange(flat), bank[6][:], ALU.add).then_inc(tn_ready, 1)
                        dve.wait_ge(ch.sem, ch.so_far())
                    else:
                        tt_(tt[:].rearrange(flat), tt[:].rearrange(flat), bank[5][:], ALU.add).then_inc(tn_ready, 1)
                elif name == "samp_prep":
                    tt_(aex[:], ar[:, 0, samp_all].unsqueeze(1).to_broadcast([P, NB, SAMP]),
                           cst[:, C_SEQ:C_SEQ + 256].rearrange("p (b t) -> p b t", b=NB), ALU.mult).then_inc(ch.sem, ch.one())
                    dve.wait_ge(turn_read, 5 * one)
                    own = cst[0:2 * SAMP, C_SQT:C_SQT + NB].unsqueeze(2).to_broadcast([2 * SAMP, NB, HEAD])
                    for h in range(2):
                        tt_(bke[:, h, :].rearrange("p (b j) -> p b j", b=NB),
                               sbk[:, h * HEAD:(h + 1) * HEAD].unsqueeze(1).to_broadcast([2 * SAMP, NB, HEAD]), own, ALU.mult).then_inc(ch.sem, ch.one())
                    if later:
                        dve.wait_ge(so_saved, 16 * p)
                    tt_(dg[:], cst[:, C_ID2:C_ID2 + HEAD].unsqueeze(1).to_broadcast([P, NB, HEAD]),
                        cum[:, NS * NB:(NS + 1) * NB].unsqueeze(2).to_broadcast([P, NB, HEAD]), ALU.mult).then_inc(sexp_ready, 1)
                elif name == "samp_pair":
                    dve.wait_ge(spair_mm, one)
                    for h in range(2):
                        tt_(sam[:, h, :], bank[2 + h][0:SAMP, 0:128], cst[0:SAMP, C_SAM:C_SAM + 128], ALU.mult).then_inc(ch.sem, ch.one())
                        tt_(stn[:, h, :], bank[2 + h][0:SAMP, 128:160], cst[0:SAMP, C_SLM:C_SLM + SAMP], ALU.mult).then_inc(ch.sem, ch.one())
                        tt_(sa2[:, h, :], bank[2 + h][0:SAMP, 128:160], cst[0:SAMP, C_SLM + SAMP:C_SLM + 2 * SAMP], ALU.mult).then_inc(ch.sem, ch.one())
                    dve.wait_ge(ch.sem, ch.so_far())
                    eye = cst[0:SAMP, C_ID:C_ID + SAMP].unsqueeze(1).to_broadcast([SAMP, 2, SAMP])
                    tt_(stn[:], stn[:], eye, ALU.add).then_inc(ch.sem, ch.one())
                    tt_(stt_s[:], sam[:, :, 0:SAMP], eye, ALU.add).then_inc(sinv_ready, 1)
                    dve.wait_ge(sinv_ready, one)
                elif name == "samp_inv_b":
                    dve.wait_ge(stt_mm, one)
                    flat = "p a b -> p (a b)"
                    tt_(stt_s[:].rearrange(flat), stt_s[:].rearrange(flat), bank[3][0:SAMP, 0:2 * SAMP], ALU.add).then_inc(stt_ready, 1)
                elif name == "samp_u":
                    dve.wait_ge(su_mm, one)
                    dve.tensor_copy(suv[0:SAMP, :], bank[3][0:SAMP, 0:P]).then_inc(su_read, 1)
                elif name[0] == "u":
                    c = int(name[1:])
                    rc = slice((c % 2) * CHUNK, (c % 2 + 1) * CHUNK)
                    dve.wait_ge(u_mm, NCH * p + c + 1)
                    dve.tensor_copy(us[rc, :], bank[5][rc, 0:P]).then_inc(u_read, 1)
                elif name[:2] == "my":
                    c = int(name[2:])
                    dve.wait_ge(m_mm, NCH * p + c + 1)
                    new = mp[(c + 1) % 2]
                    if c:
                        if c == 1 and later:
                            dve.wait_ge(fin_saved, 32 * p)
                        dve.wait_ge(m_ready, NCH * p + c)
                        tt_(mtmp[:], mp[c % 2][:], bank[6][:, 0:P], ALU.add).then_inc(ch.sem, ch.one())
                        dve.wait_ge(ch.sem, ch.so_far())
                        stt(new[:], mtmp[:], last_decay(c), bd, ALU.mult, ALU.mult).then_inc(m_ready, 1)
                    else:
                        stt(new[:], bank[6][:, 0:P], last_decay(c), bd, ALU.mult, ALU.mult).then_inc(m_ready, 1)
                elif name == "mean":
                    dve.wait_ge(mean_mm, one)
                    stt(yc[:], bank[4][:, 0:NT], -1.0 / HEAD, yf[:], ALU.mult, ALU.add).then_inc(yc_ready, 1)
                elif name == "var":
                    dve.wait_ge(var_mm, one)
                    ts(sd[:], bank[5][:, 0:NT], 1.0 / HEAD, GN_EPS, ALU.mult, ALU.add).then_inc(var_ready, 1)
                    dve.wait_ge(y_root, one)
                    dve.reciprocal(sd[:], sd[:]).then_inc(ch.sem, ch.one())
                    dve.wait_ge(ch.sem, ch.so_far())
                    stt(yc[:], yc[:], scalar(GNW), sd[:], ALU.mult, ALU.mult).then_inc(ch.sem, ch.one())
                    dve.wait_ge(ch.sem, ch.so_far())
                    stt(yc[:], yc[:], scalar(GNB), bv[:], ALU.add, ALU.add).then_inc(ch.sem, ch.one())
                    dve.wait_ge(ch.sem, ch.so_far())
                    tt_(rwo[:, bass.ds(p, 1), :].rearrange("p o t -> p (o t)"), yc[:], gout[:], ALU.mult).then_inc(rwo_ready, 1)

            def step(it, units, chain):
                rg = Count(dve_rg, it, STEPS["dve_rg"])
                ch = Count(dve_ch, it - 1, STEPS["dve_ch"])
                for slot in range(SLOTS):
                    u, q = divmod(slot, 4)
                    if q == 0:
                        if units == "loop":
                            if u == 0:
                                if chain:
                                    dve.wait_ge(rg.sem, rg.so_far())
                                    dve.wait_ge(mixed, 3 * it - 1)
                                dve.tensor_copy(ptu[:], par[:, bass.ds(it, 1), :].rearrange("p o t -> p (o t)")).then_inc(rg.sem, rg.one())
                            elif u == 1:
                                dve.wait_ge(rg.sem, rg.so_far())
                                if chain:
                                    dve.wait_ge(ch.sem, ch.so_far())
                                conv(it, rg)
                            elif u >= 4:
                                dve.wait_ge(ex_ready, 3 * it + u - 3)
                                if chain:
                                    dve.wait_ge(ch.sem, ch.so_far())
                                if not (isinstance(it, int) and it == 0 and u == 4):
                                    dve.wait_ge(mixed, 3 * it + u - 4)
                                shift_mix(ptu[:, (MUK, MUR)[u - 4]:(MUK, MUR)[u - 4] + 1], (zk, zr)[u - 4][:], rg, mixed)
                            lo(U_LOOP + it * LOOP_UNITS + u + 1, (u + 1) % 2)
                        else:
                            lo(U_GB + u + 1, (u + 1) % 2)
                    if chain:
                        for name in AT.get(slot, []):
                            stage(name, it - 1, ch)
                if units == "loop":
                    rg.end()
                if chain:
                    ch.end()

            step(0, "loop", False)
            with dve.Fori(1, KT) as it:
                step(it, "loop", True)
            step(KT, "gb", True)
            lo(U_GB + 7, 1)

            def phase(base, evict=None, start=0, split=True):
                with dve.Fori(start // 2, KT // 2 if split else KT // 2 - 1) as i:
                    for u in range(2):
                        if evict:
                            evict(2 * i + u, u, i)
                        lo(base + 2 * i + u + 2, u)
                if not split:
                    for u in range(2):
                        evict(KT - 2 + u, u, KT // 2 - 1)

            def tile(buf, k, first=0):
                return buf[:, bass.ds(k, 1), first:].rearrange("p o t -> p (o t)")

            phase(U_GB, start=6)
            for b, src in enumerate((rga[:, :, NB:], rwo[:])):
                for j in range(4):
                    dve.wait_ge(split_hi, 4 * b + j + 1)
                    tt_(sbl[b][:, 4 * j:4 * j + 4, :], src[:, 4 * j:4 * j + 4, :], sbh[b][:, 4 * j:4 * j + 4, :].bitcast(F32),
                        ALU.subtract).then_inc(split_lo, 1)

            def merge_a(k, u, i):
                dve.wait_ge(unit_done, U_RGO + k + 1)
                dve.wait_ge(g_in[u], 16 * i + 16)
                tt_(tile(rwo, k), bank[u][:, 0:NT], gt[u][:], ALU.mult).then_inc(merged, 1)

            def merge_b(k, u, i):
                dve.wait_ge(unit_done, U_RWO + k + 1)
                dve.wait_ge(g_in[u], 16 * (KT // 2) + 16 * i + 16)
                tt_(tmp[u][:], bank[u][:, 0:NT], gt[u][:], ALU.mult).then_inc(gated, 1)
                dve.wait_ge(gated, k + 1)
                tt_(tile(rwo, k), tile(rwo, k), tmp[u][:], ALU.add).then_inc(merged, 1)
                dve.wait_ge(merged_hi, k + 1)
                tt_(tile(sbl[0], k), tile(rwo, k), tile(sbh[0], k).bitcast(F32), ALU.subtract).then_inc(merged_lo, 1)

            def residual(base):
                def evict(k, u, i):
                    dve.wait_ge(unit_done, base + k + 1)
                    tt_(tile(rga, k, NB), tile(rga, k, NB), bank[u][:, 0:NT], ALU.add).then_inc(x_done, 1)
                return evict

            dve.wait_ge(split_lo, 8)
            phase(U_RGO, merge_a)
            phase(U_RWO, merge_b)
            dve.wait_ge(x_back, 16)
            phase(U_WO, residual(U_WO))
            norm(1, NT, GFFN, (xh, xl))
            n = 0
            for kind, g in FFN_PLAN:
                def hidden_lo(k, u, i, g=g):
                    dve.wait_ge(h_hi, KT * g + k + 1)
                    tt_(tile(sbl[g % 2], k), tmp[u][:], tile(sbh[g % 2], k).bitcast(F32), ALU.subtract).then_inc(h_lo, 1)

                base = U_FFN + n * KT
                if kind == "down":
                    dve.wait_ge(x_done, (g + 1) * KT)
                phase(base, hidden_lo if kind == "up" else residual(base))
                n += 1
            dve.wait_ge(pt_mm, 1)
            for k in range(2):
                dve.tensor_copy(pt[:, k, :], bank[4 + k][:, 0:NT]).then_inc(pt_ready, 1)
            dve.wait_ge(x_done, 5 * KT)
            norm(2, NT, GPLE, (xh, xl))

            def embed(k, u, i):
                dve.wait_ge(sg_ready, k + 1)
                dve.wait_ge(embed_mm, k + 1)
                tt_(tmp[u][:], tmp[u][:], bank[2 + u][:, 0:NT], ALU.mult).then_inc(tmp_ready, 1)
                dve.wait_ge(tmp_ready, k + 1)
                tt_(tile(rga, k, NB), tile(rga, k, NB), tmp[u][:], ALU.add).then_inc(x_done, 1)

            phase(U_PLE, embed, split=False)
            dve.wait_ge(x_done, 6 * KT)
            norm(3, NT, GFIN, None)

        @block.gpsimd
        def _(pool):
            pool.memset(rows[0:NPAR, :], 0.0).then_inc(rows_zero, 1)
            pool.wait_ge(par_ready, 2)
            pool.wait_ge(nrm_lo, 8)
            pool.wait_ge(nrm_copy, 8)
            for view, value in ((s0[:], 0.0), (cum[:], 1.0), (zeros[:], 0.0), (ue[:], 0.0)):
                pool.memset(view, value).then_inc(init_done, 1)

            def masked(p):
                pool.wait_ge(ab_read, 2 * (p + 1))
                for l in range(1, 6):
                    if l > 2:
                        pool.wait_ge(yy_mm, 5 * p + l - 2)
                    elif not (isinstance(p, int) and p == 0):
                        pool.wait_ge(yy_mm, 5 * p)
                    mask = cst[:, C_LM + l * P:C_LM + (l + 1) * P].unsqueeze(1).to_broadcast([P, 4, P])
                    pool.tensor_tensor(am[l % 2][:], ab[:], mask, ALU.mult).then_inc(am_ready, 1)

            masked(0)
            with pool.Fori(1, KT) as p:
                masked(p)


_INS = ['x_prompt', 'x_sample', 'p_prompt', 'p_sample', 'state_rg_h', 'state_rg_conv', 'state_rwkv', 'state_shift',
        'norm_mix', 'w_in', 'conv_w', 'conv_b', 'rg_wa', 'rg_ba', 'rg_wx', 'rg_bx', 'rg_lam', 'w_rg_o', 'mu_shift',
        'rw_w0', 'rw_w2', 'rw_a0', 'rw_a2', 'rw_g2', 'rw_kk', 'rw_ka', 'rw_rk', 'rw_gn_w', 'rw_gn_b', 'w_rw_o', 'w_o',
        'norm_ffn', 'w_up', 'w_down', 'norm_ple', 'w_ple_gate', 'w_ple', 'norm_f']
_OUTS = [("o_y_p", (1, SEQ, D)), ("o_y_s", (NB, NS, D)), ("o_h_p", (1, 1, D)), ("o_conv_p", (1, 1, 3, D)),
         ("o_rwkv_p", (1, 1, D // HEAD, HEAD, HEAD)), ("o_shift_p", (1, 1, D)),
         ("o_h_s", (1, NB, D)), ("o_conv_s", (1, NB, 3, D)), ("o_rwkv_s", (1, NB, D // HEAD, HEAD, HEAD)),
         ("o_shift_s", (1, NB, D))]


def kernel(**inputs):
    import concourse.bacc as _bacc
    from concourse.bass_utils import run_bass_kernel_spmd as _run

    nc = _bacc.Bacc("TRN2", target_bir_lowering=False, num_devices=1, dynamic_dma_scratch_size=1024)
    arrays, aps = {}, {}
    for name in _INS:
        x = np.ascontiguousarray(inputs[name])
        arrays[name] = x
        aps[name] = nc.dram_tensor(name, x.shape, mybir.dt.from_np(x.dtype), kind="ExternalInput").ap()
    arrays["const"] = constants()
    aps["const"] = nc.dram_tensor("const", arrays["const"].shape, F32, kind="ExternalInput").ap()
    for name, shape in _OUTS:
        aps[name] = nc.dram_tensor(name, shape, F32, kind="ExternalOutput").ap()
    program(nc, aps)
    r = _run(nc, [arrays], core_ids=[0])
    return tuple(r.results[0][name] for name, _ in _OUTS)
```

```python
import math
from contextlib import ExitStack

import numpy as np
import concourse.bass as bass
from concourse import mybir

F32 = mybir.dt.float32
F32R = mybir.dt.float32r
ALU = mybir.AluOpType
ACT = mybir.ActivationFunctionType

P = 128
D = 2048
KT = D // P
SEQ, NB, NS = 256, 8, 4
SAMP = NB * NS
NT = SAMP + SEQ
NX = NB + NT
HEAD = 64
CHUNK = 64
NCH = SEQ // CHUNK
RW, RA, RGL = 96, 96, 256
DFF = 4 * D
DPLE = 256
OFF_R = 2 * D
OFF_K, OFF_V = OFF_R + D, OFF_R + 2 * D
OFF_LOW = OFF_R + 3 * D
OFF_GA = OFF_LOW + RW + RA + RGL
OFF_GB = OFF_GA + D
EPS = 1e-6
GN_EPS = 64e-5

CONV_STATE, H_STATE = 0, 24
(CW, CB, BA, BX, LAM, W0, A0, KK, KA, RK, GNW, GNB, MUR, MUK, MUV, GMIX, GFFN, GPLE, GFIN) = (
    32, 36, 37, 38, 39, 40, 41, 42, 43, 44, 45, 46, 47, 48, 49, 50, 51, 52, 53)
MULOW = 54
NPAR = 58
SP8, NSP8 = 0, 1
NDER = 2

O_SHIFT, O_H, O_CONV = 0, 9, 18
NOUTF = 45

(C_ID, C_BD, C_ONE, C_AM, C_LM, C_SAM, C_SLM, C_SEQ, C_SQT, C_ID2, C_END) = np.cumsum(
    [0, 128, 128, 128, 512, 6 * 128, 128, 64, 256, 8, 64]).tolist()


def constants():
    c = np.zeros((P, C_END), np.float32)
    i, j = np.arange(P)[:, None], np.arange(P)[None, :]
    c[:, C_ID:C_ID + P] = i == j
    c[:, C_BD:C_BD + P] = i // HEAD == j // HEAD
    c[:, C_ONE:C_ONE + P] = 1 / D

    def half(t, s, m):
        return (t // (2 * m) == s // (2 * m)) & (t % (2 * m) >= m) & (s % (2 * m) < m)

    same = i // CHUNK == j // CHUNK
    c[:, C_AM:C_AM + 512] = np.concatenate([half(j, i, 1), same & (i <= j), same & (i < j), same & (i <= j)], 1)
    for l in range(6):
        c[:, C_LM + l * P:C_LM + (l + 1) * P] = half(i, j, 2 ** l)
    s, t = np.arange(SAMP)[:, None], np.arange(SAMP)[None, :]
    own = s % NB == t % NB
    c[:SAMP, C_SAM:C_SAM + 128] = np.concatenate(
        [own & half(t // NB, s // NB, 1), own & (s <= t), own & (s < t), own & (s <= t)], 1)
    c[:SAMP, C_SLM:C_SLM + 64] = np.concatenate([own & half(s // NB, t // NB, 1), own & half(s // NB, t // NB, 2)], 1)
    c[:, C_SEQ:C_SEQ + 256] = (np.arange(256)[None, :] // SAMP) == (np.arange(256)[None, :] % NB)
    c[:64, C_SQT:C_SQT + NB] = (np.arange(64)[:, None] % NB) == np.arange(NB)[None, :]
    c[:, C_ID2:C_ID2 + HEAD] = (i % HEAD) == np.arange(HEAD)[None, :]
    return c


PARTS = 8
LOOP_UNITS = 6
SLOTS = PARTS * LOOP_UNITS
U_LOW = 0
U_LOOP = 4
U_GB = U_LOOP + LOOP_UNITS * KT
U_RGO = U_GB + KT
U_RWO = U_RGO + KT
U_WO = U_RWO + KT
U_FFN = U_WO + KT
U_PLE = U_FFN + 8 * KT
U_END = U_PLE + KT

STEPS = {"dve_rg": 41, "dve_ch": 72}
ROW_LOADS = 27
N_INIT = 4
FFN_PLAN = (("up", 0), ("up", 1), ("down", 0), ("up", 2), ("down", 1), ("up", 3), ("down", 2), ("down", 3))


HI_AT, LO_AT = (0, 2), (3, 5)
EARLY = {9: ["wd"], 12: ["ad"], 14: ["kk_sum"], 16: ["decay"], 20: ["kk"], 24: ["cum"], 28: ["tilde"], 29: ["early_done"]}
LATE = {
    0: ["turn", "ar", "rg_gates"],
    2: ["gate_bonus"],
    4: ["rg_decay"],
    5: ["pairwise"],
    7: ["rg_root"],
    9: ["rg_scan"],
    10: ["invert1a"],
    12: ["invert1b", "state_in"],
    14: ["invert2a"],
    16: ["invert2b"],
    17: ["samp_pair", "samp_prep"],
    18: ["invert3a"],
    20: ["invert3b", "samp_inv_a"],
    22: ["invert4a", "samp_inv_b"],
    24: ["invert4b", "samp_r"],
    26: ["invert5a", "samp_u"],
    28: ["invert5b"],
    30: ["r0"],
    31: ["samp_out"],
    32: ["u0"],
    34: ["my0", "r1"],
    36: ["u1"],
    38: ["my1", "r2"],
    40: ["u2"],
    42: ["my2", "r3"],
    43: ["u3"],
    44: ["my3"],
    45: ["mean"],
    47: ["var"],
}


def program(nc, a):
    ctx = ExitStack()
    with ctx:
        def sb(name, shape, dt=F32, stack=ctx):
            return stack.enter_context(nc.sbuf_tensor(name, shape, dt))

        def sem(name):
            return ctx.enter_context(nc.semaphore(name))

        bank = [ctx.enter_context(nc.psum_tensor(f"bank{k}", [P, 512], F32)) for k in range(8)]

        xh = sb("xh", [P, KT, NX], F32R)
        xl = sb("xl", [P, KT, NX], F32R)
        rga = sb("rga", [P, KT, NX])
        rwo = sb("rwo", [P, KT, NT])
        raw = [sb(f"raw{s}", [P, KT, P]) for s in range(2)]
        wh = [sb(f"wh{s}", [P, KT, P], F32R) for s in range(2)]
        wl = [sb(f"wl{s}", [P, KT, P], F32R) for s in range(2)]
        cst = sb("cst", [P, C_END])
        par = sb("par", [P, KT, NPAR])
        der = sb("der", [P, KT, NDER])
        der_work = sb("der_work", [P, KT, 4])
        outf = sb("outf", [P, KT, NOUTF])
        sums = sb("sums", [P, NX])

        ident, bd, ones = (cst[:, o:o + P] for o in (C_ID, C_BD, C_ONE))
        samp_all, prompt_all = slice(0, SAMP), slice(SAMP, NT)

        mix = ExitStack()
        with mix:
            def mb(name, shape, dt=F32):
                return sb(name, shape, dt, mix)

            ptu, ptc = mb("ptu", [P, NPAR]), mb("ptc", [P, NPAR])
            dtc, dl = mb("dtc", [P, NDER]), mb("dl", [P, NCH])
            ex = mb("ex", [P, NX])
            zr, zk, zv = mb("zr", [P, NT]), mb("zk", [P, NT]), mb("zv", [P, NT])
            low = mb("low", [P, 4, NT])
            w2s, a2s, g2s = mb("w2s", [P, P]), mb("a2s", [P, P]), mb("g2s", [P, 2, P])
            was, wxs = mb("was", [P, P]), mb("wxs", [P, P])
            ue, xc, gg, gat = mb("ue", [P, 315]), mb("xc", [P, NT]), mb("gg", [P, NT]), mb("gat", [P, NT])
            rgi, th = mb("rgi", [P, NT]), mb("th", [P, NT])
            siga, sigw, gout, kp = (mb(n, [P, NT]) for n in ("siga", "sigw", "gout", "kp"))
            rn, ksq, kkn, bv = (mb(n, [P, NT]) for n in ("rn", "ksq", "kkn", "bv"))
            cum = mb("cum", [P, 5 * NB + NCH * (CHUNK + 1)])
            zeros = mb("zeros", [P, CHUNK])
            ar, btl, ktl = mb("ar", [P, 2, NT]), mb("btl", [P, NT]), mb("ktl", [P, NT])
            bkh, vv = mb("bkh", [P, 2 * SAMP]), mb("vv", [P, 2 * SAMP])
            tmb, tmv = mb("tmb", [P, 4, P]), mb("tmv", [P, 2, P])
            sbk, svv, suv = mb("sbk", [2 * SAMP, P]), mb("svv", [2 * SAMP, P]), mb("suv", [2 * SAMP, P])
            ams, ab = mb("ams", [P, 4, 512]), mb("ab", [P, 4, P])
            am = [mb(f"am{k}", [P, 4, P]) for k in range(2)]
            tt, tn, yy = mb("tt", [P, 4, P]), mb("tn", [P, 4, P]), mb("yy", [P, 4, P])
            sam, sab = mb("sam", [SAMP, 2, 128]), mb("sab", [SAMP, 2, SAMP])
            sa2, stn, stt_s, syy = (mb(n, [SAMP, 2, SAMP]) for n in ("sa2", "stn", "stt_s", "syy"))
            s0, ms = mb("s0", [P, NB, P]), mb("ms", [P, NB, P])
            aex, bke = mb("aex", [P, NB, SAMP]), mb("bke", [2 * SAMP, 2, 512])
            dg = mb("dg", [P, NB, HEAD])
            so = dg
            rs, us, sr = mb("rs", [P, P]), mb("us", [P, P]), mb("sr", [SAMP, P])
            mp, mtmp = [mb(f"mp{k}", [P, P]) for k in range(2)], mb("mtmp", [P, P])
            sfin = mtmp
            yf, yc, ysq, sd = (mb(n, [P, NT]) for n in ("yf", "yc", "ysq", "sd"))
            dif, rgr, m2 = sd, yf, ysq
            rows = ams[:, :, :].rearrange("p a b -> p (a b)")

        ffn = ExitStack()
        with ffn:
            sbh = [sb(f"sbh{k}", [P, KT, NT], F32R, ffn) for k in range(2)]
            sbl = [sb(f"sbl{k}", [P, KT, NT], F32R, ffn) for k in range(2)]
            tmp = [sb(f"tmp{k}", [P, NT], F32, ffn) for k in range(2)]
            nsq = [sb(f"nsq{k}", [P, 2, NX], F32, ffn) for k in range(2)]
            nrm = [sb(f"nrm{k}", [P, 2, NX], F32, ffn) for k in range(2)]
            acc, mean_sq = nsq[0][:, 1, 0:NT], nsq[1][:, 1, :]
            gt = [t[:, 0, 0:NT] for t in nsq]
        fin = ExitStack()
        with fin:
            wcol = [sb(f"wcol{k}", [P, 2, P], F32, fin) for k in range(2)]
            ptok, pt = sb("ptok", [P, 3, DPLE], F32, fin), sb("pt", [P, 2, NT], F32, fin)
            small_out = sb("small_out", [NOUTF, D], F32, fin)
            ytok = sb("ytok", [P, 3, D], F32, fin)
        xtok = rwo[:, :, :].rearrange("p k t -> p (k t)")[:, 0:2 * D].rearrange("p (u d) -> p u d", u=2)

        xt_dram = nc.dram_tensor("xt_scratch", [P, KT, NX], F32).ap()
        ga_dram = nc.dram_tensor("ga_scratch", [KT, P, NT], F32).ap()
        gb_dram = nc.dram_tensor("gb_scratch", [KT, P, NT], F32).ap()

        hi_done, lo_done, unit_done = (
            sem(n) for n in ("hi_done", "lo_done", "unit_done"))
        cst_in, rows_zero, rows_in, xs_in, xp_in, xp2_in, xt_mm = (
            sem(n) for n in ("cst_in", "rows_zero", "rows_in", "xs_in", "xp_in", "xp2_in", "xt_mm"))
        par_mm, par_ready, xt_act, xt_dve, xt_saved = (
            sem(n) for n in ("par_mm", "par_ready", "xt_act", "xt_dve", "xt_saved"))
        der_step, init_done, sq_ready, sum_mm, rms_var, rms_std, rms_inv = (
            sem(n) for n in ("der_step", "init_done", "sq_ready", "sum_mm", "rms_var", "rms_std", "rms_inv"))
        lam_abs, lam_exp, gated, nrm_ready, nrm_hi, nrm_lo = (
            sem(n) for n in ("lam_abs", "lam_exp", "gated", "nrm_ready", "nrm_hi", "nrm_lo"))
        nrm_copy = sem("nrm_copy")
        low_ex, low_mix, low_ready, small_in, s0_in, ga_ready, ga_saved = (
            sem(n) for n in ("low_ex", "low_mix", "low_ready", "small_in", "s0_in", "ga_ready", "ga_saved"))
        gb_ready = sem("gb_ready")
        ptc_ready, ex_ready, mixed, ue_ready, conv_ready, gelu_ready = (
            sem(n) for n in ("ptc_ready", "ex_ready", "mixed", "ue_ready", "conv_ready", "gelu_ready"))
        low_mm, low_read, ksq_ready, kk_mm, ss_ready, kk_root, rgr_mm = (
            sem(n) for n in ("low_mm", "low_read", "ksq_ready", "kk_mm", "ss_ready", "kk_root", "rgr_mm"))
        rgr_sig, rgi_mm, rgi_sig, decay_ready, rg_exp, th_ready = (
            sem(n) for n in ("rgr_sig", "rgi_mm", "rgi_sig", "decay_ready", "rg_exp", "th_ready"))
        m2_ready, m_root, bt_ready, bonus_mm, prep_done, turn_mm, turn_read = (
            sem(n) for n in ("m2_ready", "m_root", "bt_ready", "bonus_mm", "prep_done", "turn_mm", "turn_read"))
        pair_mm, ab_read, pair_read, t_start, am_ready = (
            sem(n) for n in ("pair_mm", "ab_read", "pair_read", "t_start", "am_ready"))
        state_mm, state_read, spair_mm, sinv_ready, syy_mm, syy_read, stt_mm = (
            sem(n) for n in ("state_mm", "state_read", "spair_mm", "sinv_ready", "syy_mm", "syy_read", "stt_mm"))
        stt_ready, sr_mm, sr_read, su_mm, su_read = (
            sem(n) for n in ("stt_ready", "sr_mm", "sr_read", "su_mm", "su_read"))
        so_mm, so_ready, so_saved = (
            sem(n) for n in ("so_mm", "so_ready", "so_saved"))
        yy_mm, yy_read, tn_mm, tn_ready, r_mm, u_mm, u_read = (
            sem(n) for n in ("yy_mm", "yy_read", "tn_mm", "tn_ready", "r_mm", "u_mm", "u_read"))
        m_mm, y_mm, m_ready = (
            sem(n) for n in ("m_mm", "y_mm", "m_ready"))
        yf_ready, mean_mm, yc_ready, ysq_ready, var_mm, var_ready, y_root = (
            sem(n) for n in ("yf_ready", "mean_mm", "yc_ready", "ysq_ready", "var_mm", "var_ready", "y_root"))
        rga_ready, rwo_ready = (
            sem(n) for n in ("rga_ready", "rwo_ready"))
        fin_mm, fin_read, fin_saved = (
            sem(n) for n in ("fin_mm", "fin_read", "fin_saved"))
        dve_rg, dve_ch, split_hi, split_lo, x_back = (
            sem(n) for n in ("dve_rg", "dve_ch", "split_hi", "split_lo", "x_back"))
        merged, merged_hi, merged_lo = (
            sem(n) for n in ("merged", "merged_hi", "merged_lo"))
        x_done, h_relu, h_sq, h_hi, h_lo, tmp_ready, ple_in = (
            sem(n) for n in ("x_done", "h_relu", "h_sq", "h_hi", "h_lo", "tmp_ready", "ple_in"))
        pt_mm, pt_ready, sg_ready, embed_mm, sexp_ready, sig_ready, small_mm = (
            sem(n) for n in ("pt_mm", "pt_ready", "sg_ready", "embed_mm", "sexp_ready", "sig_ready", "small_mm"))
        small_read = sem("small_read")
        y_turn, y_read, stored = (
            sem(n) for n in ("y_turn", "y_read", "stored"))
        r_read = [sem(f"r_read{k}") for k in range(4)]
        wcol_in = [sem(f"wcol_in{k}") for k in range(2)]
        gb_saved = [sem(f"gb_saved{k}") for k in range(2)]
        g_in = [sem(f"g_in{k}") for k in range(2)]
        raw_in = [sem(f"raw_in{k}") for k in range(2)]

        acc_ready, acc_clear, sq_done = sem("acc_ready"), sem("acc_clear"), sem("sq_done")
        early_in, gout_mm, gout_read, ar_ready, early_end, bonus_read, half_done = (
            sem(n) for n in ("early_in", "gout_mm", "gout_read", "ar_ready", "early_end", "bonus_read", "half_done"))

        block = ctx.enter_context(nc.Block())

        class Count:

            def __init__(self, sem, step, per_step):
                self.sem, self.n = sem, 0
                self.base, self.per_step = step * per_step if per_step else 0, per_step

            def one(self):
                self.n += 1
                return 1

            def so_far(self):
                return self.base + self.n

            def end(self):
                assert self.n == self.per_step, self.n

        def cum_of(which):
            o = 0 if which == "before" else 1
            samples = cum[:, o * NB:o * NB + SAMP]
            prompt = cum[:, 5 * NB:].rearrange("p (c t) -> p c t", c=NCH)[:, :, o:o + CHUNK]
            return samples, prompt

        def last_decay(c):
            col = 5 * NB + c * (CHUNK + 1) + CHUNK
            return cum[:, col:col + 1]

        def chunks(ap):
            return ap[:, SAMP:NT].rearrange("p (c t) -> p c t", c=NCH)

        def blocks(ap, l, odd):
            return ap.rearrange("p (n o m) -> p n o m", o=2, m=2 ** l)[:, :, odd, :]

        def unit_columns(u, it):
            return [OFF_K, OFF_R, OFF_V, 0, D, OFF_GA][u] + it * P

        @block.sync
        def _(sp):
            def load_unit(src, slot, n=None):
                if n is not None:
                    sp.wait_ge(cst_in, 16)
                    sp.wait_ge(lo_done, n - 1)
                sp.dma_start(raw[slot][:], src.rearrange("(k p) c -> p k c", p=P)).then_inc(raw_in[slot], 16)

            def in_columns(start):
                return a["w_in"][0, :, bass.ds(start, P)]

            sp.dma_start(cst[:], a["const"]).then_inc(cst_in, 16)
            sp.dma_start(xtok[0:NB, 0, :], a["state_shift"][0]).then_inc(xs_in, 16)
            for t in range(NS):
                sp.dma_start(xtok[NB + t * NB:2 * NB + t * NB, 0, :], a["x_sample"][:, t, :]).then_inc(xs_in, 16)
            sp.dma_start(xtok[:, 1, :], a["x_prompt"][0, 0:P, :]).then_inc(xp_in, 16)
            sp.wait_ge(rows_zero, 1)
            n_rows = 0
            for j in range(3):
                sp.dma_start(rows[j * NB:j * NB + NB, :], a["state_rg_conv"][0, :, j, :]).then_inc(rows_in, 16)
            sp.dma_start(rows[H_STATE:H_STATE + NB, :], a["state_rg_h"][0]).then_inc(rows_in, 16)
            sp.dma_start(rows[CW:CW + 4, :], a["conv_w"][0]).then_inc(rows_in, 16)
            n_rows = 5
            mu = a["mu_shift"][0]
            for row, src in ((CB, a["conv_b"][0]), (BA, a["rg_ba"][0]), (BX, a["rg_bx"][0]), (LAM, a["rg_lam"][0]),
                             (W0, a["rw_w0"][0]), (A0, a["rw_a0"][0]), (KK, a["rw_kk"][0]), (KA, a["rw_ka"][0]),
                             (RK, a["rw_rk"][0]), (GNW, a["rw_gn_w"][0]), (GNB, a["rw_gn_b"][0]),
                             (MUR, mu[0:D]), (MUK, mu[D:2 * D]), (MUV, mu[2 * D:3 * D]),
                             (GMIX, a["norm_mix"][0]), (GFFN, a["norm_ffn"][0]), (GPLE, a["norm_ple"][0]),
                             (GFIN, a["norm_f"])):
                width = src.shape[-1]
                src = src.rearrange("a b -> (a b)") if len(src.shape) == 2 else src
                sp.dma_start(rows[row:row + 1, :], src.rearrange("(o d) -> o d", o=1)).then_inc(rows_in, 16)
                n_rows += 1
            o = 3 * D
            for k, (o, w) in enumerate(((3 * D, RW), (3 * D + RW, RA), (3 * D + RW + RA, P), (3 * D + RW + RA + P, P))):
                sp.dma_start(rows[MULOW + k:MULOW + k + 1, 0:w],
                             mu[o:o + w].rearrange("(o d) -> o d", o=1)).then_inc(rows_in, 16)
                n_rows += 1
            assert n_rows == ROW_LOADS
            low_start = (OFF_LOW, OFF_LOW + RW, OFF_LOW + RW + RA, OFF_LOW + RW + RA + P)
            for u in range(2):
                load_unit(in_columns(low_start[u]), u)
            sp.wait_ge(xt_mm, 2)
            sp.dma_start(xtok[:, 0, :], a["x_prompt"][0, P:SEQ, :]).then_inc(xp2_in, 16)
            sp.wait_ge(xt_dve, 6)
            sp.wait_ge(xt_act, 4)
            sp.dma_start(xt_dram, rga[:]).then_inc(xt_saved, 16)

            def small_early(it):
                cols = bass.ds(it * P, P)
                sp.dma_start(w2s[0:RW, :], a["rw_w2"][0, :, cols]).then_inc(early_in, 16)
                sp.dma_start(a2s[0:RA, :], a["rw_a2"][0, :, cols]).then_inc(early_in, 16)

            def small(it, again):
                if again:
                    sp.wait_ge(cst_in, 16)
                    sp.wait_ge(bonus_mm, it)
                cols = bass.ds(it * P, P)
                sp.dma_start(g2s[:], a["rw_g2"][0, :, cols].rearrange("(k p) c -> p k c", p=P)).then_inc(small_in, 16)
                sp.dma_start(was[:], a["rg_wa"][0, bass.ds(it, 1)].rearrange("o c d -> (o c) d")).then_inc(small_in, 16)
                sp.dma_start(wxs[:], a["rg_wx"][0, bass.ds(it, 1)].rearrange("o c d -> (o c) d")).then_inc(small_in, 16)
                if again:
                    sp.wait_ge(cst_in, 16)
                    sp.wait_ge(state_mm, it)
                else:
                    sp.wait_ge(init_done, N_INIT)
                for h in range(2):
                    sp.dma_start(s0[h * HEAD:(h + 1) * HEAD, :, h * HEAD:(h + 1) * HEAD],
                                 a["state_rwkv"][0, :, bass.ds(2 * it + h, 1)].rearrange("b o i j -> (o i) b j")
                                 ).then_inc(s0_in, 16)

            def states_out(p):
                sp.wait_ge(cst_in, 16)
                sp.wait_ge(so_ready, p + 1)
                sp.dma_start(a["o_rwkv_s"][0, :, bass.ds(2 * p, 2)].rearrange("b h i j -> (h i) b j"), so[:]
                             ).then_inc(so_saved, 16)
                sp.wait_ge(cst_in, 16)
                sp.wait_ge(fin_read, p + 1)
                for h in range(2):
                    sp.dma_start(a["o_rwkv_p"][0, 0, bass.ds(2 * p + h, 1)].rearrange("o i j -> (o i) j"),
                                 sfin[h * HEAD:(h + 1) * HEAD, h * HEAD:(h + 1) * HEAD]).then_inc(fin_saved, 16)

            def step(it, last, chain):
                for u in range(LOOP_UNITS):
                    n = U_LOOP + it * LOOP_UNITS + u + 3
                    if u < 3:
                        load_unit(in_columns(unit_columns(u + 3, it)), (u + 3) % 2, n)
                    elif not last:
                        load_unit(in_columns(unit_columns(u - 3, it + 1)), (u + 3) % 2, n)
                    else:
                        load_unit(in_columns(OFF_GB + (u - 3) * P), (u + 3) % 2, n)
                    if chain and u == 1:
                        sp.wait_ge(cst_in, 16)
                        sp.wait_ge(ga_ready, it)
                        sp.dma_start(ga_dram[bass.ds(it - 1, 1)].rearrange("o p t -> (o p) t"), gat[:]).then_inc(ga_saved, 16)
                    if u == 3 and not last:
                        sp.wait_ge(cst_in, 16)
                        sp.wait_ge(kk_mm, it + 1)
                        small_early(it + 1)
                    if u == 4:
                        small(it, chain)
                if chain:
                    states_out(it - 1)

            for u in (2, 3):
                load_unit(in_columns(low_start[u]), u % 2, u)
            small_early(0)
            for u in range(3):
                load_unit(in_columns(unit_columns(u, 0)), u % 2, U_LOOP + u)
            step(0, False, False)
            with sp.Fori(1, KT - 1) as it:
                step(it, False, True)
            step(KT - 1, True, True)
            for u in range(LOOP_UNITS):
                load_unit(in_columns(OFF_GB + (u + 3) * P), (u + 3) % 2, U_GB + u + 3)
                if u == 0:
                    sp.wait_ge(ga_ready, KT)
                    sp.dma_start(ga_dram[KT - 1], gat[:]).then_inc(ga_saved, 16)
                else:
                    sp.wait_ge(gb_ready, u)
                    sp.dma_start(gb_dram[u - 1], gat[:]).then_inc(gb_saved[(u - 1) % 2], 16)
            states_out(KT - 1)

            def phase(base, src, following, extra=None, start=0, end=None):
                with sp.Fori(start // 2, (KT - 4) // 2) as i:
                    for u in range(2):
                        k = 2 * i + u
                        load_unit(src(k + 3), (u + 1) % 2, base + k + 3)
                        if extra:
                            extra(k, u, i)
                for k in range(KT - 4, KT):
                    if k + 3 < KT:
                        load_unit(src(k + 3), (k + 1) % 2, base + k + 3)
                    elif following:
                        load_unit(following(k + 3 - KT), (k + 1) % 2, base + k + 3)
                    if extra:
                        extra(k, k % 2, k // 2)
                    if end and k == KT - 3:
                        end()

            def columns(name, k0=None):
                w = a[name][0] if k0 is None else a[name][0, k0:k0 + D, :]
                return lambda k: w[:, bass.ds(k * P, P)]

            def up(g):
                return lambda k: a["w_up"][0, :, bass.ds(g * D + k * P, P)]

            sp.wait_ge(gb_ready, 6)
            sp.dma_start(gb_dram[5], gat[:]).then_inc(gb_saved[1], 16)

            def gb_store(k, u, i):
                sp.wait_ge(cst_in, 16)
                sp.wait_ge(gb_ready, k + 1)
                sp.dma_start(gb_dram[bass.ds(k, 1)].rearrange("o p t -> (o p) t"), tmp[u][:]).then_inc(gb_saved[u], 16)

            phase(U_GB, lambda k: in_columns(OFF_GB + k * P), columns("w_rg_o"), gb_store, start=6)

            def gate_load(dram, first, k, u, free=True):
                if free:
                    sp.wait_ge(cst_in, 16)
                    sp.wait_ge(merged, first + k - 1)
                sp.dma_start(gt[u][:], dram[bass.ds(k, 1)].rearrange("o p t -> (o p) t")).then_inc(g_in[u], 16)

            sp.wait_ge(ga_saved, 16 * KT)
            sp.wait_ge(gb_saved[0], 8 * KT)
            sp.wait_ge(gb_saved[1], 8 * KT)

            def x_again():
                sp.wait_ge(split_lo, 8)
                sp.dma_start(rga[:], xt_dram).then_inc(x_back, 16)

            def ga_next(k, u, i):
                if isinstance(k, int) and k == KT - 1:
                    gate_load(gb_dram, KT, 0, 0)
                else:
                    gate_load(ga_dram, 0, k + 1, 1 - u)

            def gb_next(k, u, i):
                if not (isinstance(k, int) and k == KT - 1):
                    gate_load(gb_dram, KT, k + 1, 1 - u)

            for u in range(2):
                load_unit(a["w_rg_o"][0, :, (u + 3) * P:(u + 4) * P], (u + 1) % 2, U_RGO + u + 3)
                if u == 0:
                    gate_load(ga_dram, 0, 0, 0, False)
                    gate_load(ga_dram, 0, 1, 1, False)
                else:
                    ga_next(1, 1, 0)
            phase(U_RGO, columns("w_rg_o"), columns("w_rw_o"), ga_next, start=2, end=x_again)
            phase(U_RWO, columns("w_rw_o"), columns("w_o"), gb_next)
            phase(U_WO, columns("w_o"), up(0))
            plan = [("up", 0), ("up", 1), ("down", 0), ("up", 2), ("down", 1), ("up", 3), ("down", 2), ("down", 3)]
            srcs = [up(g) if kind == "up" else columns("w_down", g * D) for kind, g in plan] + [columns("w_ple_gate")]

            def ple_loads():
                sp.wait_ge(cst_in, 16)
                sp.wait_ge(unit_done, U_FFN + 7 * KT)
                for t in range(NS):
                    sp.dma_start(ptok[t * NB:t * NB + NB, 0, :], a["p_sample"][0, :, t, :]).then_inc(ple_in, 16)
                sp.dma_start(ptok[:, 1:3, :], a["p_prompt"][0, 0].rearrange("(u p) c -> p u c", p=P)).then_inc(ple_in, 16)

            for f in range(8):
                phase(U_FFN + f * KT, srcs[f], srcs[f + 1], end=ple_loads if f == 7 else None)

            def col_load(k, u, free=True):
                if free:
                    sp.wait_ge(cst_in, 16)
                    sp.wait_ge(embed_mm, k - 1)
                sp.dma_start(wcol[u][:], a["w_ple"][0, :, bass.ds(k * P, P)].rearrange("(k p) c -> p k c", p=P)
                             ).then_inc(wcol_in[u], 16)

            def col_next(k, u, i):
                if not (isinstance(k, int) and k == KT - 1):
                    col_load(k + 1, 1 - u)

            for u in range(2):
                load_unit(srcs[8](u + 3), (u + 1) % 2, U_PLE + u + 3)
                if u == 0:
                    col_load(0, 0, False)
                    col_load(1, 1, False)
                else:
                    col_next(1, 1, 0)
            phase(U_PLE, srcs[8], None, col_next, start=2)

            sp.wait_ge(small_read, 4)
            for dst, row, n in ((a["o_shift_p"][0], O_SHIFT, 1), (a["o_shift_s"][0], O_SHIFT + 1, NB),
                                (a["o_h_p"][0], O_H, 1), (a["o_h_s"][0], O_H + 1, NB),
                                (a["o_conv_p"][0, 0], O_CONV, 3),
                                (a["o_conv_s"][0, :, 0, :], O_CONV + 3, NB), (a["o_conv_s"][0, :, 1, :], O_CONV + 3 + NB, NB),
                                (a["o_conv_s"][0, :, 2, :], O_CONV + 3 + 2 * NB, NB)):
                sp.dma_start(dst, small_out[row:row + n, :]).then_inc(stored, 16)
            sp.wait_ge(y_read, 3 * 8)
            for t in range(NS):
                sp.dma_start(a["o_y_s"][:, t, :], ytok[t * NB:t * NB + NB, 0, :]).then_inc(stored, 16)
            sp.dma_start(a["o_y_p"][0].rearrange("(u p) d -> p u d", p=P), ytok[:, 1:3, :]).then_inc(stored, 16)
            sp.wait_ge(stored, 16 * 13)
            sp.wait_ge(so_saved, 16 * KT)
            sp.wait_ge(fin_saved, 32 * KT)
            sp.wait_ge(xt_saved, 16)

        @block.tensor
        def _(pe):
            def mm(out, lhsT, rhs, start, stop):
                return pe.matmul(out, lhsT, rhs, start=start, stop=stop, skip_group_check=True)

            def apart(value):
                if not isinstance(value, int):
                    value = pe.snap(value)
                    pe.wait_ge(cst_in, 16)
                return value

            def unit_part(slot, hi, lo, first, last, q, parts=PARTS):
                out = bank[slot][:, 0:last - first]
                for kt in range(KT // parts * q, KT // parts * (q + 1)):
                    x1, x2 = hi[:, kt, first:last], lo[:, kt, first:last]
                    mm(out, wh[slot][:, kt, :], x1, kt == 0, False)
                    mm(out, wh[slot][:, kt, :], x2, False, False)
                    done = mm(out, wl[slot][:, kt, :], x1, False, kt == KT - 1)
                if q == parts - 1:
                    done.then_inc(unit_done, 1)

            def unit_ready(n, read, count):
                pe.wait_ge(lo_done, n + 1)
                if read:
                    pe.wait_ge(read, count)

            def turn(out, in_):
                return pe.transpose(out, in_, ident)

            pe.wait_ge(cst_in, 16)
            pe.wait_ge(xs_in, 16 * 5)
            for b in range(2):
                for k in range(8):
                    done = pe.transpose(bank[b][:, k * 40:(k + 1) * 40], xtok[0:40, 0, (b * 8 + k) * P:(b * 8 + k + 1) * P], cst[0:40, C_ID:C_ID + 40])
                done.then_inc(xt_mm, 1)
            pe.wait_ge(xp_in, 16)
            for b in range(4):
                for k in range(4):
                    done = turn(bank[2 + b][:, k * P:(k + 1) * P], xtok[:, 1, (b * 4 + k) * P:(b * 4 + k + 1) * P])
                done.then_inc(xt_mm, 1)
            pe.wait_ge(rows_in, 16 * ROW_LOADS)
            for b in range(2):
                for k in range(8):
                    done = pe.transpose(bank[6 + b][:, k * NPAR:(k + 1) * NPAR], rows[0:NPAR, (b * 8 + k) * P:(b * 8 + k + 1) * P], cst[0:NPAR, C_ID:C_ID + NPAR])
                done.then_inc(par_mm, 1)
            pe.wait_ge(xp2_in, 16)
            for b in range(4):
                if b < 2:
                    pe.wait_ge(xt_dve, b + 1)
                else:
                    pe.wait_ge(xt_act, b - 1)
                for k in range(4):
                    done = turn(bank[b][:, k * P:(k + 1) * P], xtok[:, 0, (b * 4 + k) * P:(b * 4 + k + 1) * P])
                done.then_inc(xt_mm, 1)

            pe.wait_ge(par_ready, 2)
            for j in range(8):
                pe.wait_ge(sq_ready, j + 1)
                for h in range(2):
                    done = mm(bank[7][:, 0:NX], ones, nsq[j % 2][:, h, 0:NX], j == 0 and h == 0, j == 7 and h == 1)
                done.then_inc(sum_mm, 1)

            def norm(k):
                pe.wait_ge(acc_ready, k * KT)
                mm(bank[7][:, 0:NT], ones, acc, True, True).then_inc(sum_mm, 1)

            for n in range(4):
                unit_ready(n, low_ex if n > 1 else None, n - 1)
                for q in range(PARTS if n == 0 else 1):
                    if n == 0:
                        pe.wait_ge(nrm_lo, q + 1)
                    unit_part(n % 2, xh, xl, 0, NX, q, PARTS if n == 0 else 1)

            def early(name, it):
                one = it + 1
                if name == "wd":
                    pe.wait_ge(early_in, 32 * one)
                    if isinstance(it, int) and it == 0:
                        pe.wait_ge(low_ready, 3)
                    else:
                        pe.wait_ge(pair_read, 4 * it)
                    mm(bank[7][:, 0:NT], w2s[0:RW, :], low[0:RW, 0, :], True, True).then_inc(low_mm, 1)
                elif name == "ad":
                    pe.wait_ge(sig_ready, 2 * it + 1)
                    mm(bank[7][:, 0:NT], a2s[0:RA, :], low[0:RA, 1, :], True, True).then_inc(low_mm, 1)
                elif name == "kk_sum":
                    pe.wait_ge(sig_ready, 2 * it + 2)
                    pe.wait_ge(ksq_ready, one)
                    mm(bank[7][:, 0:NT], bd, ksq[:], True, True).then_inc(kk_mm, 1)

            def stage(name, p, last):
                one = p + 1
                if name == "rg_gates":
                    pe.wait_ge(small_in, 48 * one)
                    pe.wait_ge(conv_ready, one)
                    if not (isinstance(p, int) and p == 0):
                        pe.wait_ge(yf_ready, p)
                    mm(bank[7][:, 0:NT], was[:], xc[:], True, True).then_inc(rgr_mm, 1)
                    mm(bank[6][:, 0:NT], wxs[:], xc[:], True, True).then_inc(rgi_mm, 1)
                elif name == "gate_bonus":
                    mm(bank[4][:, 0:NT], g2s[:, 0, :], low[:, 2, :], True, False)
                    mm(bank[4][:, 0:NT], g2s[:, 1, :], low[:, 3, :], False, True).then_inc(gout_mm, 1)
                    pe.wait_ge(bt_ready, one)
                    mm(bank[5][:, 0:NT], bd, bv[:], True, True).then_inc(bonus_mm, 1)
                elif name == "turn":
                    pe.wait_ge(early_end, one)
                    if not (isinstance(p, int) and p == 0):
                        pe.wait_ge(fin_read, p)
                    for k, src in enumerate((btl, ktl)):
                        for g in range(2):
                            turn(bank[2][:, (2 * k + g) * P:(2 * k + g + 1) * P], src[:, SAMP + g * P:SAMP + (g + 1) * P])
                    for g in range(2):
                        turn(bank[3][:, g * P:(g + 1) * P], zv[:, SAMP + g * P:SAMP + (g + 1) * P])
                    turn(bank[3][0:2 * SAMP, 256:384], bkh[:])
                    turn(bank[3][0:2 * SAMP, 384:512], vv[:]).then_inc(turn_mm, 1)
                elif name == "pairwise":
                    pe.wait_ge(ar_ready, one)
                    pe.wait_ge(bonus_read, one)
                    pe.wait_ge(gout_read, one)
                    pe.wait_ge(rgi_sig, one)
                    for g in range(2):
                        cols = slice(SAMP + g * P, SAMP + (g + 1) * P)
                        for part, src in enumerate((btl, ktl)):
                            for h in range(2):
                                rows_h = slice(h * HEAD, (h + 1) * HEAD)
                                done = mm(bank[4 + 2 * g + h][:, part * 256:(part + 1) * 256], src[rows_h, cols], ar[rows_h, :, cols], True, True)
                                if part:
                                    done.then_inc(pair_mm, 1)
                    pe.wait_ge(turn_read, 5 * one)
                    for g in range(2):
                        cols = slice(SAMP + g * P, SAMP + (g + 1) * P)
                        for h in range(2):
                            rows_h = slice(h * HEAD, (h + 1) * HEAD)
                            done = mm(bank[2 + h][:, g * P:(g + 1) * P], ar[rows_h, 0, cols], btl[rows_h, cols], True, True)
                    done.then_inc(pair_mm, 1)
                elif name[:6] == "invert":
                    l, part = int(name[6]), name[7]
                    if part == "a":
                        if l == 1:
                            pe.wait_ge(t_start, one)
                            pe.wait_ge(pair_read, 4 * one)
                        else:
                            pe.wait_ge(tn_ready, 5 * p + l - 1)
                        pe.wait_ge(am_ready, 5 * p + l)
                        for q in range(4):
                            done = mm(bank[4][:, q * P:(q + 1) * P], am[l % 2][:, q, :], tt[:, q, :], True, True)
                        done.then_inc(yy_mm, 1)
                    else:
                        pe.wait_ge(yy_read, 5 * p + l)
                        for q in range(4):
                            done = mm(bank[5][:, q * HEAD:(q + 1) * HEAD], tn[:, q, :], blocks(yy[:, q, :], l, 1), True, True)
                        if l < 5:
                            for q in range(4):
                                done = mm(bank[6][:, q * HEAD:(q + 1) * HEAD], yy[:, q, :], blocks(tn[:, q, :], l, 0), True, True)
                        done.then_inc(tn_mm, 1)
                elif name == "state_in":
                    pe.wait_ge(s0_in, 32 * one)
                    pe.wait_ge(ab_read, 2 * one)
                    for b in range(NB):
                        done = turn(bank[2 + b // 4][:, (b % 4) * P:(b % 4 + 1) * P], s0[:, b, :])
                    done.then_inc(state_mm, 1)
                elif name == "samp_pair":
                    count = apart(2 * one)
                    pe.wait_ge(state_read, count)
                    for h in range(2):
                        rows_h = slice(h * HEAD, (h + 1) * HEAD)
                        out = bank[2 + h]
                        mm(out[0:SAMP, 0:64], btl[rows_h, 0:SAMP], ar[rows_h, :, 0:SAMP], True, True)
                        mm(out[0:SAMP, 64:128], ktl[rows_h, 0:SAMP], ar[rows_h, :, 0:SAMP], True, True)
                        done = mm(out[0:SAMP, 128:160], ar[rows_h, 0, 0:SAMP], btl[rows_h, 0:SAMP], True, True)
                    done.then_inc(spair_mm, 1)
                elif name == "samp_inv_a":
                    count = apart(one)
                    pe.wait_ge(sinv_ready, count)
                    for h in range(2):
                        done = mm(bank[2][0:SAMP, h * SAMP:(h + 1) * SAMP], sa2[:, h, :], stt_s[:, h, :], True, True)
                    done.then_inc(syy_mm, 1)
                elif name == "samp_inv_b":
                    count = apart(one)
                    pe.wait_ge(syy_read, count)
                    for h in range(2):
                        done = mm(bank[3][0:SAMP, h * SAMP:(h + 1) * SAMP], stn[:, h, :], syy[:, h, :], True, True)
                    done.then_inc(stt_mm, 1)
                elif name == "samp_r":
                    pe.wait_ge(sexp_ready, one)
                    for b in range(NB):
                        mm(bank[2][0:SAMP, 0:P], aex[:, b, :], ms[:, b, :], b == 0, False)
                    for h in range(2):
                        done = mm(bank[2][0:SAMP, h * HEAD:(h + 1) * HEAD], sam[:, h, 64:96], svv[0:SAMP, h * HEAD:(h + 1) * HEAD], False, True)
                    done.then_inc(sr_mm, 1)
                elif name == "samp_u":
                    count = apart(one)
                    pe.wait_ge(sr_read, count)
                    pe.wait_ge(stt_ready, one)
                    for h in range(2):
                        done = mm(bank[3][0:SAMP, h * HEAD:(h + 1) * HEAD], stt_s[:, h, :], sr[:, h * HEAD:(h + 1) * HEAD], True, True)
                    done.then_inc(su_mm, 1)
                elif name == "samp_out":
                    if not last:
                        pe.wait_ge(ss_ready, p + 2)
                    count = apart(one)
                    pe.wait_ge(su_read, count)
                    for b in range(NB):
                        mm(bank[7][:, b:SAMP:NB], ms[:, b, :], ar[:, 1, b:SAMP:NB], b == 0, False)
                    for h in range(2):
                        hc = slice(h * HEAD, (h + 1) * HEAD)
                        mm(bank[7][hc, 0:SAMP], suv[0:SAMP, hc], sam[:, h, 32:64], False, False)
                        mm(bank[7][hc, 0:SAMP], svv[0:SAMP, hc], sam[:, h, 96:128], False, True)
                    for b in range(NB):
                        mm(bank[3][:, b * HEAD:(b + 1) * HEAD], ms[:, b, :], dg[:, b, :], b == 0, False)
                    for h in range(2):
                        hc = slice(h * HEAD, (h + 1) * HEAD)
                        done = mm(bank[3][hc, 0:512], suv[:, hc], bke[:, h, :], False, True)
                    done.then_inc(so_mm, 1)
                elif name[0] == "r" and name[1:].isdigit():
                    c = int(name[1:])
                    g, rc = c // 2, slice((c % 2) * CHUNK, (c % 2 + 1) * CHUNK)
                    cc = (c % 2) * CHUNK
                    if c == 0:
                        count = apart(5 * one)
                        pe.wait_ge(tn_ready, count)
                    else:
                        count = apart(NCH * p + c)
                        pe.wait_ge(m_ready, count)
                        mm(bank[4][rc, 0:P], ar[:, 0, SAMP + c * CHUNK:SAMP + (c + 1) * CHUNK], mp[c % 2][:], True, False)
                    for h in range(2):
                        hc = slice(h * HEAD, (h + 1) * HEAD)
                        done = mm(bank[4][rc, hc], ams[rc, 2 * h + g, 256 + cc:256 + cc + CHUNK], tmv[rc, g, hc], c == 0, True)
                    done.then_inc(r_mm, 1)
                elif name[0] == "u":
                    c = int(name[1:])
                    g, rc = c // 2, slice((c % 2) * CHUNK, (c % 2 + 1) * CHUNK)
                    cc = (c % 2) * CHUNK
                    count = apart(one)
                    pe.wait_ge(r_read[c], count)
                    for h in range(2):
                        hc = slice(h * HEAD, (h + 1) * HEAD)
                        done = mm(bank[5][rc, hc], tt[rc, 2 * h + g, cc:cc + CHUNK], rs[rc, hc], True, True)
                    done.then_inc(u_mm, 1)
                elif name[:2] == "my":
                    c = int(name[2:])
                    g, rc = c // 2, slice((c % 2) * CHUNK, (c % 2 + 1) * CHUNK)
                    cc = (c % 2) * CHUNK
                    ycols = slice(SAMP + c * CHUNK, SAMP + (c + 1) * CHUNK)
                    count = apart(NCH * p + c + 1)
                    pe.wait_ge(u_read, count)
                    mm(bank[6][:, 0:P], tmb[rc, g, :], us[rc, :], True, False)
                    mm(bank[6][:, 0:P], tmb[rc, 2 + g, :], tmv[rc, g, :], False, True).then_inc(m_mm, 1)
                    if c:
                        mm(bank[7][:, ycols], mp[c % 2][:], ar[:, 1, ycols], True, False)
                    for h in range(2):
                        hc = slice(h * HEAD, (h + 1) * HEAD)
                        mm(bank[7][hc, ycols], us[rc, hc], ams[rc, 2 * h + g, 128 + cc:128 + cc + CHUNK], c == 0, False)
                        done = mm(bank[7][hc, ycols], tmv[rc, g, hc], ams[rc, 2 * h + g, 384 + cc:384 + cc + CHUNK], False, True)
                    done.then_inc(y_mm, 1)
                elif name == "mean":
                    pe.wait_ge(m_ready, NCH * one)
                    turn(bank[2][:, 0:P], mp[NCH % 2][:]).then_inc(fin_mm, 1)
                    pe.wait_ge(yf_ready, one)
                    mm(bank[4][:, 0:NT], bd, yf[:], True, True).then_inc(mean_mm, 1)
                elif name == "var":
                    pe.wait_ge(ysq_ready, one)
                    mm(bank[5][:, 0:NT], bd, ysq[:], True, True).then_inc(var_mm, 1)

            def step(it, units, chain):
                for slot in range(SLOTS):
                    u, q = divmod(slot, PARTS)
                    if units == "loop":
                        first = 0 if u < 3 else NB
                        if q == 0:
                            read, count = [(gelu_ready, it), (ga_ready, it), (ex_ready, 3 * it + 1), (ex_ready, 3 * it + 2),
                                           (ex_ready, 3 * it + 3), (ue_ready, it + 1)][u]
                            if not chain and u < 2:
                                read, count = low_ex, 3 + u
                            unit_ready(U_LOOP + it * LOOP_UNITS + u, read, count)
                    else:
                        first = NB
                        if q == 0:
                            unit_ready(U_GB + u, *((gelu_ready, KT), (ga_ready, KT))[u] if u < 2 else (gb_ready, u - 1))
                    unit_part(u % 2, xh, xl, first, NX, q)
                    if chain:
                        for name in LATE.get(slot, []):
                            stage(name, it - 1, units != "loop")
                    if units == "loop":
                        for name in EARLY.get(slot, []):
                            early(name, it)

            step(0, "loop", False)
            step(1, "loop", True)
            with pe.Fori(2, KT) as it:
                step(it, "loop", True)
            step(KT, "gb", True)

            def phase(base, hi, lo, first, last, read, before=None, extra=None, start=2, ready=None):
                def one(k, u):
                    if ready and isinstance(k, int) and k == 0:
                        for q in range(PARTS):
                            pe.wait_ge(ready[0], ready[1] + (q + 1) * ready[2])
                            unit_part(u, hi, lo, first, last, q)
                    else:
                        unit_part(u, hi, lo, first, last, 0, 1)
                    if extra:
                        extra(k, u)

                if before:
                    for k in range(2):
                        unit_ready(base + k, before[0], before[1] - 1 + k)
                        one(k, k)
                with pe.Fori(start // 2, KT // 2) as i:
                    for u in range(2):
                        unit_ready(base + 2 * i + u, read[0], read[1] + 2 * i + u - 1)
                        one(2 * i + u, u)

            phase(U_GB, xh, xl, NB, NX, (gb_ready, 0), start=6)
            pe.wait_ge(split_lo, 8)
            phase(U_RGO, sbh[0], sbl[0], 0, NT, (merged, 0), (gb_ready, KT))
            pe.wait_ge(split_lo, 8 + KT)
            phase(U_RWO, sbh[1], sbl[1], 0, NT, (gated, 0), (merged, KT))
            phase(U_WO, sbh[0], sbl[0], 0, NT, (x_done, 0), (gated, KT), ready=(merged_lo, 0, 2))
            norm(1)
            f, before = 0, (x_done, KT)
            for kind, g in FFN_PLAN:
                base = U_FFN + f * KT
                if kind == "up":
                    phase(base, xh, xl, NB, NX, (h_relu, KT * g), before, ready=(nrm_lo, 8, 1) if g == 0 else None)
                    before = (h_relu, KT * (g + 1))
                else:
                    pe.wait_ge(h_lo, KT * (g + 1))
                    phase(base, sbh[g % 2], sbl[g % 2], 0, NT, (x_done, KT * (g + 1)), before)
                    before = (x_done, KT * (g + 2))
                f += 1
            pe.wait_ge(ple_in, 16 * 5)
            for k in range(2):
                pe.transpose(bank[4 + k][:, 0:SAMP], ptok[0:SAMP, 0, k * P:(k + 1) * P], cst[0:SAMP, C_ID:C_ID + SAMP])
                for u in range(2):
                    done = turn(bank[4 + k][:, SAMP + u * P:SAMP + (u + 1) * P], ptok[:, 1 + u, k * P:(k + 1) * P])
            done.then_inc(pt_mm, 1)
            norm(2)
            pe.wait_ge(pt_ready, 2)

            def embed(k, u):
                pe.wait_ge(wcol_in[u], 8 * (k - u) + 16)
                pe.wait_ge(x_done, 5 * KT + k - 1)
                mm(bank[2 + u][:, 0:NT], wcol[u][:, 0, :], pt[:, 0, :], True, False)
                mm(bank[2 + u][:, 0:NT], wcol[u][:, 1, :], pt[:, 1, :], False, True).then_inc(embed_mm, 1)

            phase(U_PLE, xh, xl, NB, NX, (sg_ready, 0), before, embed, ready=(nrm_lo, 16, 1))
            for b in range(4):
                for k in range(4):
                    done = turn(bank[4 + b % 2][0:NOUTF, k * P:(k + 1) * P], outf[:, b * 4 + k, :])
                done.then_inc(small_mm, 1)
                if b in (1, 2):
                    pe.wait_ge(small_read, b)
            pe.wait_ge(small_read, 4)
            norm(3)
            for j in range(8):
                pe.wait_ge(nrm_ready, 24 + j + 1)
                if j >= 2:
                    pe.wait_ge(y_read, 3 * (j - 1))
                b3 = (2, 3, 4) if j % 2 == 0 else (5, 6, 1)
                for k in range(2):
                    kc = slice(k * P, (k + 1) * P)
                    turn(bank[b3[0]][0:SAMP, kc], nrm[j % 2][:, k, NB:NB + SAMP])
                    for u in range(2):
                        o = NB + SAMP + u * P
                        done = turn(bank[b3[1 + u]][:, kc], nrm[j % 2][:, k, o:o + P])
                done.then_inc(y_turn, 1)

        @block.scalar
        def _(act):
            def hi(n, slot, half):
                act.wait_ge(raw_in[slot], 16 * half + 16)
                if not (isinstance(n, int) and n < 2):
                    act.wait_ge(unit_done, n - 1)
                act.activation(wh[slot][:], raw[slot][:], ACT.Copy).then_inc(hi_done, 1)

            hi(0, 0, 0)
            hi(1, 1, 0)
            for b in range(4):
                act.wait_ge(xt_mm, 3 + b)
                act.activation(rga[:, 4 * b:4 * b + 4, 40:40 + P], bank[2 + b][:].rearrange("p (k t) -> p k t", k=4), ACT.Copy).then_inc(xt_act, 1)

            def norm(k, width):
                if k == 0:
                    for j in range(8):
                        if j >= 2:
                            act.wait_ge(sum_mm, j - 1)
                        act.activation(nsq[j % 2][:, :, :], rga[:, 2 * j:2 * j + 2, :], ACT.Square).then_inc(sq_ready, 1)
                act.wait_ge(rms_var, k + 1)
                act.activation(sums[:, NX - width:], mean_sq[:, NX - width:], ACT.Sqrt).then_inc(rms_std, 1)

            def norm_split(k, width, out):
                for j in range(8):
                    act.wait_ge(nrm_ready, 8 * k + j + 1)
                    act.activation(out[:, 2 * j:2 * j + 2, NX - width:], nrm[j % 2][:, :, NX - width:], ACT.Copy).then_inc(nrm_hi, 1)

            act.wait_ge(xt_dve, 6)
            act.wait_ge(xt_act, 4)
            norm(0, NX)
            norm_split(0, NX, xh)

            act.wait_ge(lam_abs, 1)
            act.activation(der_work[:, :, 1], der_work[:, :, 1], ACT.Exp, scale=-1.0).then_inc(lam_exp, 1)

            for n in range(4):
                act.wait_ge(unit_done, n + 1)
                if n:
                    act.wait_ge(low_mix, n)
                act.activation(ex[:], bank[n % 2][:, 0:NX], ACT.Copy).then_inc(low_ex, 1)
                if n < 3:
                    hi(n + 2, n % 2, n // 2 + 1)
            act.wait_ge(low_mix, 4)
            act.activation(low[0:RW, 0, :], low[0:RW, 0, :], ACT.Tanh).then_inc(low_ready, 1)
            act.activation(low[:, 2, :], low[:, 2, :], ACT.Sigmoid).then_inc(low_ready, 1)
            act.activation(low[:, 3, :], low[:, 3, :], ACT.Sigmoid).then_inc(low_ready, 1)

            def scalar(col):
                return ptc[:, col:col + 1]

            def early(name, it):
                one = it + 1
                if name == "wd":
                    act.wait_ge(mixed, 3 * it + 1)
                    act.activation(ksq[:], zk[:], ACT.Square, scale=ptu[:, KK:KK + 1]).then_inc(ksq_ready, 1)
                    act.wait_ge(low_mm, 2 * it + 1)
                    act.activation(sigw[:], bank[7][:, 0:NT], ACT.Sigmoid, bias=ptu[:, W0:W0 + 1]).then_inc(sig_ready, 1)
                elif name == "ad":
                    act.wait_ge(low_mm, 2 * it + 2)
                    act.activation(siga[:], bank[7][:, 0:NT], ACT.Sigmoid, bias=ptu[:, A0:A0 + 1]).then_inc(sig_ready, 1)
                elif name == "decay":
                    act.wait_ge(sig_ready, 2 * it + 2)
                    act.activation(sigw[:], sigw[:], ACT.Exp, scale=-math.exp(-0.5)).then_inc(decay_ready, 1)
                    act.wait_ge(ss_ready, one)
                    act.activation(rn[:], rn[:], ACT.Sqrt).then_inc(kk_root, 1)

            def stage(name, p):
                one = p + 1
                if name == "rg_gates":
                    act.wait_ge(ptc_ready, one)
                    act.wait_ge(rgr_mm, one)
                    act.activation(rgr[:], bank[7][:, 0:NT], ACT.Sigmoid, bias=scalar(BA)).then_inc(rgr_sig, 1)
                    act.wait_ge(rgi_mm, one)
                    act.activation(rgi[:], bank[6][:, 0:NT], ACT.Sigmoid, bias=scalar(BX)).then_inc(rgi_sig, 1)
                    act.wait_ge(rgr_sig, one)
                    act.activation(th[:], rgr[:], ACT.Tanh, scale=dtc[:, SP8:SP8 + 1]).then_inc(th_ready, 1)
                elif name == "gate_bonus":
                    act.wait_ge(gout_mm, one)
                    act.activation(gout[:], bank[4][:, 0:NT], ACT.Copy).then_inc(gout_read, 1)
                elif name == "rg_decay":
                    act.wait_ge(th_ready, one)
                    act.activation(rgr[:], rgr[:], ACT.Exp, scale=dtc[:, NSP8:NSP8 + 1]).then_inc(rg_exp, 1)
                elif name == "rg_root":
                    act.wait_ge(m2_ready, one)
                    act.activation(m2[:], m2[:], ACT.Sqrt).then_inc(m_root, 1)
                elif name == "turn":
                    act.wait_ge(turn_mm, one)
                    act.activation(tmb[:].rearrange("p a b -> p (a b)"), bank[2][:], ACT.Copy).then_inc(turn_read, 1)
                    act.activation(tmv[:].rearrange("p a b -> p (a b)"), bank[3][:, 0:256], ACT.Copy).then_inc(turn_read, 1)
                    act.activation(sbk[:], bank[3][0:64, 256:384], ACT.Copy).then_inc(turn_read, 1)
                    act.activation(svv[:], bank[3][0:64, 384:512], ACT.Copy).then_inc(turn_read, 1)
                    act.activation(suv[SAMP:2 * SAMP, :], bank[3][SAMP:2 * SAMP, 384:512], ACT.Copy).then_inc(turn_read, 1)
                elif name == "pairwise":
                    act.wait_ge(pair_mm, 5 * one)
                    for h in range(2):
                        act.activation(ab[:, 2 * h:2 * h + 2, :].rearrange("p a b -> p (a b)"), bank[2 + h][:, 0:256], ACT.Copy).then_inc(ab_read, 1)
                elif name[:6] == "invert" and name[7] == "a":
                    act.wait_ge(yy_mm, 5 * p + int(name[6]))
                    act.activation(yy[:].rearrange("p a b -> p (a b)"), bank[4][:], ACT.Copy).then_inc(yy_read, 1)
                elif name == "state_in":
                    act.wait_ge(state_mm, one)
                    for b in range(2):
                        act.activation(ms[:, 4 * b:4 * b + 4, :].rearrange("p a b -> p (a b)"), bank[2 + b][:], ACT.Copy).then_inc(state_read, 1)
                elif name == "samp_inv_a":
                    act.wait_ge(syy_mm, one)
                    act.activation(syy[:].rearrange("p a b -> p (a b)"), bank[2][0:SAMP, 0:2 * SAMP], ACT.Copy).then_inc(syy_read, 1)
                elif name == "samp_r":
                    act.wait_ge(sr_mm, one)
                    act.activation(sr[:], bank[2][0:SAMP, 0:P], ACT.Copy).then_inc(sr_read, 1)
                elif name == "samp_out":
                    act.wait_ge(so_mm, one)
                    act.activation(so[:].rearrange("p a b -> p (a b)"), bank[3][:], ACT.Copy).then_inc(so_ready, 1)
                elif name[0] == "r" and name[1:].isdigit():
                    c = int(name[1:])
                    rc = slice((c % 2) * CHUNK, (c % 2 + 1) * CHUNK)
                    act.wait_ge(r_mm, NCH * p + c + 1)
                    act.activation(rs[rc, :], bank[4][rc, 0:P], ACT.Copy).then_inc(r_read[c], 1)
                elif name == "mean":
                    act.wait_ge(fin_mm, one)
                    act.activation(sfin[:], bank[2][:, 0:P], ACT.Copy).then_inc(fin_read, 1)
                    act.wait_ge(y_mm, NCH * one)
                    act.activation(yf[:], bank[7][:, 0:NT], ACT.Copy).then_inc(yf_ready, 1)
                    act.wait_ge(yc_ready, one)
                    act.activation(ysq[:], yc[:], ACT.Square).then_inc(ysq_ready, 1)
                elif name == "var":
                    act.wait_ge(var_ready, one)
                    act.activation(sd[:], sd[:], ACT.Sqrt).then_inc(y_root, 1)

            def evict(u, it):
                if u == 3:
                    return
                act.wait_ge(unit_done, U_LOOP + it * LOOP_UNITS + u + 1)
                out = bank[u % 2]
                if u == 4:
                    if not (isinstance(it, int) and it == 0):
                        act.wait_ge(rga_ready, it)
                    act.activation(gg[:], out[:, 0:NT], ACT.Gelu_apprx_tanh).then_inc(gelu_ready, 1)
                elif u == 5:
                    if not (isinstance(it, int) and it == 0):
                        act.wait_ge(ga_saved, 16 * it)
                    act.activation(gat[:], out[:, 0:NT], ACT.Sigmoid).then_inc(ga_ready, 1)
                else:
                    if not (isinstance(it, int) and it == 0 and u == 0):
                        act.wait_ge(mixed, 3 * it + u)
                    act.activation(ex[:], out[:, 0:NX], ACT.Copy).then_inc(ex_ready, 1)

            def gb_evict(u):
                act.wait_ge(unit_done, U_GB + u + 1)
                act.wait_ge(ga_saved, 16 * KT)
                if u:
                    act.wait_ge(gb_saved[(u - 1) % 2], 16 * ((u - 1) // 2 + 1))
                act.activation(gat[:], bank[u % 2][:, 0:NT], ACT.Sigmoid).then_inc(gb_ready, 1)

            def hi_half(n, slot, half, part):
                if part == 0:
                    act.wait_ge(raw_in[slot], 16 * half + 16)
                    act.wait_ge(unit_done, n - 1)
                k = slice(part * KT // 2, (part + 1) * KT // 2)
                act.activation(wh[slot][:, k, :], raw[slot][:, k, :], ACT.Copy).then_inc((half_done, hi_done)[part], 1)

            def step(it, units, chain):
                for slot in range(SLOTS):
                    u, q = divmod(slot, PARTS)
                    if q == 0:
                        if units == "loop":
                            if u:
                                evict(u - 1, it)
                            elif chain:
                                evict(5, it - 1)
                        elif u:
                            gb_evict(u - 1)
                        else:
                            evict(5, it - 1)
                    if q in HI_AT:
                        n, half = ((U_LOOP + it * LOOP_UNITS + u + 1, (U_LOOP + u + 1) // 2 + it * (LOOP_UNITS // 2)) if units == "loop"
                                   else (U_GB + u + 1, (U_GB + u + 1) // 2))
                        hi_half(n, (u + 1) % 2, half, HI_AT.index(q))
                    if chain:
                        for name in LATE.get(slot, []):
                            stage(name, it - 1)
                    if units == "loop":
                        for name in EARLY.get(slot, []):
                            early(name, it)

            step(0, "loop", False)
            step(1, "loop", True)
            with act.Fori(2, KT) as it:
                step(it, "loop", True)
            step(KT, "gb", True)
            gb_evict(5)
            hi(U_GB + 7, 1, (U_GB + 7) // 2)

            def phase(base, evict=None, start=0, stop=KT, ahead=True):
                with act.Fori(start // 2, (stop if ahead else stop - 2) // 2) as i:
                    for u in range(2):
                        if evict:
                            evict(2 * i + u, u, i)
                        hi(base + 2 * i + u + 2, u, base // 2 + i + 1)
                if not ahead:
                    for u in range(2):
                        evict(KT - 2 + u, u, KT // 2 - 1)

            def gb_evict_rest(k, u, i):
                act.wait_ge(unit_done, U_GB + k + 1)
                act.wait_ge(gb_saved[u], 16 * i)
                act.activation(tmp[u][:], bank[u][:, 0:NT], ACT.Sigmoid).then_inc(gb_ready, 1)

            act.wait_ge(rwo_ready, KT)
            act.wait_ge(y_mm, NCH * KT)
            act.wait_ge(rga_ready, KT)

            def gb_and_split(k, u, i):
                gb_evict_rest(k, u, i)
                two = bass.ds(2 * k - 12, 2)
                act.activation(sbh[0][:, two, :], rga[:, two, NB:], ACT.Copy).then_inc(split_hi, 1)

            phase(U_GB, gb_and_split, start=6, stop=14)
            phase(U_GB, gb_evict_rest, start=14)

            def split_b(k, u, i):
                one = bass.ds(k, 1)
                act.activation(sbh[1][:, one, :], rwo[:, one, :], ACT.Copy).then_inc(split_hi, 1)

            phase(U_RGO, split_b)

            def split_merged(k, u, i):
                act.wait_ge(merged, KT + k + 1)
                act.activation(sbh[0][:, bass.ds(k, 1), :].rearrange("p o t -> p (o t)"), rwo[:, bass.ds(k, 1), :].rearrange("p o t -> p (o t)"), ACT.Copy).then_inc(merged_hi, 1)

            phase(U_RWO, split_merged)
            phase(U_WO)
            act.wait_ge(x_done, KT)
            norm(1, NT)
            norm_split(1, NT, xh)
            n = 0
            for kind, g in FFN_PLAN:
                base = U_FFN + n * KT

                def hidden(k, u, i, base=base, g=g):
                    act.wait_ge(unit_done, base + k + 1)
                    if not (g == 0 and isinstance(i, int)):
                        act.wait_ge(h_lo, KT * g + k - 1)
                    act.activation(tmp[u][:], bank[u][:, 0:NT], ACT.Relu).then_inc(h_relu, 1)
                    act.wait_ge(h_relu, KT * g + k + 1)
                    act.activation(tmp[u][:], tmp[u][:], ACT.Square).then_inc(h_sq, 1)
                    act.wait_ge(h_sq, KT * g + k + 1)
                    act.activation(sbh[g % 2][:, bass.ds(k, 1), :].rearrange("p o t -> p (o t)"), tmp[u][:], ACT.Copy).then_inc(h_hi, 1)

                if kind == "up" and g == 0:
                    for u in range(2):
                        hidden(u, u, 0)
                        hi(base + u + 2, u, base // 2 + 1)
                    phase(base, lambda k, u, i, h=hidden: h(k, u, i), start=2)
                else:
                    phase(base, hidden if kind == "up" else None)
                n += 1
            act.wait_ge(x_done, 5 * KT)
            norm(2, NT)
            norm_split(2, NT, xh)

            def ple_gate(k, u, i):
                act.wait_ge(unit_done, U_PLE + k + 1)
                act.wait_ge(x_done, 5 * KT + k - 1)
                act.activation(tmp[u][:], bank[u][:, 0:NT], ACT.Sigmoid).then_inc(sg_ready, 1)

            phase(U_PLE, ple_gate, ahead=False)
            for b in range(4):
                act.wait_ge(small_mm, b + 1)
                act.activation(small_out[:, b * 512:(b + 1) * 512], bank[4 + b % 2][0:NOUTF, :], ACT.Copy).then_inc(small_read, 1)
            act.wait_ge(x_done, 6 * KT)
            norm(3, NT)
            for j in range(8):
                act.wait_ge(y_turn, j + 1)
                b3 = (2, 3, 4) if j % 2 == 0 else (5, 6, 1)
                cols = slice(j * 256, (j + 1) * 256)
                act.activation(ytok[0:SAMP, 0, cols], bank[b3[0]][0:SAMP, 0:256], ACT.Copy).then_inc(y_read, 1)
                for u in range(2):
                    act.activation(ytok[:, 1 + u, cols], bank[b3[1 + u]][:, 0:256], ACT.Copy).then_inc(y_read, 1)

        @block.vector
        def _(dve):
            def lo(n, slot):
                dve.wait_ge(hi_done, n + 1)
                dve.tensor_tensor(wl[slot][:], raw[slot][:], wh[slot][:].bitcast(F32), ALU.subtract).then_inc(lo_done, 1)

            def tt_(out, x, y, op):
                return dve.tensor_tensor(out, x, y, op)

            def stt(out, x, s, y, op0, op1):
                return dve.scalar_tensor_tensor(out, x, s, y, op0, op1)

            def ts(out, x, s1, s2=None, op0=ALU.mult, op1=ALU.bypass):
                return dve.tensor_scalar(out, x, s1, s2, op0, op1)

            lo(0, 0)
            lo(1, 1)
            for b in range(2):
                dve.wait_ge(xt_mm, b + 1)
                dve.tensor_copy(rga[:, 8 * b:8 * b + 8, 0:40], bank[b][:, 0:320].rearrange("p (k t) -> p k t", k=8)).then_inc(xt_dve, 1)
            for b in range(2):
                dve.wait_ge(par_mm, b + 1)
                dve.tensor_copy(par[:, 8 * b:8 * b + 8, :], bank[6 + b][:, 0:8 * NPAR].rearrange("p (k t) -> p k t", k=8)).then_inc(par_ready, 1)
            for b in range(4):
                dve.wait_ge(xt_mm, 7 + b)
                dve.tensor_copy(rga[:, 4 * b:4 * b + 4, 40 + P:NX], bank[b][:].rearrange("p (k t) -> p k t", k=4)).then_inc(xt_dve, 1)

            def norm(k, width, gain, split):
                first = NX - width
                v, y, t = mean_sq[:, first:], sums[:, first:], nsq[0][:, 0, first:]
                dve.wait_ge(sum_mm, 8 + k)
                ts(v, bank[7][:, 0:width], EPS, op0=ALU.add).then_inc(rms_var, 1)
                dve.wait_ge(rms_std, k + 1)
                dve.reciprocal(y, y).then_inc(rms_inv, 1)
                dve.wait_ge(rms_inv, 5 * k + 1)
                tt_(t, y, y, ALU.mult).then_inc(rms_inv, 1)
                dve.wait_ge(rms_inv, 5 * k + 2)
                tt_(t, t, v, ALU.mult).then_inc(rms_inv, 1)
                dve.wait_ge(rms_inv, 5 * k + 3)
                ts(t, t, -0.5, 1.5, ALU.mult, ALU.add).then_inc(rms_inv, 1)
                dve.wait_ge(rms_inv, 5 * k + 4)
                tt_(y, y, t, ALU.mult).then_inc(rms_inv, 1)
                dve.wait_ge(rms_inv, 5 * k + 5)

                def low_part(j):
                    dve.wait_ge(nrm_hi, 8 * k + j + 1)
                    tt_(split[1][:, 2 * j:2 * j + 2, first:], nrm[j % 2][:, :, first:], split[0][:, 2 * j:2 * j + 2, first:].bitcast(F32),
                        ALU.subtract).then_inc(nrm_lo, 1)

                for j in range(8):
                    n = nrm[j % 2]
                    if j >= 2:
                        if split:
                            dve.wait_ge(nrm_lo, 8 * k + j - 1)
                        else:
                            dve.wait_ge(y_turn, j - 1)
                    if k == 0:
                        if j >= 2:
                            dve.wait_ge(nrm_copy, j - 1)
                        dve.tensor_copy(n[:, :, 0:NB], rga[:, 2 * j:2 * j + 2, 0:NB])
                    for h in range(2):
                        ins = stt(n[:, h, NB:], rga[:, 2 * j + h, NB:], par[:, 2 * j + h, gain:gain + 1], sums[:, NB:], ALU.mult, ALU.mult)
                    ins.then_inc(nrm_ready, 1)
                    if k == 0:
                        dve.wait_ge(nrm_ready, j + 1)
                        dve.tensor_copy(outf[:, 2 * j:2 * j + 2, O_SHIFT:O_SHIFT + 1], n[:, :, NX - 1:NX])
                        dve.tensor_copy(outf[:, 2 * j:2 * j + 2, O_SHIFT + 1:O_SHIFT + 1 + NB], n[:, :, NB + SAMP - NB:NB + SAMP]).then_inc(nrm_copy, 1)
                    if split and j:
                        low_part(j - 1)
                if split:
                    low_part(7)

            norm(0, NX, GMIX, (xh, xl))

            head = Count(der_step, 0, 0)
            lam = par[:, :, LAM]
            w1, w2, w3, w4 = (der_work[:, :, k] for k in range(4))
            ts(w1, lam, -1.0).then_inc(head.sem, head.one())
            dve.wait_ge(head.sem, head.so_far())
            tt_(w1, w1, lam, ALU.max).then_inc(head.sem, head.one())
            dve.wait_ge(head.sem, head.so_far())
            dve.tensor_copy(w2, w1).then_inc(lam_abs, 1)
            dve.wait_ge(lam_exp, 1)
            ts(w3, w2, 2.0, op0=ALU.add).then_inc(head.sem, head.one())
            dve.wait_ge(head.sem, head.so_far())
            dve.reciprocal(w3, w3).then_inc(head.sem, head.one())
            dve.wait_ge(head.sem, head.so_far())
            tt_(w2, w2, w3, ALU.mult).then_inc(head.sem, head.one())
            dve.wait_ge(head.sem, head.so_far())
            tt_(w3, w2, w2, ALU.mult).then_inc(head.sem, head.one())
            dve.memset(w4, 1.0 / 19).then_inc(head.sem, head.one())
            dve.wait_ge(head.sem, head.so_far())
            for k in range(8, -1, -1):
                tt_(w4, w4, w3, ALU.mult).then_inc(head.sem, head.one())
                dve.wait_ge(head.sem, head.so_far())
                ts(w4, w4, 1.0 / (2 * k + 1), op0=ALU.add).then_inc(head.sem, head.one())
                dve.wait_ge(head.sem, head.so_far())
            tt_(w4, w4, w2, ALU.mult).then_inc(head.sem, head.one())
            ts(w1, lam, -1.0, 0.0, ALU.mult, ALU.max).then_inc(head.sem, head.one())
            dve.wait_ge(head.sem, head.so_far())
            stt(w4, w4, 2.0, w1, ALU.mult, ALU.add).then_inc(head.sem, head.one())
            dve.wait_ge(head.sem, head.so_far())
            ts(der[:, :, SP8], w4, 8.0).then_inc(head.sem, head.one())
            ts(der[:, :, NSP8], w4, -8.0).then_inc(head.sem, head.one())
            dve.wait_ge(head.sem, head.so_far())

            def shift_mix(mu, z, chain, done):
                tt_(dif[:, 0:SAMP], ex[:, 0:SAMP], ex[:, NB:NB + SAMP], ALU.subtract).then_inc(chain.sem, chain.one())
                ts(dif[:, SAMP:SAMP + 1], ex[:, NB + SAMP:NB + SAMP + 1], -1.0).then_inc(chain.sem, chain.one())
                tt_(dif[:, SAMP + 1:NT], ex[:, NB + SAMP:NX - 1], ex[:, NB + SAMP + 1:NX], ALU.subtract).then_inc(chain.sem, chain.one())
                dve.wait_ge(chain.sem, chain.so_far())
                stt(z, dif[:], mu, ex[:, NB:NX], ALU.mult, ALU.add).then_inc(done, 1)

            for n in range(4):
                dve.wait_ge(low_ex, n + 1)
                if n:
                    dve.wait_ge(low_mix, n)
                shift_mix(par[:, 0, MULOW + n:MULOW + n + 1], low[:, n, :], head, low_mix)
                if n < 3:
                    lo(n + 2, n % 2)

            def conv(it, chain):
                dve.wait_ge(unit_done, U_LOOP + it * LOOP_UNITS + 4)
                if isinstance(it, int) and it == 0:
                    dve.wait_ge(init_done, N_INIT)
                else:
                    dve.wait_ge(rgi_mm, it)
                dve.tensor_copy(ue[:, 24:24 + SAMP], bank[1][:, 0:SAMP]).then_inc(chain.sem, chain.one())
                dve.tensor_copy(ue[:, 59:315], bank[1][:, SAMP:NT]).then_inc(ue_ready, 1)
                dve.tensor_copy(ue[:, 0:24], ptu[:, CONV_STATE:CONV_STATE + 24]).then_inc(chain.sem, chain.one())
                dve.wait_ge(chain.sem, chain.so_far())
                dve.wait_ge(ue_ready, it + 1)
                parts = ((0, SAMP, 0, NB), (SAMP, NT, 56, 1))
                for x0, x1, o, by in parts:
                    ts(xc[:, x0:x1], ue[:, o:o + x1 - x0], ptu[:, CW:CW + 1], ptu[:, CB:CB + 1], ALU.mult, ALU.add).then_inc(chain.sem, chain.one())
                for j in range(1, 4):
                    dve.wait_ge(chain.sem, chain.so_far())
                    for x0, x1, o, by in parts:
                        ins = stt(xc[:, x0:x1], ue[:, o + j * by:o + j * by + x1 - x0], ptu[:, CW + j:CW + j + 1], xc[:, x0:x1], ALU.mult, ALU.add)
                        if j == 3 and x0:
                            ins.then_inc(conv_ready, 1)
                        else:
                            ins.then_inc(chain.sem, chain.one())
                dve.tensor_copy(outf[:, bass.ds(it, 1), O_CONV:O_CONV + 3].rearrange("p o t -> p (o t)"), ue[:, 312:315]).then_inc(chain.sem, chain.one())
                dve.tensor_copy(outf[:, bass.ds(it, 1), O_CONV + 3:NOUTF].rearrange("p o t -> p (o t)"), ue[:, 24 + NB:24 + SAMP]).then_inc(chain.sem, chain.one())

            def scalar(col):
                return ptc[:, col:col + 1]

            def early(name, it, rg):
                one = it + 1
                if name == "ad":
                    dve.wait_ge(sig_ready, 2 * it + 2)
                    (ts(kp[:], siga[:], 1.0, ptu[:, KA:KA + 1], ALU.subtract, ALU.mult)).then_inc(rg.sem, rg.one())
                    dve.wait_ge(rg.sem, rg.so_far())
                    (stt(kp[:], kp[:], 1.0, zk[:], ALU.add, ALU.mult)).then_inc(rg.sem, rg.one())
                elif name == "kk_sum":
                    dve.wait_ge(kk_mm, one)
                    ts(rn[:], bank[7][:, 0:NT], 1e-24, op0=ALU.max).then_inc(ss_ready, 1)
                elif name == "kk":
                    dve.wait_ge(kk_root, one)
                    dve.reciprocal(rn[:], rn[:]).then_inc(rg.sem, rg.one())
                    dve.wait_ge(rg.sem, rg.so_far())
                    stt(kkn[:], zk[:], ptu[:, KK:KK + 1], rn[:], ALU.mult, ALU.mult).then_inc(rg.sem, rg.one())
                elif name == "cum":
                    dve.wait_ge(decay_ready, one)
                    if isinstance(it, int) and it == 0:
                        dve.wait_ge(init_done, N_INIT)
                    for c in range(NCH):
                        o = 5 * NB + c * (CHUNK + 1) + 1
                        dve.tensor_tensor_scan(cum[:, o:o + CHUNK], sigw[:, SAMP + c * CHUNK:SAMP + (c + 1) * CHUNK], zeros[:], 1.0,
                                               ALU.mult, ALU.add).then_inc(rg.sem, rg.one())
                    for t in range(NS):
                        dve.wait_ge(rg.sem, rg.so_far())
                        tt_(cum[:, (t + 1) * NB:(t + 2) * NB], cum[:, t * NB:(t + 1) * NB], sigw[:, t * NB:(t + 1) * NB],
                            ALU.mult).then_inc(rg.sem, rg.one())
                    dve.wait_ge(rg.sem, rg.so_far())
                    at = cum_of("at")
                    dve.reciprocal(rn[:, samp_all], at[0]).then_inc(rg.sem, rg.one())
                    dve.reciprocal(chunks(rn[:]), at[1]).then_inc(rg.sem, rg.one())
                elif name == "tilde":
                    tt_(btl[:], kkn[:], siga[:], ALU.mult).then_inc(rg.sem, rg.one())
                    dve.wait_ge(rg.sem, rg.so_far())
                    tt_(btl[:], btl[:], rn[:], ALU.mult).then_inc(rg.sem, rg.one())
                    tt_(ktl[:], kp[:], rn[:], ALU.mult).then_inc(rg.sem, rg.one())
                    dve.wait_ge(rg.sem, rg.so_far())
                    last = cum[:, NS * NB:(NS + 1) * NB].unsqueeze(1).to_broadcast([P, NS, NB])
                    for k, src in enumerate((btl, ktl)):
                        tt_(bkh[:, k * SAMP:(k + 1) * SAMP].rearrange("p (t b) -> p t b", b=NB),
                            src[:, samp_all].rearrange("p (t b) -> p t b", b=NB), last, ALU.mult).then_inc(rg.sem, rg.one())
                elif name == "early_done":
                    dve.wait_ge(mixed, 3 * one)
                    dve.tensor_copy(vv[:, 0:SAMP], zv[:, samp_all]).then_inc(rg.sem, rg.one())
                    dve.tensor_copy(vv[:, SAMP:], zv[:, samp_all]).then_inc(early_end, 1)

            def stage(name, p, ch):
                one = p + 1
                later = not (isinstance(p, int) and p == 0)
                if name == "ar":
                    if later:
                        dve.wait_ge(rwo_ready, p)
                        dve.wait_ge(m_ready, NCH * p)
                        dve.wait_ge(sexp_ready, p)
                    dve.wait_ge(early_end, one)
                    (dve.tensor_copy(dtc[:], der[:, bass.ds(p, 1), :].rearrange("p o t -> p (o t)"))).then_inc(ch.sem, ch.one())
                    dve.tensor_copy(ptc[:], par[:, bass.ds(p, 1), :].rearrange("p o t -> p (o t)")).then_inc(ptc_ready, 1)
                    dve.wait_ge(ptc_ready, one)
                    stt(bv[:], zr[:], scalar(RK), kp[:], ALU.mult, ALU.mult).then_inc(bt_ready, 1)
                    for c in range(NCH):
                        dve.tensor_copy(dl[:, c:c + 1], last_decay(c)).then_inc(ch.sem, ch.one())
                    before, at = cum_of("before"), cum_of("at")
                    for out, x, s, y in ((ar[:, 0, samp_all], kkn[:, samp_all], -1.0, before[0]),
                                         (chunks(ar[:, 0, :]), chunks(kkn[:]), -1.0, before[1]),
                                         (ar[:, 1, samp_all], zr[:, samp_all], 1.0, at[0])):
                        stt(out, x, s, y, ALU.mult, ALU.mult).then_inc(ch.sem, ch.one())
                    tt_(chunks(ar[:, 1, :]), chunks(zr[:]), at[1], ALU.mult).then_inc(ar_ready, 1)
                elif name == "rg_gates":
                    dve.wait_ge(rgi_sig, one)
                    dve.wait_ge(rgr_sig, one)
                    tt_(rgi[:], rgi[:], xc[:], ALU.mult).then_inc(ch.sem, ch.one())
                elif name == "gate_bonus":
                    dve.wait_ge(bonus_mm, one)
                    tt_(bv[:], bank[5][:, 0:NT], zv[:], ALU.mult).then_inc(bonus_read, 1)
                elif name == "rg_decay":
                    dve.wait_ge(rg_exp, one)
                    tt_(m2[:], rgr[:], rgr[:], ALU.mult).then_inc(ch.sem, ch.one())
                    dve.wait_ge(ch.sem, ch.so_far())
                    stt(m2[:], m2[:], 1.0, th[:], ALU.add, ALU.mult).then_inc(m2_ready, 1)
                elif name == "rg_scan":
                    dve.wait_ge(m_root, one)
                    dve.memset(m2[:, SAMP:SAMP + 1], 1.0).then_inc(ch.sem, ch.one())
                    dve.wait_ge(ch.sem, ch.so_far())
                    tt_(m2[:], m2[:], rgi[:], ALU.mult).then_inc(ch.sem, ch.one())
                    dve.wait_ge(ch.sem, ch.so_far())
                    dve.tensor_tensor_scan(th[:, SAMP:NT], rgr[:, SAMP:NT], m2[:, SAMP:NT], 0.0, ALU.mult, ALU.add).then_inc(ch.sem, ch.one())
                    for t in range(NS):
                        now = slice(t * NB, (t + 1) * NB)
                        prev = ptc[:, H_STATE:H_STATE + NB] if t == 0 else th[:, (t - 1) * NB:t * NB]
                        tt_(th[:, now], rgr[:, now], prev, ALU.mult).then_inc(ch.sem, ch.one())
                        dve.wait_ge(ch.sem, ch.so_far())
                        tt_(th[:, now], th[:, now], m2[:, now], ALU.add).then_inc(ch.sem, ch.one())
                        dve.wait_ge(ch.sem, ch.so_far())
                    dve.tensor_copy(outf[:, bass.ds(p, 1), O_H:O_H + 1].rearrange("p o t -> p (o t)"), th[:, NT - 1:NT]).then_inc(ch.sem, ch.one())
                    dve.tensor_copy(outf[:, bass.ds(p, 1), O_H + 1:O_H + 1 + NB].rearrange("p o t -> p (o t)"), th[:, SAMP - NB:SAMP]).then_inc(ch.sem, ch.one())
                    dve.wait_ge(gelu_ready, one)
                    if not later:
                        dve.wait_ge(xt_saved, 16)
                    tt_(rga[:, bass.ds(p, 1), NB:].rearrange("p o t -> p (o t)"), th[:], gg[:], ALU.mult).then_inc(rga_ready, 1)
                elif name == "pairwise":
                    masks = cst[:, C_AM:C_AM + 512]
                    for g in range(2):
                        for h in range(2):
                            dve.wait_ge(pair_mm, 5 * p + 2 * g + h + 1)
                            tt_(ams[:, 2 * h + g, :], bank[4 + 2 * g + h][:], masks, ALU.mult).then_inc(pair_read, 1)
                    dve.wait_ge(ab_read, 2 * one)
                    tt_(tn[:], ab[:], cst[:, C_LM:C_LM + P].unsqueeze(1).to_broadcast([P, 4, P]), ALU.mult).then_inc(ch.sem, ch.one())
                    eye = ident.unsqueeze(1).to_broadcast([P, 4, P])
                    dve.wait_ge(pair_read, 4 * one)
                    tt_(tt[:], ams[:, :, 0:P], eye, ALU.add).then_inc(ch.sem, ch.one())
                    dve.wait_ge(ch.sem, ch.so_far())
                    tt_(tn[:], tn[:], eye, ALU.add).then_inc(t_start, 1)
                    dve.wait_ge(t_start, one)
                elif name[:6] == "invert" and name[7] == "b":
                    l = int(name[6])
                    dve.wait_ge(tn_mm, 5 * p + l)
                    if l > 1:
                        dve.wait_ge(tn_ready, 5 * p + l - 1)
                    for out, b, part in ((tt, 5, 1), (tn, 6, 0))[:2 if l < 5 else 1]:
                        for q in range(4):
                            at = blocks(out[:, q, :], l, part)
                            ins = tt_(at, at, bank[b][:, q * HEAD:(q + 1) * HEAD].rearrange("p (n m) -> p n m", m=2 ** l), ALU.add)
                            if q == 3 and b == (6 if l < 5 else 5):
                                ins.then_inc(tn_ready, 1)
                            else:
                                ins.then_inc(ch.sem, ch.one())
                    dve.wait_ge(ch.sem, ch.so_far())
                elif name == "samp_prep":
                    tt_(aex[:], ar[:, 0, samp_all].unsqueeze(1).to_broadcast([P, NB, SAMP]),
                           cst[:, C_SEQ:C_SEQ + 256].rearrange("p (b t) -> p b t", b=NB), ALU.mult).then_inc(ch.sem, ch.one())
                    dve.wait_ge(turn_read, 5 * one)
                    own = cst[0:2 * SAMP, C_SQT:C_SQT + NB].unsqueeze(2).to_broadcast([2 * SAMP, NB, HEAD])
                    for h in range(2):
                        tt_(bke[:, h, :].rearrange("p (b j) -> p b j", b=NB),
                               sbk[:, h * HEAD:(h + 1) * HEAD].unsqueeze(1).to_broadcast([2 * SAMP, NB, HEAD]), own, ALU.mult).then_inc(ch.sem, ch.one())
                    if later:
                        dve.wait_ge(so_saved, 16 * p)
                    tt_(dg[:], cst[:, C_ID2:C_ID2 + HEAD].unsqueeze(1).to_broadcast([P, NB, HEAD]),
                        cum[:, NS * NB:(NS + 1) * NB].unsqueeze(2).to_broadcast([P, NB, HEAD]), ALU.mult).then_inc(sexp_ready, 1)
                elif name == "samp_pair":
                    dve.wait_ge(spair_mm, one)
                    for h in range(2):
                        tt_(sam[:, h, :], bank[2 + h][0:SAMP, 0:128], cst[0:SAMP, C_SAM:C_SAM + 128], ALU.mult).then_inc(ch.sem, ch.one())
                        tt_(stn[:, h, :], bank[2 + h][0:SAMP, 128:160], cst[0:SAMP, C_SLM:C_SLM + SAMP], ALU.mult).then_inc(ch.sem, ch.one())
                        tt_(sa2[:, h, :], bank[2 + h][0:SAMP, 128:160], cst[0:SAMP, C_SLM + SAMP:C_SLM + 2 * SAMP], ALU.mult).then_inc(ch.sem, ch.one())
                    dve.wait_ge(ch.sem, ch.so_far())
                    eye = cst[0:SAMP, C_ID:C_ID + SAMP].unsqueeze(1).to_broadcast([SAMP, 2, SAMP])
                    tt_(stn[:], stn[:], eye, ALU.add).then_inc(ch.sem, ch.one())
                    tt_(stt_s[:], sam[:, :, 0:SAMP], eye, ALU.add).then_inc(sinv_ready, 1)
                    dve.wait_ge(sinv_ready, one)
                elif name == "samp_inv_b":
                    dve.wait_ge(stt_mm, one)
                    flat = "p a b -> p (a b)"
                    tt_(stt_s[:].rearrange(flat), stt_s[:].rearrange(flat), bank[3][0:SAMP, 0:2 * SAMP], ALU.add).then_inc(stt_ready, 1)
                elif name == "samp_u":
                    dve.wait_ge(su_mm, one)
                    dve.tensor_copy(suv[0:SAMP, :], bank[3][0:SAMP, 0:P]).then_inc(su_read, 1)
                elif name[0] == "u":
                    c = int(name[1:])
                    rc = slice((c % 2) * CHUNK, (c % 2 + 1) * CHUNK)
                    dve.wait_ge(u_mm, NCH * p + c + 1)
                    dve.tensor_copy(us[rc, :], bank[5][rc, 0:P]).then_inc(u_read, 1)
                elif name[:2] == "my":
                    c = int(name[2:])
                    dve.wait_ge(m_mm, NCH * p + c + 1)
                    new = mp[(c + 1) % 2]
                    if c:
                        if c == 1 and later:
                            dve.wait_ge(fin_saved, 32 * p)
                        dve.wait_ge(m_ready, NCH * p + c)
                        tt_(mtmp[:], mp[c % 2][:], bank[6][:, 0:P], ALU.add).then_inc(ch.sem, ch.one())
                        dve.wait_ge(ch.sem, ch.so_far())
                        stt(new[:], mtmp[:], dl[:, c:c + 1], bd, ALU.mult, ALU.mult).then_inc(m_ready, 1)
                    else:
                        stt(new[:], bank[6][:, 0:P], dl[:, c:c + 1], bd, ALU.mult, ALU.mult).then_inc(m_ready, 1)
                elif name == "mean":
                    dve.wait_ge(mean_mm, one)
                    stt(yc[:], bank[4][:, 0:NT], -1.0 / HEAD, yf[:], ALU.mult, ALU.add).then_inc(yc_ready, 1)
                elif name == "var":
                    dve.wait_ge(var_mm, one)
                    ts(sd[:], bank[5][:, 0:NT], 1.0 / HEAD, GN_EPS, ALU.mult, ALU.add).then_inc(var_ready, 1)
                    dve.wait_ge(y_root, one)
                    dve.reciprocal(sd[:], sd[:]).then_inc(ch.sem, ch.one())
                    dve.wait_ge(ch.sem, ch.so_far())
                    stt(yc[:], yc[:], scalar(GNW), sd[:], ALU.mult, ALU.mult).then_inc(ch.sem, ch.one())
                    dve.wait_ge(ch.sem, ch.so_far())
                    stt(yc[:], yc[:], scalar(GNB), bv[:], ALU.add, ALU.add).then_inc(ch.sem, ch.one())
                    dve.wait_ge(ch.sem, ch.so_far())
                    tt_(rwo[:, bass.ds(p, 1), :].rearrange("p o t -> p (o t)"), yc[:], gout[:], ALU.mult).then_inc(rwo_ready, 1)

            def lo_half(n, slot, part):
                dve.wait_ge((half_done, hi_done)[part], n - U_LOOP if part == 0 else n + 1)
                k = slice(part * KT // 2, (part + 1) * KT // 2)
                ins = dve.tensor_tensor(wl[slot][:, k, :], raw[slot][:, k, :], wh[slot][:, k, :].bitcast(F32), ALU.subtract)
                if part:
                    ins.then_inc(lo_done, 1)

            def step(it, units, chain):
                rg = Count(dve_rg, it, STEPS["dve_rg"])
                ch = Count(dve_ch, it - 1, STEPS["dve_ch"])
                for slot in range(SLOTS):
                    u, q = divmod(slot, PARTS)
                    if q == 0 and units == "loop":
                        if u == 0:
                            if chain:
                                dve.wait_ge(rg.sem, rg.so_far())
                                dve.wait_ge(conv_ready, it)
                            dve.tensor_copy(ptu[:], par[:, bass.ds(it, 1), :].rearrange("p o t -> p (o t)")).then_inc(rg.sem, rg.one())
                        elif u <= 3:
                            if chain:
                                dve.wait_ge(ch.sem, ch.so_far())
                            dve.wait_ge(ex_ready, 3 * it + u)
                            if not (isinstance(it, int) and it == 0 and u == 1):
                                dve.wait_ge(mixed, 3 * it + u - 1)
                            if u == 1:
                                dve.wait_ge(rg.sem, rg.so_far())
                            col = (MUK, MUR, MUV)[u - 1]
                            shift_mix(ptu[:, col:col + 1], (zk, zr, zv)[u - 1][:], rg, mixed)
                        elif u == 4:
                            if chain:
                                dve.wait_ge(ch.sem, ch.so_far())
                            conv(it, rg)
                    if q in LO_AT:
                        n = U_LOOP + it * LOOP_UNITS + u + 1 if units == "loop" else U_GB + u + 1
                        lo_half(n, (u + 1) % 2, LO_AT.index(q))
                    if chain:
                        for name in LATE.get(slot, []):
                            stage(name, it - 1, ch)
                    if units == "loop":
                        for name in EARLY.get(slot, []):
                            early(name, it, rg)
                if units == "loop":
                    rg.end()
                if chain:
                    ch.end()

            step(0, "loop", False)
            step(1, "loop", True)
            with dve.Fori(2, KT) as it:
                step(it, "loop", True)
            step(KT, "gb", True)
            lo(U_GB + 7, 1)

            def phase(base, evict=None, start=0, stop=KT, ahead=True):
                with dve.Fori(start // 2, (stop if ahead else stop - 2) // 2) as i:
                    for u in range(2):
                        if evict:
                            evict(2 * i + u, u, i)
                        lo(base + 2 * i + u + 2, u)
                if not ahead:
                    for u in range(2):
                        evict(KT - 2 + u, u, KT // 2 - 1)

            def tile(buf, k, first=0):
                return buf[:, bass.ds(k, 1), first:].rearrange("p o t -> p (o t)")

            def split_a(k, u, i):
                dve.wait_ge(split_hi, k - 5)
                two = bass.ds(2 * k - 12, 2)
                tt_(sbl[0][:, two, :], rga[:, two, NB:], sbh[0][:, two, :].bitcast(F32), ALU.subtract).then_inc(split_lo, 1)

            phase(U_GB, split_a, start=6, stop=14)
            phase(U_GB, start=14)

            def merge_a(k, u, i):
                dve.wait_ge(split_hi, 8 + k + 1)
                tt_(tile(sbl[1], k), tile(rwo, k), tile(sbh[1], k).bitcast(F32), ALU.subtract).then_inc(split_lo, 1)
                dve.wait_ge(split_lo, 8 + k + 1)
                dve.wait_ge(unit_done, U_RGO + k + 1)
                dve.wait_ge(g_in[u], 16 * i + 16)
                tt_(tile(rwo, k), bank[u][:, 0:NT], gt[u][:], ALU.mult).then_inc(merged, 1)

            def merge_b(k, u, i):
                dve.wait_ge(unit_done, U_RWO + k + 1)
                dve.wait_ge(g_in[u], 16 * (KT // 2) + 16 * i + 16)
                tt_(tmp[u][:], bank[u][:, 0:NT], gt[u][:], ALU.mult).then_inc(gated, 1)
                dve.wait_ge(gated, k + 1)
                tt_(tile(rwo, k), tile(rwo, k), tmp[u][:], ALU.add).then_inc(merged, 1)
                dve.wait_ge(merged_hi, k + 1)
                tt_(tile(sbl[0], k), tile(rwo, k), tile(sbh[0], k).bitcast(F32), ALU.subtract).then_inc(merged_lo, 1)

            def square_sum(k, u, n):
                dve.wait_ge(x_done, n)
                sq = nsq[u][:, 0, 0:NT]
                tt_(sq, tile(rga, k, NB), tile(rga, k, NB), ALU.mult).then_inc(sq_done, 1)

            def square_add(u, n):
                dve.wait_ge(sq_done, n)
                dve.wait_ge(acc_clear, 1)
                tt_(acc, acc, nsq[u][:, 0, 0:NT], ALU.add).then_inc(acc_ready, 1)

            def residual(base, squares=None):
                def evict(k, u, i):
                    dve.wait_ge(unit_done, base + k + 1)
                    tt_(tile(rga, k, NB), tile(rga, k, NB), bank[u][:, 0:NT], ALU.add).then_inc(x_done, 1)
                    if squares is not None:
                        square_sum(k, u, squares[0] + k + 1)
                        square_add(u, squares[1] + k + 1)
                return evict

            phase(U_RGO, merge_a)
            phase(U_RWO, merge_b)
            dve.wait_ge(x_back, 16)
            dve.wait_ge(merged_lo, KT)
            dve.memset(acc, 0.0).then_inc(acc_clear, 1)
            phase(U_WO, residual(U_WO, (0, 0)))
            norm(1, NT, GFFN, (xh, xl))
            n = 0
            for kind, g in FFN_PLAN:
                def hidden_lo(k, u, i, g=g):
                    dve.wait_ge(h_hi, KT * g + k + 1)
                    tt_(tile(sbl[g % 2], k), tmp[u][:], tile(sbh[g % 2], k).bitcast(F32), ALU.subtract).then_inc(h_lo, 1)

                base = U_FFN + n * KT
                if kind == "down":
                    dve.wait_ge(x_done, (g + 1) * KT)
                if n == 7:
                    dve.memset(acc, 0.0).then_inc(acc_clear, 1)
                phase(base, hidden_lo if kind == "up" else residual(base, (4 * KT, KT) if n == 7 else None))
                n += 1
            dve.wait_ge(pt_mm, 1)
            for k in range(2):
                dve.tensor_copy(pt[:, k, :], bank[4 + k][:, 0:NT]).then_inc(pt_ready, 1)
            dve.wait_ge(x_done, 5 * KT)
            norm(2, NT, GPLE, (xh, xl))

            def embed(k, u, i):
                dve.wait_ge(sg_ready, k + 1)
                dve.wait_ge(embed_mm, k + 1)
                tt_(tmp[u][:], tmp[u][:], bank[2 + u][:, 0:NT], ALU.mult).then_inc(tmp_ready, 1)
                dve.wait_ge(tmp_ready, k + 1)
                tt_(tile(rga, k, NB), tile(rga, k, NB), tmp[u][:], ALU.add).then_inc(x_done, 1)
                square_sum(k, u, 5 * KT + k + 1)
                square_add(u, 2 * KT + k + 1)

            dve.memset(acc, 0.0).then_inc(acc_clear, 1)
            phase(U_PLE, embed, ahead=False)
            dve.wait_ge(x_done, 6 * KT)
            norm(3, NT, GFIN, None)

        @block.gpsimd
        def _(pool):
            pool.memset(rows[0:NPAR, :], 0.0).then_inc(rows_zero, 1)
            pool.wait_ge(par_ready, 2)
            pool.wait_ge(nrm_lo, 8)
            pool.wait_ge(nrm_copy, 8)
            for view, value in ((s0[:], 0.0), (cum[:], 1.0), (zeros[:], 0.0), (ue[:], 0.0)):
                pool.memset(view, value).then_inc(init_done, 1)

            def masked(p):
                pool.wait_ge(ab_read, 2 * (p + 1))
                for l in range(1, 6):
                    if l > 2:
                        pool.wait_ge(yy_mm, 5 * p + l - 2)
                    elif not (isinstance(p, int) and p == 0):
                        pool.wait_ge(yy_mm, 5 * p)
                    mask = cst[:, C_LM + l * P:C_LM + (l + 1) * P].unsqueeze(1).to_broadcast([P, 4, P])
                    pool.tensor_tensor(am[l % 2][:], ab[:], mask, ALU.mult).then_inc(am_ready, 1)

            masked(0)
            with pool.Fori(1, KT) as p:
                masked(p)


_INS = ['x_prompt', 'x_sample', 'p_prompt', 'p_sample', 'state_rg_h', 'state_rg_conv', 'state_rwkv', 'state_shift',
        'norm_mix', 'w_in', 'conv_w', 'conv_b', 'rg_wa', 'rg_ba', 'rg_wx', 'rg_bx', 'rg_lam', 'w_rg_o', 'mu_shift',
        'rw_w0', 'rw_w2', 'rw_a0', 'rw_a2', 'rw_g2', 'rw_kk', 'rw_ka', 'rw_rk', 'rw_gn_w', 'rw_gn_b', 'w_rw_o', 'w_o',
        'norm_ffn', 'w_up', 'w_down', 'norm_ple', 'w_ple_gate', 'w_ple', 'norm_f']
_OUTS = [("o_y_p", (1, SEQ, D)), ("o_y_s", (NB, NS, D)), ("o_h_p", (1, 1, D)), ("o_conv_p", (1, 1, 3, D)),
         ("o_rwkv_p", (1, 1, D // HEAD, HEAD, HEAD)), ("o_shift_p", (1, 1, D)),
         ("o_h_s", (1, NB, D)), ("o_conv_s", (1, NB, 3, D)), ("o_rwkv_s", (1, NB, D // HEAD, HEAD, HEAD)),
         ("o_shift_s", (1, NB, D))]


def kernel(**inputs):
    import concourse.bacc as _bacc
    from concourse.bass_utils import run_bass_kernel_spmd as _run

    nc = _bacc.Bacc("TRN2", target_bir_lowering=False, num_devices=1, dynamic_dma_scratch_size=1024)
    arrays, aps = {}, {}
    for name in _INS:
        x = np.ascontiguousarray(inputs[name])
        arrays[name] = x
        aps[name] = nc.dram_tensor(name, x.shape, mybir.dt.from_np(x.dtype), kind="ExternalInput").ap()
    arrays["const"] = constants()
    aps["const"] = nc.dram_tensor("const", arrays["const"].shape, F32, kind="ExternalInput").ap()
    for name, shape in _OUTS:
        aps[name] = nc.dram_tensor(name, shape, F32, kind="ExternalOutput").ap()
    program(nc, aps)
    r = _run(nc, [arrays], core_ids=[0])
    return tuple(r.results[0][name] for name, _ in _OUTS)
```

```python
import math
from contextlib import ExitStack

import numpy as np
import concourse.bass as bass
from concourse import mybir

F32 = mybir.dt.float32
F32R = mybir.dt.float32r
ALU = mybir.AluOpType
ACT = mybir.ActivationFunctionType

P = 128
D = 2048
KT = D // P
SEQ, NB, NS = 256, 8, 4
SAMP = NB * NS
NT = SAMP + SEQ
NX = NB + NT
HEAD = 64
CHUNK = 64
NCH = SEQ // CHUNK
RW, RA, RGL = 96, 96, 256
DPLE = 256
OFF_R = 2 * D
OFF_K, OFF_V = OFF_R + D, OFF_R + 2 * D
OFF_LOW = OFF_R + 3 * D
OFF_GA = OFF_LOW + RW + RA + RGL
OFF_GB = OFF_GA + D
EPS = 1e-6
GN_EPS = 64e-5

CONV_STATE, H_STATE = 0, 24
(CW, CB, BA, BX, LAM, W0, A0, KK, KA, RK, GNW, GNB, MUR, MUK, MUV, GMIX, GFFN, GPLE, GFIN) = (
    32, 36, 37, 38, 39, 40, 41, 42, 43, 44, 45, 46, 47, 48, 49, 50, 51, 52, 53)
MULOW = 54
NPAR = 58
SP8, NSP8 = 0, 1
NDER = 2

O_SHIFT, O_H, O_CONV = 0, 9, 18
NOUTF = 45

(C_ID, C_BD, C_ONE, C_AM, C_LM, C_SAM, C_SLM, C_SEQ, C_SQT, C_ID2, C_END) = np.cumsum(
    [0, 128, 128, 128, 4 * 64, 6 * 64, 128, 64, 256, 8, 64]).tolist()


def constants():
    c = np.zeros((P, C_END), np.float32)
    i, j = np.arange(P)[:, None], np.arange(P)[None, :]
    c[:, C_ID:C_ID + P] = i == j
    c[:, C_BD:C_BD + P] = i // HEAD == j // HEAD
    c[:, C_ONE:C_ONE + P] = 1 / D

    def half(t, s, m):
        return (t // (2 * m) == s // (2 * m)) & (t % (2 * m) >= m) & (s % (2 * m) < m)

    i, j = i % CHUNK, np.arange(CHUNK)[None, :]
    c[:, C_AM:C_AM + 4 * CHUNK] = np.concatenate([half(j, i, 1), i <= j, i < j, i <= j], 1)
    for l in range(6):
        c[:, C_LM + l * CHUNK:C_LM + (l + 1) * CHUNK] = half(i, j, 2 ** l)
    s, t = np.arange(SAMP)[:, None], np.arange(SAMP)[None, :]
    own = s % NB == t % NB
    c[:SAMP, C_SAM:C_SAM + 128] = np.concatenate(
        [own & half(t // NB, s // NB, 1), own & (s <= t), own & (s < t), own & (s <= t)], 1)
    c[:SAMP, C_SLM:C_SLM + 64] = np.concatenate([own & half(s // NB, t // NB, 1), own & half(s // NB, t // NB, 2)], 1)
    c[:, C_SEQ:C_SEQ + 256] = (np.arange(256)[None, :] // SAMP) == (np.arange(256)[None, :] % NB)
    c[:64, C_SQT:C_SQT + NB] = (np.arange(64)[:, None] % NB) == np.arange(NB)[None, :]
    c[:, C_ID2:C_ID2 + HEAD] = i == j
    return c


PARTS = 8
LOOP_UNITS = 6
SLOTS = PARTS * LOOP_UNITS
U_LOOP = 4
U_GB = U_LOOP + LOOP_UNITS * KT
U_RGO = U_GB + KT
U_RWO = U_RGO + KT
U_WO = U_RWO + KT
U_FFN = U_WO + KT
U_PLE = U_FFN + 8 * KT

STEPS = {"dve_rg": 41, "dve_ch": 43}
ROW_LOADS = 27
N_INIT = 4
FFN_PLAN = (("up", 0), ("up", 1), ("down", 0), ("up", 2), ("down", 1), ("up", 3), ("down", 2), ("down", 3))


HI_AT, LO_AT = (0, 2), (3, 4)
EARLY = {
    9: ["wd"],
    10: ["ad"],
    13: ["kk_sum"],
    15: ["decay"],
    18: ["kk"],
    22: ["cum"],
    28: ["tilde"],
    29: ["early_done"],
}
LATE = {
    0: ["turn", "ar", "rg_gates"],
    2: ["gate", "bonus"],
    4: ["rg_decay"],
    5: ["pairwise"],
    6: ["rg_root"],
    9: ["invert1a"],
    10: ["invert1b", "rg_scan"],
    11: ["state_in"],
    12: ["invert2a"],
    14: ["invert2b"],
    15: ["samp_pair"],
    16: ["invert3a"],
    18: ["invert3b"],
    21: ["samp_inv_a", "invert4a", "samp_inv_b"],
    22: ["invert4b"],
    23: ["samp_r"],
    25: ["invert5a"],
    26: ["samp_u", "invert5b"],
    28: ["samp_out", "r0"],
    30: ["u0"],
    31: ["my0"],
    34: ["r1", "u1"],
    36: ["my1"],
    37: ["r2"],
    39: ["u2"],
    40: ["my2"],
    41: ["r3"],
    42: ["u3"],
    43: ["my3"],
    44: ["fin"],
    45: ["mean"],
    46: ["var"],
}


def program(nc, a):
    ctx = ExitStack()
    with ctx:
        def sb(name, shape, dt=F32, stack=ctx):
            return stack.enter_context(nc.sbuf_tensor(name, shape, dt))

        def sem(name):
            return ctx.enter_context(nc.semaphore(name))

        bank = [ctx.enter_context(nc.psum_tensor(f"bank{k}", [P, 512], F32)) for k in range(8)]

        xh = sb("xh", [P, KT, NX], F32R)
        xl = sb("xl", [P, KT, NX], F32R)
        rga = sb("rga", [P, KT, NX])
        rwo = sb("rwo", [P, KT, NT])
        raw = [sb(f"raw{s}", [P, KT, P]) for s in range(2)]
        wh = [sb(f"wh{s}", [P, KT, P], F32R) for s in range(2)]
        wl = [sb(f"wl{s}", [P, KT, P], F32R) for s in range(2)]
        cst = sb("cst", [P, C_END])
        par = sb("par", [P, KT, NPAR])
        der = sb("der", [P, KT, NDER])
        der_work = sb("der_work", [P, KT, 4])
        outf = sb("outf", [P, KT, NOUTF])
        early_root = sb("early_root", [P, 4])
        sums = sb("sums", [P, NX])

        ident, bd, ones = (cst[:, o:o + P] for o in (C_ID, C_BD, C_ONE))
        samp_all = slice(0, SAMP)

        start = ExitStack()
        with start:
            xtok2 = sb("xtok2", [P, D], F32, start)
        mix = ExitStack()
        with mix:
            def mb(name, shape, dt=F32):
                return sb(name, shape, dt, mix)

            ptu, ptc = mb("ptu", [P, NPAR]), mb("ptc", [P, NPAR])
            dtc, dl = mb("dtc", [P, NDER]), mb("dl", [P, NCH])
            ex = mb("ex", [P, NX])
            zr, zk, zv = mb("zr", [P, NT]), mb("zk", [P, NT]), mb("zv", [P, NT])
            low = mb("low", [P, 4, NT])
            w2s, a2s, g2s = mb("w2s", [P, P]), mb("a2s", [P, P]), mb("g2s", [P, 2, P])
            was, wxs = mb("was", [P, P]), mb("wxs", [P, P])
            ue, xc, gg, gat = mb("ue", [P, 315]), mb("xc", [P, NT]), mb("gg", [P, NT]), mb("gat", [P, NT])
            rgi, th = mb("rgi", [P, NT]), mb("th", [P, NT])
            siga, sigw, gout, kp = (mb(n, [P, NT]) for n in ("siga", "sigw", "gout", "kp"))
            rn, ksq, kkn, bv = (mb(n, [P, NT]) for n in ("rn", "ksq", "kkn", "bv"))
            cum = mb("cum", [P, 5 * NB + NCH * (CHUNK + 1)])
            zeros = mb("zeros", [P, CHUNK])
            ar, btl, ktl = mb("ar", [P, 2, NT]), mb("btl", [P, NT]), mb("ktl", [P, NT])
            bkh, vv = mb("bkh", [P, 2 * SAMP]), mb("vv", [P, 2 * SAMP])
            tmb, tmv = mb("tmb", [P, 4, P]), mb("tmv", [P, 2, P])
            sbk, svv, suv = mb("sbk", [2 * SAMP, P]), mb("svv", [2 * SAMP, P]), mb("suv", [2 * SAMP, P])
            both = mb("both", [P, 9 * 4 * CHUNK])
            ams = both[:, 0:16 * CHUNK].rearrange("p (q t) -> p q t", q=4)
            am = both[:, 16 * CHUNK:].rearrange("p (l q t) -> p l q t", l=5, q=4)
            ab, yy = mb("ab", [P, 4, CHUNK]), mb("yy", [P, 4, CHUNK])
            inv = mb("inv", [P, 8 * CHUNK])
            tt, tn = (inv[:, k * 256:(k + 1) * 256].rearrange("p (q t) -> p q t", q=4) for k in range(2))
            sam = mb("sam", [SAMP, 2, 128])
            sa2, stn, stt_s, syy = (mb(n, [SAMP, 2, SAMP]) for n in ("sa2", "stn", "stt_s", "syy"))
            s0, ms = mb("s0", [P, NB, P]), mb("ms", [P, NB, P])
            aex, bke = mb("aex", [P, NB, SAMP]), mb("bke", [2 * SAMP, 2, 512])
            dg = mb("dg", [P, NB, HEAD + NS])
            so = dg[:, :, 0:HEAD]
            rs, us, sr = mb("rs", [P, P]), mb("us", [P, P]), mb("sr", [SAMP, P])
            mp, mtmp = [mb(f"mp{k}", [P, P]) for k in range(2)], mb("mtmp", [P, P])
            sfin = mtmp
            yf, yc, ysq, sd = (mb(n, [P, NT]) for n in ("yf", "yc", "ysq", "sd"))
            dif, rgr, m2 = sd, yf, ysq
            rows = both[:, 0:D]

        ffn = ExitStack()
        with ffn:
            sbh = [sb(f"sbh{k}", [P, KT, NT], F32R, ffn) for k in range(2)]
            sbl = [sb(f"sbl{k}", [P, KT, NT], F32R, ffn) for k in range(2)]
            tmp = [sb(f"tmp{k}", [P, NT], F32, ffn) for k in range(2)]
            nsq = [sb(f"nsq{k}", [P, 2, NX], F32, ffn) for k in range(2)]
            nrm = [sb(f"nrm{k}", [P, 2, NX], F32, ffn) for k in range(2)]
            acc, mean_sq = nsq[0][:, 1, 0:NT], nsq[1][:, 1, :]
            gt = [t[:, 0, 0:NT] for t in nsq]
        fin = ExitStack()
        with fin:
            wcol = [sb(f"wcol{k}", [P, 2, P], F32, fin) for k in range(2)]
            ptok, pt = sb("ptok", [P, 3, DPLE], F32, fin), sb("pt", [P, 2, NT], F32, fin)
            small_out = sb("small_out", [NOUTF, D], F32, fin)
            ytok = sb("ytok", [P, 3, D], F32, fin)
        xtok = rwo[:, :, :].rearrange("p k t -> p (k t)")[:, 0:2 * D].rearrange("p (u d) -> p u d", u=2)

        xt_dram = nc.dram_tensor("xt_scratch", [P, KT, NX], F32).ap()
        ga_dram = nc.dram_tensor("ga_scratch", [KT, P, NT], F32).ap()
        gb_dram = nc.dram_tensor("gb_scratch", [KT, P, NT], F32).ap()

        def sems(names):
            return [sem(name) for name in names.split()]

        raw_in = sems("raw_in0 raw_in1")
        half_done, hi_done, lo_done, unit_done = sems("half_done hi_done lo_done unit_done")
        cst_in, rows_zero, rows_in, xs_in, xp_in, xp2_in = sems("cst_in rows_zero rows_in xs_in xp_in xp2_in")
        xt_mm, par_mm, par_ready, xt_act, xt_dve, xt_saved = sems("xt_mm par_mm par_ready xt_act xt_dve xt_saved")
        sq_ready, sq_done, acc_ready, sum_mm = sems("sq_ready sq_done acc_ready sum_mm")
        rms_var, rms_std, rms_inv, nrm_ready, nrm_hi, nrm_lo = sems("rms_var rms_std rms_inv nrm_ready nrm_hi nrm_lo")
        der_step, init_done, lam_abs, lam_exp = sems("der_step init_done lam_abs lam_exp")
        low_ex, low_mix, low_ready = sems("low_ex low_mix low_ready")
        ex_ready, mixed, ue_ready, conv_ready, gelu_ready = sems("ex_ready mixed ue_ready conv_ready gelu_ready")
        ga_ready, ga_saved, gb_ready = sems("ga_ready ga_saved gb_ready")
        gb_saved = sems("gb_saved0 gb_saved1")
        early_in, low_mm, sig_ready, decay_ready, ksq_ready = sems("early_in low_mm sig_ready decay_ready ksq_ready")
        kk_mm, ss_ready, kk_root, early_end = sems("kk_mm ss_ready kk_root early_end")
        small_in, rgr_mm, rgr_sig, rgi_mm, rgi_sig, rg_exp, th_ready, m2_ready, m_root, rga_ready = sems(
            "small_in rgr_mm rgr_sig rgi_mm rgi_sig rg_exp th_ready m2_ready m_root rga_ready")
        ptc_ready, turn_mm, turn_read, ar_ready = sems("ptc_ready turn_mm turn_read ar_ready")
        gout_mm, gout_read, bt_ready, bonus_mm, bonus_read = sems("gout_mm gout_read bt_ready bonus_mm bonus_read")
        pair_mm, pair_read, ab_read, am_ready, yy_mm, tn_mm = sems("pair_mm pair_read ab_read am_ready yy_mm tn_mm")
        yy_read = sems("yy_read1 yy_read2 yy_read3 yy_read4 yy_read5")
        tn_ready = sems("tn_ready0 tn_ready1 tn_ready2 tn_ready3 tn_ready4 tn_ready5")
        s0_in, state_mm, state_read, spair_mm, sinv_ready = sems("s0_in state_mm state_read spair_mm sinv_ready")
        syy_mm, syy_read, stt_mm, stt_ready, sexp_ready = sems("syy_mm syy_read stt_mm stt_ready sexp_ready")
        sr_mm, sr_read, su_mm, su_read, so_mm, so_ready, so_saved = sems("sr_mm sr_read su_mm su_read so_mm so_ready so_saved")
        r_mm, u_mm, u_read, m_mm, y_mm, m_ready = sems("r_mm u_mm u_read m_mm y_mm m_ready")
        r_read = sems("r_read0 r_read1 r_read2 r_read3")
        fin_mm, fin_read, fin_saved = sems("fin_mm fin_read fin_saved")
        yf_ready, mean_mm, yc_ready, ysq_ready, var_mm, var_ready, y_root, rwo_ready = sems(
            "yf_ready mean_mm yc_ready ysq_ready var_mm var_ready y_root rwo_ready")
        dve_rg, dve_ch = sems("dve_rg dve_ch")
        split_hi, split_lo, gated, merged, merged_hi, merged_lo = sems("split_hi split_lo gated merged merged_hi merged_lo")
        g_in, x_back, x_done = sems("g_in0 g_in1"), *sems("x_back x_done")
        h_relu, h_sq, h_hi, h_lo = sems("h_relu h_sq h_hi h_lo")
        ple_in, pt_mm, pt_ready, sg_ready, embed_mm, tmp_ready = sems("ple_in pt_mm pt_ready sg_ready embed_mm tmp_ready")
        wcol_in = sems("wcol_in0 wcol_in1")
        small_mm, small_read, y_turn, y_read, stored = sems("small_mm small_read y_turn y_read stored")

        block = ctx.enter_context(nc.Block())

        class Count:

            def __init__(self, sem, step, per_step):
                self.sem, self.n = sem, 0
                self.base, self.per_step = step * per_step if per_step else 0, per_step

            def one(self):
                self.n += 1
                return 1

            def so_far(self):
                return self.base + self.n

            def end(self):
                assert self.n == self.per_step, self.n

        def cum_of(which):
            o = 0 if which == "before" else 1
            samples = cum[:, o * NB:o * NB + SAMP]
            prompt = cum[:, 5 * NB:].rearrange("p (c t) -> p c t", c=NCH)[:, :, o:o + CHUNK]
            return samples, prompt

        def sample_out(k):
            return bank[3 - k][:, 0:4 * (HEAD + NS)].rearrange("p (b j) -> p b j", b=4)

        def last_decay(c):
            col = 5 * NB + c * (CHUNK + 1) + CHUNK
            return cum[:, col:col + 1]

        def chunks(ap):
            return ap[:, SAMP:NT].rearrange("p (c t) -> p c t", c=NCH)

        def unit_columns(u, it):
            return [OFF_K, OFF_R, OFF_V, 0, D, OFF_GA][u] + it * P

        @block.sync
        def _(sp):
            def load_unit(src, slot, n=None):
                if n is not None:
                    sp.wait_ge(cst_in, 16)
                    sp.wait_ge(lo_done, n - 1)
                sp.dma_start(raw[slot][:], src.rearrange("(k p) c -> p k c", p=P)).then_inc(raw_in[slot], 16)

            def in_columns(start):
                return a["w_in"][0, :, bass.ds(start, P)]

            sp.dma_start(cst[:], a["const"]).then_inc(cst_in, 16)
            sp.dma_start(xtok[0:NB, 0, :], a["state_shift"][0]).then_inc(xs_in, 16)
            for t in range(NS):
                sp.dma_start(xtok[NB + t * NB:2 * NB + t * NB, 0, :], a["x_sample"][:, t, :]).then_inc(xs_in, 16)
            sp.dma_start(xtok[:, 1, :], a["x_prompt"][0, 0:P, :]).then_inc(xp_in, 16)
            sp.dma_start(xtok2[:, :], a["x_prompt"][0, P:SEQ, :]).then_inc(xp2_in, 16)
            low_start = (OFF_LOW, OFF_LOW + RW, OFF_LOW + RW + RA, OFF_LOW + RW + RA + P)
            for u in range(2):
                load_unit(in_columns(low_start[u]), u)
            sp.wait_ge(rows_zero, 1)
            n_rows = 0
            for j in range(3):
                sp.dma_start(rows[j * NB:j * NB + NB, :], a["state_rg_conv"][0, :, j, :]).then_inc(rows_in, 16)
            sp.dma_start(rows[H_STATE:H_STATE + NB, :], a["state_rg_h"][0]).then_inc(rows_in, 16)
            sp.dma_start(rows[CW:CW + 4, :], a["conv_w"][0]).then_inc(rows_in, 16)
            n_rows = 5
            mu = a["mu_shift"][0]
            for row, src in ((CB, a["conv_b"][0]), (BA, a["rg_ba"][0]), (BX, a["rg_bx"][0]), (LAM, a["rg_lam"][0]),
                             (W0, a["rw_w0"][0]), (A0, a["rw_a0"][0]), (KK, a["rw_kk"][0]), (KA, a["rw_ka"][0]),
                             (RK, a["rw_rk"][0]), (GNW, a["rw_gn_w"][0]), (GNB, a["rw_gn_b"][0]),
                             (MUR, mu[0:D]), (MUK, mu[D:2 * D]), (MUV, mu[2 * D:3 * D]),
                             (GMIX, a["norm_mix"][0]), (GFFN, a["norm_ffn"][0]), (GPLE, a["norm_ple"][0]),
                             (GFIN, a["norm_f"])):
                src = src.rearrange("a b -> (a b)") if len(src.shape) == 2 else src
                sp.dma_start(rows[row:row + 1, :], src.rearrange("(o d) -> o d", o=1)).then_inc(rows_in, 16)
                n_rows += 1
            for k, (o, w) in enumerate(((3 * D, RW), (3 * D + RW, RA), (3 * D + RW + RA, P), (3 * D + RW + RA + P, P))):
                sp.dma_start(rows[MULOW + k:MULOW + k + 1, 0:w],
                             mu[o:o + w].rearrange("(o d) -> o d", o=1)).then_inc(rows_in, 16)
                n_rows += 1
            assert n_rows == ROW_LOADS
            sp.wait_ge(xt_dve, 6)
            sp.wait_ge(xt_act, 4)
            sp.dma_start(xt_dram, rga[:]).then_inc(xt_saved, 16)

            def small_early(it):
                cols = bass.ds(it * P, P)
                sp.dma_start(w2s[0:RW, :], a["rw_w2"][0, :, cols]).then_inc(early_in, 16)
                sp.dma_start(a2s[0:RA, :], a["rw_a2"][0, :, cols]).then_inc(early_in, 16)

            def small(it, again):
                if again:
                    sp.wait_ge(cst_in, 16)
                    sp.wait_ge(bonus_mm, it)
                cols = bass.ds(it * P, P)
                sp.dma_start(g2s[:], a["rw_g2"][0, :, cols].rearrange("(k p) c -> p k c", p=P)).then_inc(small_in, 16)
                sp.dma_start(was[:], a["rg_wa"][0, bass.ds(it, 1)].rearrange("o c d -> (o c) d")).then_inc(small_in, 16)
                sp.dma_start(wxs[:], a["rg_wx"][0, bass.ds(it, 1)].rearrange("o c d -> (o c) d")).then_inc(small_in, 16)
                if again:
                    sp.wait_ge(cst_in, 16)
                    sp.wait_ge(state_mm, it)
                else:
                    sp.wait_ge(init_done, N_INIT)
                for h in range(2):
                    sp.dma_start(s0[h * HEAD:(h + 1) * HEAD, :, h * HEAD:(h + 1) * HEAD],
                                 a["state_rwkv"][0, :, bass.ds(2 * it + h, 1)].rearrange("b o i j -> (o i) b j")
                                 ).then_inc(s0_in, 16)

            def states_out(p):
                sp.wait_ge(cst_in, 16)
                sp.wait_ge(so_ready, p + 1)
                sp.dma_start(a["o_rwkv_s"][0, :, bass.ds(2 * p, 2)].rearrange("b h i j -> (h i) b j"), so
                             ).then_inc(so_saved, 16)
                sp.wait_ge(cst_in, 16)
                sp.wait_ge(fin_read, p + 1)
                for h in range(2):
                    sp.dma_start(a["o_rwkv_p"][0, 0, bass.ds(2 * p + h, 1)].rearrange("o i j -> (o i) j"),
                                 sfin[h * HEAD:(h + 1) * HEAD, h * HEAD:(h + 1) * HEAD]).then_inc(fin_saved, 16)

            def step(it, last, chain):
                for u in range(LOOP_UNITS):
                    n = U_LOOP + it * LOOP_UNITS + u + 3
                    if u < 3:
                        load_unit(in_columns(unit_columns(u + 3, it)), (u + 3) % 2, n)
                    elif not last:
                        load_unit(in_columns(unit_columns(u - 3, it + 1)), (u + 3) % 2, n)
                    else:
                        load_unit(in_columns(OFF_GB + (u - 3) * P), (u + 3) % 2, n)
                    if chain and u == 1:
                        sp.wait_ge(cst_in, 16)
                        sp.wait_ge(ga_ready, it)
                        sp.dma_start(ga_dram[bass.ds(it - 1, 1)].rearrange("o p t -> (o p) t"), gat[:]).then_inc(ga_saved, 16)
                    if u == 3 and not last:
                        sp.wait_ge(cst_in, 16)
                        sp.wait_ge(kk_mm, it + 1)
                        small_early(it + 1)
                    if u == 4:
                        small(it, chain)
                if chain:
                    states_out(it - 1)

            for u in (2, 3):
                load_unit(in_columns(low_start[u]), u % 2, u)
            small_early(0)
            for u in range(3):
                load_unit(in_columns(unit_columns(u, 0)), u % 2, U_LOOP + u)
            step(0, False, False)
            with sp.Fori(1, KT - 1) as it:
                step(it, False, True)
            step(KT - 1, True, True)
            for u in range(LOOP_UNITS):
                load_unit(in_columns(OFF_GB + (u + 3) * P), (u + 3) % 2, U_GB + u + 3)
                if u == 0:
                    sp.wait_ge(ga_ready, KT)
                    sp.dma_start(ga_dram[KT - 1], gat[:]).then_inc(ga_saved, 16)
                else:
                    sp.wait_ge(gb_ready, u)
                    sp.dma_start(gb_dram[u - 1], gat[:]).then_inc(gb_saved[(u - 1) % 2], 16)
            states_out(KT - 1)

            def phase(base, src, following, extra=None, start=0, end=None):
                with sp.Fori(start // 2, (KT - 4) // 2) as i:
                    for u in range(2):
                        k = 2 * i + u
                        load_unit(src(k + 3), (u + 1) % 2, base + k + 3)
                        if extra:
                            extra(k, u, i)
                for k in range(KT - 4, KT):
                    if k + 3 < KT:
                        load_unit(src(k + 3), (k + 1) % 2, base + k + 3)
                    elif following:
                        load_unit(following(k + 3 - KT), (k + 1) % 2, base + k + 3)
                    if extra:
                        extra(k, k % 2, k // 2)
                    if end and k == KT - 3:
                        end()

            def columns(name, k0=None):
                w = a[name][0] if k0 is None else a[name][0, k0:k0 + D, :]
                return lambda k: w[:, bass.ds(k * P, P)]

            def up(g):
                return lambda k: a["w_up"][0, :, bass.ds(g * D + k * P, P)]

            sp.wait_ge(gb_ready, 6)
            sp.dma_start(gb_dram[5], gat[:]).then_inc(gb_saved[1], 16)

            def gb_store(k, u, i):
                sp.wait_ge(cst_in, 16)
                sp.wait_ge(gb_ready, k + 1)
                sp.dma_start(gb_dram[bass.ds(k, 1)].rearrange("o p t -> (o p) t"), tmp[u][:]).then_inc(gb_saved[u], 16)

            phase(U_GB, lambda k: in_columns(OFF_GB + k * P), columns("w_rg_o"), gb_store, start=6)

            def gate_load(dram, first, k, u, free=True):
                if free:
                    sp.wait_ge(cst_in, 16)
                    sp.wait_ge(merged, first + k - 1)
                sp.dma_start(gt[u][:], dram[bass.ds(k, 1)].rearrange("o p t -> (o p) t")).then_inc(g_in[u], 16)

            sp.wait_ge(ga_saved, 16 * KT)
            sp.wait_ge(gb_saved[0], 8 * KT)
            sp.wait_ge(gb_saved[1], 8 * KT)

            def x_again():
                sp.wait_ge(split_lo, 8)
                sp.dma_start(rga[:], xt_dram).then_inc(x_back, 16)

            def ga_next(k, u, i):
                if isinstance(k, int) and k == KT - 1:
                    gate_load(gb_dram, KT, 0, 0)
                else:
                    gate_load(ga_dram, 0, k + 1, 1 - u)

            def gb_next(k, u, i):
                if not (isinstance(k, int) and k == KT - 1):
                    gate_load(gb_dram, KT, k + 1, 1 - u)

            for u in range(2):
                load_unit(a["w_rg_o"][0, :, (u + 3) * P:(u + 4) * P], (u + 1) % 2, U_RGO + u + 3)
                if u == 0:
                    gate_load(ga_dram, 0, 0, 0, False)
                    gate_load(ga_dram, 0, 1, 1, False)
                else:
                    ga_next(1, 1, 0)
            phase(U_RGO, columns("w_rg_o"), columns("w_rw_o"), ga_next, start=2, end=x_again)
            phase(U_RWO, columns("w_rw_o"), columns("w_o"), gb_next)
            phase(U_WO, columns("w_o"), up(0))
            srcs = [up(g) if kind == "up" else columns("w_down", g * D) for kind, g in FFN_PLAN] + [columns("w_ple_gate")]

            def ple_loads():
                sp.wait_ge(cst_in, 16)
                sp.wait_ge(unit_done, U_FFN + 7 * KT)
                for t in range(NS):
                    sp.dma_start(ptok[t * NB:t * NB + NB, 0, :], a["p_sample"][0, :, t, :]).then_inc(ple_in, 16)
                sp.dma_start(ptok[:, 1:3, :], a["p_prompt"][0, 0].rearrange("(u p) c -> p u c", p=P)).then_inc(ple_in, 16)

            for f in range(8):
                phase(U_FFN + f * KT, srcs[f], srcs[f + 1], end=ple_loads if f == 7 else None)

            def col_load(k, u, free=True):
                if free:
                    sp.wait_ge(cst_in, 16)
                    sp.wait_ge(embed_mm, k - 1)
                sp.dma_start(wcol[u][:], a["w_ple"][0, :, bass.ds(k * P, P)].rearrange("(k p) c -> p k c", p=P)
                             ).then_inc(wcol_in[u], 16)

            def col_next(k, u, i):
                if not (isinstance(k, int) and k == KT - 1):
                    col_load(k + 1, 1 - u)

            for u in range(2):
                load_unit(srcs[8](u + 3), (u + 1) % 2, U_PLE + u + 3)
                if u == 0:
                    col_load(0, 0, False)
                    col_load(1, 1, False)
                else:
                    col_next(1, 1, 0)
            phase(U_PLE, srcs[8], None, col_next, start=2)

            sp.wait_ge(small_read, 4)
            for dst, row, n in ((a["o_shift_p"][0], O_SHIFT, 1), (a["o_shift_s"][0], O_SHIFT + 1, NB),
                                (a["o_h_p"][0], O_H, 1), (a["o_h_s"][0], O_H + 1, NB),
                                (a["o_conv_p"][0, 0], O_CONV, 3),
                                (a["o_conv_s"][0, :, 0, :], O_CONV + 3, NB), (a["o_conv_s"][0, :, 1, :], O_CONV + 3 + NB, NB),
                                (a["o_conv_s"][0, :, 2, :], O_CONV + 3 + 2 * NB, NB)):
                sp.dma_start(dst, small_out[row:row + n, :]).then_inc(stored, 16)
            sp.wait_ge(y_read, 3 * 8)
            for t in range(NS):
                sp.dma_start(a["o_y_s"][:, t, :], ytok[t * NB:t * NB + NB, 0, :]).then_inc(stored, 16)
            sp.dma_start(a["o_y_p"][0].rearrange("(u p) d -> p u d", p=P), ytok[:, 1:3, :]).then_inc(stored, 16)
            sp.wait_ge(stored, 16 * 13)
            sp.wait_ge(so_saved, 16 * KT)
            sp.wait_ge(fin_saved, 32 * KT)
            sp.wait_ge(xt_saved, 16)

        @block.tensor
        def _(pe):
            def mm(out, lhsT, rhs, start, stop):
                return pe.matmul(out, lhsT, rhs, start=start, stop=stop, skip_group_check=True)

            def apart(value):
                if not isinstance(value, int):
                    value = pe.snap(value)
                    pe.wait_ge(cst_in, 16)
                return value

            def unit_part(slot, hi, lo, first, last, q, parts=PARTS):
                out = bank[slot][:, 0:last - first]
                for kt in range(KT // parts * q, KT // parts * (q + 1)):
                    x1, x2 = hi[:, kt, first:last], lo[:, kt, first:last]
                    mm(out, wh[slot][:, kt, :], x1, kt == 0, False)
                    mm(out, wh[slot][:, kt, :], x2, False, False)
                    done = mm(out, wl[slot][:, kt, :], x1, False, kt == KT - 1)
                if q == parts - 1:
                    done.then_inc(unit_done, 1)

            def unit_ready(n, read, count):
                pe.wait_ge(lo_done, n + 1)
                if read:
                    pe.wait_ge(read, count)

            def turn(out, in_):
                return pe.transpose(out, in_, ident)

            pe.wait_ge(cst_in, 16)
            pe.wait_ge(xs_in, 16 * 5)
            for b in range(2):
                for k in range(8):
                    done = pe.transpose(bank[b][:, k * 40:(k + 1) * 40], xtok[0:40, 0, (b * 8 + k) * P:(b * 8 + k + 1) * P], cst[0:40, C_ID:C_ID + 40])
                done.then_inc(xt_mm, 1)
            pe.wait_ge(xp_in, 16)
            for b in range(4):
                for k in range(4):
                    done = turn(bank[2 + b][:, k * P:(k + 1) * P], xtok[:, 1, (b * 4 + k) * P:(b * 4 + k + 1) * P])
                done.then_inc(xt_mm, 1)
            pe.wait_ge(xp2_in, 16)
            for b, to in enumerate((6, 7, 0, 1)):
                if to < 2:
                    pe.wait_ge(xt_dve, to + 1)
                for k in range(4):
                    done = turn(bank[to][:, k * P:(k + 1) * P], xtok2[:, (b * 4 + k) * P:(b * 4 + k + 1) * P])
                done.then_inc(xt_mm, 1)

            pe.wait_ge(xt_dve, 4)
            for j in range(8):
                pe.wait_ge(sq_ready, j + 1)
                for h in range(2):
                    done = mm(bank[7][:, 0:NX], ones, nsq[j % 2][:, h, 0:NX], j == 0 and h == 0, j == 7 and h == 1)
                done.then_inc(sum_mm, 1)
            pe.wait_ge(rows_in, 16 * ROW_LOADS)
            for b in range(2):
                pe.wait_ge(xt_act, b + 1)
                for k in range(8):
                    cols = slice((b * 8 + k) * P, (b * 8 + k + 1) * P)
                    done = pe.transpose(bank[2 + b][:, k * NPAR:(k + 1) * NPAR], rows[0:NPAR, cols], cst[0:NPAR, C_ID:C_ID + NPAR])
                done.then_inc(par_mm, 1)

            def norm(k):
                pe.wait_ge(acc_ready, k * KT)
                mm(bank[7][:, 0:NT], ones, acc, True, True).then_inc(sum_mm, 1)

            for n in range(4):
                unit_ready(n, low_ex if n > 1 else None, n - 1)
                for q in range(PARTS if n == 0 else 1):
                    if n == 0:
                        pe.wait_ge(nrm_lo, q + 1)
                    unit_part(n % 2, xh, xl, 0, NX, q, PARTS if n == 0 else 1)

            def early(name, it):
                one = it + 1
                if name == "wd":
                    pe.wait_ge(early_in, 32 * one)
                    if isinstance(it, int) and it == 0:
                        pe.wait_ge(low_ready, 3)
                    else:
                        pe.wait_ge(rgr_sig, it)
                    mm(bank[7][:, 0:NT], w2s[0:RW, :], low[0:RW, 0, :], True, True).then_inc(low_mm, 1)
                elif name == "ad":
                    pe.wait_ge(sig_ready, 2 * it + 1)
                    mm(bank[7][:, 0:NT], a2s[0:RA, :], low[0:RA, 1, :], True, True).then_inc(low_mm, 1)
                elif name == "kk_sum":
                    pe.wait_ge(sig_ready, 2 * it + 2)
                    pe.wait_ge(ksq_ready, one)
                    mm(bank[7][:, 0:NT], bd, ksq[:], True, True).then_inc(kk_mm, 1)

            def stage(name, p, last):
                one = p + 1
                if name == "rg_gates":
                    pe.wait_ge(small_in, 48 * one)
                    pe.wait_ge(conv_ready, one)
                    if not (isinstance(p, int) and p == 0):
                        pe.wait_ge(yf_ready, p)
                    mm(bank[7][:, 0:NT], was[:], xc[:], True, True).then_inc(rgr_mm, 1)
                    mm(bank[6][:, 0:NT], wxs[:], xc[:], True, True).then_inc(rgi_mm, 1)
                elif name == "gate":
                    mm(bank[4][:, 0:NT], g2s[:, 0, :], low[:, 2, :], True, False)
                    mm(bank[4][:, 0:NT], g2s[:, 1, :], low[:, 3, :], False, True).then_inc(gout_mm, 1)
                elif name == "bonus":
                    pe.wait_ge(bt_ready, one)
                    mm(bank[5][:, 0:NT], bd, bv[:], True, True).then_inc(bonus_mm, 1)
                elif name == "turn":
                    pe.wait_ge(early_end, one)
                    if not (isinstance(p, int) and p == 0):
                        pe.wait_ge(fin_read, p)
                    for k, src in enumerate((btl, ktl)):
                        for g in range(2):
                            turn(bank[2][:, (2 * k + g) * P:(2 * k + g + 1) * P], src[:, SAMP + g * P:SAMP + (g + 1) * P])
                    for g in range(2):
                        turn(bank[3][:, g * P:(g + 1) * P], zv[:, SAMP + g * P:SAMP + (g + 1) * P])
                    turn(bank[3][0:2 * SAMP, 256:384], bkh[:])
                    turn(bank[3][0:2 * SAMP, 384:512], vv[:]).then_inc(turn_mm, 1)
                elif name == "pairwise":
                    count = apart(one)
                    pe.wait_ge(ar_ready, count)
                    pe.wait_ge(bonus_read, count)
                    pe.wait_ge(gout_read, count)
                    pe.wait_ge(rgi_sig, count)
                    for part, src in enumerate((btl, ktl)):
                        for g in range(2):
                            for c in (2 * g, 2 * g + 1):
                                cols, rc = slice(SAMP + c * CHUNK, SAMP + (c + 1) * CHUNK), slice((c % 2) * CHUNK, (c % 2 + 1) * CHUNK)
                                for h in range(2):
                                    rows_h, o = slice(h * HEAD, (h + 1) * HEAD), g * 256 + part * 128
                                    done = mm(bank[4 + h][rc, o:o + 128], src[rows_h, cols], ar[rows_h, :, cols], True, True)
                                    if part and c == NCH - 1:
                                        done.then_inc(pair_mm, 1)
                    count = apart(one)
                    pe.wait_ge(turn_read, count)
                    for c in range(NCH):
                        cols, rc = slice(SAMP + c * CHUNK, SAMP + (c + 1) * CHUNK), slice((c % 2) * CHUNK, (c % 2 + 1) * CHUNK)
                        for h in range(2):
                            rows_h, o = slice(h * HEAD, (h + 1) * HEAD), c // 2 * CHUNK
                            done = mm(bank[2 + h][rc, o:o + CHUNK], ar[rows_h, 0, cols], btl[rows_h, cols], True, True)
                    done.then_inc(pair_mm, 1)
                elif name[:6] == "invert":
                    l, part, count = int(name[6]), name[7], apart(one)
                    halves = [(q, bank[5 + c], slice(c * CHUNK, (c + 1) * CHUNK)) for q in range(4) for c in range(2)]
                    if part == "a":
                        pe.wait_ge(tn_ready[l - 1], count)
                        if l == 1:
                            pe.wait_ge(am_ready, count)
                        for q, out, rc in halves:
                            done = mm(out[rc, q * CHUNK:(q + 1) * CHUNK], am[rc, l - 1, q, :], tt[rc, q, :], True, True)
                        done.then_inc(yy_mm, 1)
                    else:
                        pe.wait_ge(yy_read[l - 1], count)
                        for q, out, rc in halves:
                            done = mm(out[rc, q * CHUNK:(q + 1) * CHUNK], tn[rc, q, :], yy[rc, q, :], True, True)
                        if l < 5:
                            for q, out, rc in halves:
                                o = 256 + q * CHUNK
                                done = mm(out[rc, o:o + CHUNK], yy[rc, q, :], tn[rc, q, :], True, True)
                        done.then_inc(tn_mm, 1)
                elif name == "state_in":
                    pe.wait_ge(s0_in, 32 * one)
                    pe.wait_ge(ab_read, 2 * one)
                    for b in range(NB):
                        done = turn(bank[2 + b // 4][:, (b % 4) * P:(b % 4 + 1) * P], s0[:, b, :])
                    done.then_inc(state_mm, 1)
                elif name == "samp_pair":
                    count = apart(2 * one)
                    pe.wait_ge(state_read, count)
                    for h in range(2):
                        rows_h = slice(h * HEAD, (h + 1) * HEAD)
                        out = bank[2 + h]
                        mm(out[0:SAMP, 0:64], btl[rows_h, 0:SAMP], ar[rows_h, :, 0:SAMP], True, True)
                        mm(out[0:SAMP, 64:128], ktl[rows_h, 0:SAMP], ar[rows_h, :, 0:SAMP], True, True)
                        done = mm(out[0:SAMP, 128:160], ar[rows_h, 0, 0:SAMP], btl[rows_h, 0:SAMP], True, True)
                    done.then_inc(spair_mm, 1)
                elif name == "samp_inv_a":
                    count = apart(one)
                    pe.wait_ge(sinv_ready, count)
                    for h in range(2):
                        done = mm(bank[2][0:SAMP, h * SAMP:(h + 1) * SAMP], sa2[:, h, :], stt_s[:, h, :], True, True)
                    done.then_inc(syy_mm, 1)
                elif name == "samp_inv_b":
                    count = apart(one)
                    pe.wait_ge(syy_read, count)
                    for h in range(2):
                        done = mm(bank[3][0:SAMP, h * SAMP:(h + 1) * SAMP], stn[:, h, :], syy[:, h, :], True, True)
                    done.then_inc(stt_mm, 1)
                elif name == "samp_r":
                    pe.wait_ge(sexp_ready, one)
                    for b in range(NB):
                        mm(bank[2][0:SAMP, 0:P], aex[:, b, :], ms[:, b, :], b == 0, False)
                    for h in range(2):
                        done = mm(bank[2][0:SAMP, h * HEAD:(h + 1) * HEAD], sam[:, h, 64:96], svv[0:SAMP, h * HEAD:(h + 1) * HEAD], False, True)
                    done.then_inc(sr_mm, 1)
                elif name == "samp_u":
                    count = apart(one)
                    pe.wait_ge(sr_read, count)
                    pe.wait_ge(stt_ready, one)
                    for h in range(2):
                        done = mm(bank[3][0:SAMP, h * HEAD:(h + 1) * HEAD], stt_s[:, h, :], sr[:, h * HEAD:(h + 1) * HEAD], True, True)
                    done.then_inc(su_mm, 1)
                elif name == "samp_out":
                    count = apart(one)
                    pe.wait_ge(su_read, count)
                    for b in range(NB):
                        mm(sample_out(b // 4)[:, b % 4, :], ms[:, b, :], dg[:, b, :], b % 4 == 0, False)
                    for k in range(2):
                        out, own = sample_out(k), slice(4 * k, 4 * k + 4)
                        for h in range(2):
                            hc = slice(h * HEAD, (h + 1) * HEAD)
                            for o, x in ((32, suv), (96, svv)):
                                by_seq = sam[:, h, o:o + SAMP].rearrange("s (t b) -> s b t", b=NB)
                                mm(out[hc, :, HEAD:], x[0:SAMP, hc], by_seq[:, own, :], False, False)
                            done = mm(out[hc, :, 0:HEAD], suv[:, hc], bke[:, h, :].rearrange("p (b j) -> p b j", b=NB)[:, own, :], False, True)
                    done.then_inc(so_mm, 1)
                elif name[0] == "r" and name[1:].isdigit():
                    c = int(name[1:])
                    g, rc = c // 2, slice((c % 2) * CHUNK, (c % 2 + 1) * CHUNK)
                    if c == 0:
                        count = apart(one)
                        pe.wait_ge(tn_ready[5], count)
                    else:
                        count = apart(NCH * p + c)
                        pe.wait_ge(m_ready, count)
                        mm(bank[4][rc, 0:P], ar[:, 0, SAMP + c * CHUNK:SAMP + (c + 1) * CHUNK], mp[c % 2][:], True, False)
                    for h in range(2):
                        hc = slice(h * HEAD, (h + 1) * HEAD)
                        done = mm(bank[4][rc, hc], ams[rc, 2 * h + g, 128:192], tmv[rc, g, hc], c == 0, True)
                    done.then_inc(r_mm, 1)
                elif name[0] == "u":
                    c = int(name[1:])
                    g, rc = c // 2, slice((c % 2) * CHUNK, (c % 2 + 1) * CHUNK)
                    count = apart(one)
                    pe.wait_ge(r_read[c], count)
                    for h in range(2):
                        hc = slice(h * HEAD, (h + 1) * HEAD)
                        done = mm(bank[5][rc, hc], tt[rc, 2 * h + g, :], rs[rc, hc], True, True)
                    done.then_inc(u_mm, 1)
                elif name[:2] == "my":
                    c = int(name[2:])
                    g, rc = c // 2, slice((c % 2) * CHUNK, (c % 2 + 1) * CHUNK)
                    ycols = slice(SAMP + c * CHUNK, SAMP + (c + 1) * CHUNK)
                    if c == 0 and not last:
                        pe.wait_ge(ss_ready, p + 2)
                    count = apart(NCH * p + c + 1)
                    pe.wait_ge(u_read, count)
                    mm(bank[6][:, 0:P], tmb[rc, g, :], us[rc, :], True, False)
                    mm(bank[6][:, 0:P], tmb[rc, 2 + g, :], tmv[rc, g, :], False, True).then_inc(m_mm, 1)
                    if c:
                        mm(bank[7][:, ycols], mp[c % 2][:], ar[:, 1, ycols], True, False)
                    for h in range(2):
                        hc = slice(h * HEAD, (h + 1) * HEAD)
                        mm(bank[7][hc, ycols], us[rc, hc], ams[rc, 2 * h + g, 64:128], c == 0, False)
                        done = mm(bank[7][hc, ycols], tmv[rc, g, hc], ams[rc, 2 * h + g, 192:256], False, True)
                    done.then_inc(y_mm, 1)
                elif name == "fin":
                    pe.wait_ge(m_ready, NCH * one)
                    pe.wait_ge(so_ready, one)
                    turn(bank[2][:, 0:P], mp[NCH % 2][:]).then_inc(fin_mm, 1)
                elif name == "mean":
                    pe.wait_ge(yf_ready, one)
                    mm(bank[4][:, 0:NT], bd, yf[:], True, True).then_inc(mean_mm, 1)
                elif name == "var":
                    pe.wait_ge(ysq_ready, one)
                    mm(bank[5][:, 0:NT], bd, ysq[:], True, True).then_inc(var_mm, 1)

            def step(it, units, chain):
                for slot in range(SLOTS):
                    u, q = divmod(slot, PARTS)
                    if units == "loop":
                        first = 0 if u < 3 else NB
                        if q == 0:
                            read, count = [(gelu_ready, it), (ga_ready, it), (ex_ready, 3 * it + 1), (ex_ready, 3 * it + 2),
                                           (ex_ready, 3 * it + 3), (ue_ready, it + 1)][u]
                            if not chain and u < 2:
                                read, count = low_ex, 3 + u
                            unit_ready(U_LOOP + it * LOOP_UNITS + u, read, count)
                    else:
                        first = NB
                        if q == 0:
                            unit_ready(U_GB + u, *((gelu_ready, KT), (ga_ready, KT))[u] if u < 2 else (gb_ready, u - 1))
                    unit_part(u % 2, xh, xl, first, NX, q)
                    if chain:
                        for name in LATE.get(slot, []):
                            stage(name, it - 1, units != "loop")
                    if units == "loop":
                        for name in EARLY.get(slot, []):
                            early(name, it)

            step(0, "loop", False)
            step(1, "loop", True)
            with pe.Fori(2, KT) as it:
                step(it, "loop", True)
            step(KT, "gb", True)

            def phase(base, hi, lo, first, last, read, before=None, extra=None, start=2, ready=None):
                def one(k, u):
                    if ready and isinstance(k, int) and k == 0:
                        for q in range(PARTS):
                            pe.wait_ge(ready[0], ready[1] + (q + 1) * ready[2])
                            unit_part(u, hi, lo, first, last, q)
                    else:
                        unit_part(u, hi, lo, first, last, 0, 1)
                    if extra:
                        extra(k, u)

                if before:
                    for k in range(2):
                        unit_ready(base + k, before[0], before[1] - 1 + k)
                        one(k, k)
                with pe.Fori(start // 2, KT // 2) as i:
                    for u in range(2):
                        unit_ready(base + 2 * i + u, read[0], read[1] + 2 * i + u - 1)
                        one(2 * i + u, u)

            phase(U_GB, xh, xl, NB, NX, (gb_ready, 0), start=6)
            pe.wait_ge(split_lo, 8)
            phase(U_RGO, sbh[0], sbl[0], 0, NT, (merged, 0), (gb_ready, KT))
            pe.wait_ge(split_lo, 8 + KT)
            phase(U_RWO, sbh[1], sbl[1], 0, NT, (gated, 0), (merged, KT))
            phase(U_WO, sbh[0], sbl[0], 0, NT, (x_done, 0), (gated, KT), ready=(merged_lo, 0, 2))
            norm(1)
            f, before = 0, (x_done, KT)
            for kind, g in FFN_PLAN:
                base = U_FFN + f * KT
                if kind == "up":
                    phase(base, xh, xl, NB, NX, (h_relu, KT * g), before, ready=(nrm_lo, 8, 1) if g == 0 else None)
                    before = (h_relu, KT * (g + 1))
                else:
                    pe.wait_ge(h_lo, KT * (g + 1))
                    phase(base, sbh[g % 2], sbl[g % 2], 0, NT, (x_done, KT * (g + 1)), before)
                    before = (x_done, KT * (g + 2))
                f += 1
            pe.wait_ge(ple_in, 16 * 5)
            for k in range(2):
                pe.transpose(bank[4 + k][:, 0:SAMP], ptok[0:SAMP, 0, k * P:(k + 1) * P], cst[0:SAMP, C_ID:C_ID + SAMP])
                for u in range(2):
                    done = turn(bank[4 + k][:, SAMP + u * P:SAMP + (u + 1) * P], ptok[:, 1 + u, k * P:(k + 1) * P])
            done.then_inc(pt_mm, 1)
            norm(2)
            pe.wait_ge(pt_ready, 2)

            def embed(k, u):
                pe.wait_ge(wcol_in[u], 8 * (k - u) + 16)
                pe.wait_ge(x_done, 5 * KT + k - 1)
                mm(bank[2 + u][:, 0:NT], wcol[u][:, 0, :], pt[:, 0, :], True, False)
                mm(bank[2 + u][:, 0:NT], wcol[u][:, 1, :], pt[:, 1, :], False, True).then_inc(embed_mm, 1)

            phase(U_PLE, xh, xl, NB, NX, (sg_ready, 0), before, embed, ready=(nrm_lo, 16, 1))
            for b in range(4):
                for k in range(4):
                    done = turn(bank[4 + b % 2][0:NOUTF, k * P:(k + 1) * P], outf[:, b * 4 + k, :])
                done.then_inc(small_mm, 1)
                if b in (1, 2):
                    pe.wait_ge(small_read, b)
            pe.wait_ge(small_read, 4)
            norm(3)
            for j in range(8):
                pe.wait_ge(nrm_ready, 24 + j + 1)
                if j >= 2:
                    pe.wait_ge(y_read, 3 * (j - 1))
                b3 = (2, 3, 4) if j % 2 == 0 else (5, 6, 1)
                for k in range(2):
                    kc = slice(k * P, (k + 1) * P)
                    turn(bank[b3[0]][0:SAMP, kc], nrm[j % 2][:, k, NB:NB + SAMP])
                    for u in range(2):
                        o = NB + SAMP + u * P
                        done = turn(bank[b3[1 + u]][:, kc], nrm[j % 2][:, k, o:o + P])
                done.then_inc(y_turn, 1)

        @block.scalar
        def _(act):
            def hi(n, slot, half):
                act.wait_ge(raw_in[slot], 16 * half + 16)
                if not (isinstance(n, int) and n < 2):
                    act.wait_ge(unit_done, n - 1)
                act.activation(wh[slot][:], raw[slot][:], ACT.Copy).then_inc(hi_done, 1)

            for b in range(4):
                act.wait_ge(xt_mm, 3 + b)
                act.activation(rga[:, 4 * b:4 * b + 4, 40:40 + P], bank[2 + b][:].rearrange("p (k t) -> p k t", k=4), ACT.Copy).then_inc(xt_act, 1)

            hi(0, 0, 0)
            hi(1, 1, 0)

            def norm(k, width):
                if k == 0:
                    for j in range(8):
                        if j >= 2:
                            act.wait_ge(sum_mm, j - 1)
                        act.activation(nsq[j % 2][:, :, :], rga[:, 2 * j:2 * j + 2, :], ACT.Square).then_inc(sq_ready, 1)
                act.activation(early_root[:, k:k + 1], cst[:, C_ID:C_ID + 1], ACT.Sqrt)
                act.wait_ge(rms_var, k + 1)
                act.activation(sums[:, NX - width:], mean_sq[:, NX - width:], ACT.Sqrt).then_inc(rms_std, 1)

            def norm_split(k, width, out):
                for j in range(8):
                    act.wait_ge(nrm_ready, 8 * k + j + 1)
                    act.activation(out[:, 2 * j:2 * j + 2, NX - width:], nrm[j % 2][:, :, NX - width:], ACT.Copy).then_inc(nrm_hi, 1)

            act.wait_ge(xt_dve, 6)
            act.wait_ge(xt_act, 4)
            norm(0, NX)
            norm_split(0, NX, xh)

            act.wait_ge(lam_abs, 1)
            act.activation(der_work[:, :, 1], der_work[:, :, 1], ACT.Exp, scale=-1.0).then_inc(lam_exp, 1)

            for n in range(4):
                act.wait_ge(unit_done, n + 1)
                if n:
                    act.wait_ge(low_mix, n)
                act.activation(ex[:], bank[n % 2][:, 0:NX], ACT.Copy).then_inc(low_ex, 1)
                if n < 3:
                    hi(n + 2, n % 2, n // 2 + 1)
            act.wait_ge(low_mix, 4)
            act.activation(low[0:RW, 0, :], low[0:RW, 0, :], ACT.Tanh).then_inc(low_ready, 1)
            act.activation(low[:, 2, :], low[:, 2, :], ACT.Sigmoid).then_inc(low_ready, 1)
            act.activation(low[:, 3, :], low[:, 3, :], ACT.Sigmoid).then_inc(low_ready, 1)

            def scalar(col):
                return ptc[:, col:col + 1]

            def early(name, it):
                one = it + 1
                if name == "wd":
                    act.wait_ge(mixed, 3 * it + 1)
                    act.activation(ksq[:], zk[:], ACT.Square, scale=ptu[:, KK:KK + 1]).then_inc(ksq_ready, 1)
                    act.wait_ge(low_mm, 2 * it + 1)
                    act.activation(sigw[:], bank[7][:, 0:NT], ACT.Sigmoid, bias=ptu[:, W0:W0 + 1]).then_inc(sig_ready, 1)
                elif name == "ad":
                    act.wait_ge(low_mm, 2 * it + 2)
                    act.activation(siga[:], bank[7][:, 0:NT], ACT.Sigmoid, bias=ptu[:, A0:A0 + 1]).then_inc(sig_ready, 1)
                elif name == "decay":
                    act.wait_ge(sig_ready, 2 * it + 2)
                    act.activation(sigw[:], sigw[:], ACT.Exp, scale=-math.exp(-0.5)).then_inc(decay_ready, 1)
                    act.wait_ge(ss_ready, one)
                    act.activation(rn[:], rn[:], ACT.Sqrt).then_inc(kk_root, 1)

            def stage(name, p):
                one = p + 1
                if name == "rg_gates":
                    act.wait_ge(ptc_ready, one)
                    act.wait_ge(rgr_mm, one)
                    act.activation(rgr[:], bank[7][:, 0:NT], ACT.Sigmoid, bias=scalar(BA)).then_inc(rgr_sig, 1)
                    act.wait_ge(rgi_mm, one)
                    act.activation(rgi[:], bank[6][:, 0:NT], ACT.Sigmoid, bias=scalar(BX)).then_inc(rgi_sig, 1)
                    act.wait_ge(rgr_sig, one)
                    act.activation(th[:], rgr[:], ACT.Tanh, scale=dtc[:, SP8:SP8 + 1]).then_inc(th_ready, 1)
                elif name == "gate":
                    act.wait_ge(gout_mm, one)
                    act.activation(gout[:], bank[4][:, 0:NT], ACT.Copy).then_inc(gout_read, 1)
                elif name == "rg_decay":
                    act.wait_ge(th_ready, one)
                    act.activation(rgr[:], rgr[:], ACT.Exp, scale=dtc[:, NSP8:NSP8 + 1]).then_inc(rg_exp, 1)
                elif name == "rg_root":
                    act.wait_ge(m2_ready, one)
                    act.activation(m2[:], m2[:], ACT.Sqrt).then_inc(m_root, 1)
                elif name == "turn":
                    act.wait_ge(turn_mm, one)
                    act.activation(tmb[:].rearrange("p a b -> p (a b)"), bank[2][:], ACT.Copy)
                    act.activation(tmv[:].rearrange("p a b -> p (a b)"), bank[3][:, 0:256], ACT.Copy)
                    act.activation(sbk[:], bank[3][0:64, 256:384], ACT.Copy)
                    act.activation(svv[:], bank[3][0:64, 384:512], ACT.Copy)
                    act.activation(suv[SAMP:2 * SAMP, :], bank[3][SAMP:2 * SAMP, 384:512], ACT.Copy).then_inc(turn_read, 1)
                elif name == "pairwise":
                    act.wait_ge(pair_mm, 3 * one)
                    for h in range(2):
                        act.activation(ab[:, 2 * h:2 * h + 2, :].rearrange("p a b -> p (a b)"), bank[2 + h][:, 0:2 * CHUNK], ACT.Copy).then_inc(ab_read, 1)
                elif name[:6] == "invert" and name[7] == "a":
                    act.wait_ge(yy_mm, 5 * p + int(name[6]))
                    flat = yy[:].rearrange("p a b -> p (a b)")
                    act.activation(flat[0:64, :], bank[5][0:64, 0:256], ACT.Copy)
                    act.activation(flat[64:128, :], bank[6][64:128, 0:256], ACT.Copy).then_inc(yy_read[int(name[6]) - 1], 1)
                elif name == "state_in":
                    act.wait_ge(state_mm, one)
                    for b in range(2):
                        act.activation(ms[:, 4 * b:4 * b + 4, :].rearrange("p a b -> p (a b)"), bank[2 + b][:], ACT.Copy).then_inc(state_read, 1)
                elif name == "samp_inv_a":
                    act.wait_ge(syy_mm, one)
                    act.activation(syy[:].rearrange("p a b -> p (a b)"), bank[2][0:SAMP, 0:2 * SAMP], ACT.Copy).then_inc(syy_read, 1)
                elif name == "samp_r":
                    act.wait_ge(sr_mm, one)
                    act.activation(sr[:], bank[2][0:SAMP, 0:P], ACT.Copy).then_inc(sr_read, 1)
                elif name == "samp_out":
                    act.wait_ge(so_mm, one)
                    y_samples = yf[:, 0:SAMP].rearrange("p (t b) -> p b t", b=NB)
                    for k in range(2):
                        own = slice(4 * k, 4 * k + 4)
                        act.activation(y_samples[:, own, :], sample_out(k)[:, :, HEAD:], ACT.Copy)
                        ins = act.activation(so[:, own, :], sample_out(k)[:, :, 0:HEAD], ACT.Copy)
                    ins.then_inc(so_ready, 1)
                elif name[0] == "r" and name[1:].isdigit():
                    c = int(name[1:])
                    rc = slice((c % 2) * CHUNK, (c % 2 + 1) * CHUNK)
                    act.wait_ge(r_mm, NCH * p + c + 1)
                    act.activation(rs[rc, :], bank[4][rc, 0:P], ACT.Copy).then_inc(r_read[c], 1)
                elif name == "fin":
                    act.wait_ge(y_mm, NCH * one)
                    act.activation(yf[:, SAMP:], bank[7][:, SAMP:NT], ACT.Copy).then_inc(yf_ready, 1)
                    act.wait_ge(fin_mm, one)
                    act.activation(sfin[:], bank[2][:, 0:P], ACT.Copy).then_inc(fin_read, 1)
                elif name == "mean":
                    act.wait_ge(yc_ready, one)
                    act.activation(ysq[:], yc[:], ACT.Square).then_inc(ysq_ready, 1)
                elif name == "var":
                    act.wait_ge(var_ready, one)
                    act.activation(sd[:], sd[:], ACT.Sqrt).then_inc(y_root, 1)

            def evict(u, it):
                if u == 3:
                    return
                act.wait_ge(unit_done, U_LOOP + it * LOOP_UNITS + u + 1)
                out = bank[u % 2]
                if u == 4:
                    if not (isinstance(it, int) and it == 0):
                        act.wait_ge(rga_ready, it)
                    act.activation(gg[:], out[:, 0:NT], ACT.Gelu_apprx_tanh).then_inc(gelu_ready, 1)
                elif u == 5:
                    if not (isinstance(it, int) and it == 0):
                        act.wait_ge(ga_saved, 16 * it)
                    act.activation(gat[:], out[:, 0:NT], ACT.Sigmoid).then_inc(ga_ready, 1)
                else:
                    if not (isinstance(it, int) and it == 0 and u == 0):
                        act.wait_ge(mixed, 3 * it + u)
                    act.activation(ex[:], out[:, 0:NX], ACT.Copy).then_inc(ex_ready, 1)

            def gb_evict(u):
                act.wait_ge(unit_done, U_GB + u + 1)
                act.wait_ge(ga_saved, 16 * KT)
                if u:
                    act.wait_ge(gb_saved[(u - 1) % 2], 16 * ((u - 1) // 2 + 1))
                act.activation(gat[:], bank[u % 2][:, 0:NT], ACT.Sigmoid).then_inc(gb_ready, 1)

            def hi_half(n, slot, half, part):
                if part == 0:
                    act.wait_ge(raw_in[slot], 16 * half + 16)
                    act.wait_ge(unit_done, n - 1)
                k = slice(part * KT // 2, (part + 1) * KT // 2)
                act.activation(wh[slot][:, k, :], raw[slot][:, k, :], ACT.Copy).then_inc((half_done, hi_done)[part], 1)

            def step(it, units, chain):
                for slot in range(SLOTS):
                    u, q = divmod(slot, PARTS)
                    if q == 0:
                        if units == "loop":
                            if u:
                                evict(u - 1, it)
                            elif chain:
                                evict(5, it - 1)
                        elif u:
                            gb_evict(u - 1)
                        else:
                            evict(5, it - 1)
                    if q in HI_AT:
                        n, half = ((U_LOOP + it * LOOP_UNITS + u + 1, (U_LOOP + u + 1) // 2 + it * (LOOP_UNITS // 2)) if units == "loop"
                                   else (U_GB + u + 1, (U_GB + u + 1) // 2))
                        hi_half(n, (u + 1) % 2, half, HI_AT.index(q))
                    if chain:
                        for name in LATE.get(slot, []):
                            stage(name, it - 1)
                    if units == "loop":
                        for name in EARLY.get(slot, []):
                            early(name, it)

            step(0, "loop", False)
            step(1, "loop", True)
            with act.Fori(2, KT) as it:
                step(it, "loop", True)
            step(KT, "gb", True)
            gb_evict(5)
            hi(U_GB + 7, 1, (U_GB + 7) // 2)

            def phase(base, evict=None, start=0, stop=KT, ahead=True):
                with act.Fori(start // 2, (stop if ahead else stop - 2) // 2) as i:
                    for u in range(2):
                        if evict:
                            evict(2 * i + u, u, i)
                        hi(base + 2 * i + u + 2, u, base // 2 + i + 1)
                if not ahead:
                    for u in range(2):
                        evict(KT - 2 + u, u, KT // 2 - 1)

            def gb_evict_rest(k, u, i):
                act.wait_ge(unit_done, U_GB + k + 1)
                act.wait_ge(gb_saved[u], 16 * i)
                act.activation(tmp[u][:], bank[u][:, 0:NT], ACT.Sigmoid).then_inc(gb_ready, 1)

            act.wait_ge(rwo_ready, KT)
            act.wait_ge(y_mm, NCH * KT)
            act.wait_ge(rga_ready, KT)
            act.wait_ge(so_saved, 16 * KT)
            act.wait_ge(fin_saved, 32 * KT)

            def gb_and_split(k, u, i):
                gb_evict_rest(k, u, i)
                two = bass.ds(2 * k - 12, 2)
                act.activation(sbh[0][:, two, :], rga[:, two, NB:], ACT.Copy).then_inc(split_hi, 1)

            phase(U_GB, gb_and_split, start=6, stop=14)
            phase(U_GB, gb_evict_rest, start=14)

            def split_b(k, u, i):
                one = bass.ds(k, 1)
                act.activation(sbh[1][:, one, :], rwo[:, one, :], ACT.Copy).then_inc(split_hi, 1)

            phase(U_RGO, split_b)

            def split_merged(k, u, i):
                act.wait_ge(merged, KT + k + 1)
                act.activation(sbh[0][:, bass.ds(k, 1), :].rearrange("p o t -> p (o t)"), rwo[:, bass.ds(k, 1), :].rearrange("p o t -> p (o t)"), ACT.Copy).then_inc(merged_hi, 1)

            phase(U_RWO, split_merged)
            phase(U_WO)
            act.wait_ge(x_done, KT)
            norm(1, NT)
            norm_split(1, NT, xh)
            n = 0
            for kind, g in FFN_PLAN:
                base = U_FFN + n * KT

                def hidden(k, u, i, base=base, g=g):
                    act.wait_ge(unit_done, base + k + 1)
                    if not (g == 0 and isinstance(i, int)):
                        act.wait_ge(h_lo, KT * g + k - 1)
                    act.activation(tmp[u][:], bank[u][:, 0:NT], ACT.Relu).then_inc(h_relu, 1)
                    act.wait_ge(h_relu, KT * g + k + 1)
                    act.activation(tmp[u][:], tmp[u][:], ACT.Square).then_inc(h_sq, 1)
                    act.wait_ge(h_sq, KT * g + k + 1)
                    act.activation(sbh[g % 2][:, bass.ds(k, 1), :].rearrange("p o t -> p (o t)"), tmp[u][:], ACT.Copy).then_inc(h_hi, 1)

                if kind == "up" and g == 0:
                    for u in range(2):
                        hidden(u, u, 0)
                        hi(base + u + 2, u, base // 2 + 1)
                    phase(base, lambda k, u, i, h=hidden: h(k, u, i), start=2)
                else:
                    phase(base, hidden if kind == "up" else None)
                n += 1
            act.wait_ge(x_done, 5 * KT)
            norm(2, NT)
            norm_split(2, NT, xh)

            def ple_gate(k, u, i):
                act.wait_ge(unit_done, U_PLE + k + 1)
                act.wait_ge(x_done, 5 * KT + k - 1)
                act.activation(tmp[u][:], bank[u][:, 0:NT], ACT.Sigmoid).then_inc(sg_ready, 1)

            phase(U_PLE, ple_gate, ahead=False)
            for b in range(4):
                act.wait_ge(small_mm, b + 1)
                act.activation(small_out[:, b * 512:(b + 1) * 512], bank[4 + b % 2][0:NOUTF, :], ACT.Copy).then_inc(small_read, 1)
            act.wait_ge(x_done, 6 * KT)
            norm(3, NT)
            for j in range(8):
                act.wait_ge(y_turn, j + 1)
                b3 = (2, 3, 4) if j % 2 == 0 else (5, 6, 1)
                cols = slice(j * 256, (j + 1) * 256)
                act.activation(ytok[0:SAMP, 0, cols], bank[b3[0]][0:SAMP, 0:256], ACT.Copy).then_inc(y_read, 1)
                for u in range(2):
                    act.activation(ytok[:, 1 + u, cols], bank[b3[1 + u]][:, 0:256], ACT.Copy).then_inc(y_read, 1)

        @block.vector
        def _(dve):
            def lo(n, slot):
                dve.wait_ge(hi_done, n + 1)
                dve.tensor_tensor(wl[slot][:], raw[slot][:], wh[slot][:].bitcast(F32), ALU.subtract).then_inc(lo_done, 1)

            def tt_(out, x, y, op):
                return dve.tensor_tensor(out, x, y, op)

            def stt(out, x, s, y, op0, op1):
                return dve.scalar_tensor_tensor(out, x, s, y, op0, op1)

            def ts(out, x, s1, s2=None, op0=ALU.mult, op1=ALU.bypass):
                return dve.tensor_scalar(out, x, s1, s2, op0, op1)

            for b in range(2):
                dve.wait_ge(xt_mm, b + 1)
                dve.tensor_copy(rga[:, 8 * b:8 * b + 8, 0:40], bank[b][:, 0:320].rearrange("p (k t) -> p k t", k=8)).then_inc(xt_dve, 1)
            for b in range(4):
                dve.wait_ge(xt_mm, 7 + b)
                dve.tensor_copy(rga[:, 4 * b:4 * b + 4, 40 + P:NX], bank[(6, 7, 0, 1)[b]][:].rearrange("p (k t) -> p k t", k=4)).then_inc(xt_dve, 1)
            lo(0, 0)
            lo(1, 1)

            def norm(k, width, gain, split):
                first = NX - width
                v, y, t = mean_sq[:, first:], sums[:, first:], nsq[0][:, 0, first:]
                dve.wait_ge(sum_mm, 8 + k)
                ts(v, bank[7][:, 0:width], EPS, op0=ALU.add).then_inc(rms_var, 1)
                dve.wait_ge(rms_std, k + 1)
                dve.reciprocal(y, y).then_inc(rms_inv, 1)
                dve.wait_ge(rms_inv, 4 * k + 1)
                tt_(t, y, y, ALU.mult).then_inc(rms_inv, 1)
                dve.wait_ge(rms_inv, 4 * k + 2)
                stt(t, t, -0.5, v, ALU.mult, ALU.mult).then_inc(rms_inv, 1)
                dve.wait_ge(rms_inv, 4 * k + 3)
                stt(y, t, 1.5, y, ALU.add, ALU.mult).then_inc(rms_inv, 1)
                dve.wait_ge(rms_inv, 4 * k + 4)
                if k == 0:
                    for b in range(2):
                        dve.wait_ge(par_mm, b + 1)
                        dve.tensor_copy(par[:, 8 * b:8 * b + 8, :], bank[2 + b][:, 0:8 * NPAR].rearrange("p (k t) -> p k t", k=8)).then_inc(par_ready, 1)
                    dve.wait_ge(par_ready, 2)

                def low_part(j):
                    dve.wait_ge(nrm_hi, 8 * k + j + 1)
                    tt_(split[1][:, 2 * j:2 * j + 2, first:], nrm[j % 2][:, :, first:], split[0][:, 2 * j:2 * j + 2, first:].bitcast(F32),
                        ALU.subtract).then_inc(nrm_lo, 1)

                for j in range(8):
                    n = nrm[j % 2]
                    if j >= 2:
                        if split:
                            dve.wait_ge(nrm_lo, 8 * k + j - 1)
                        else:
                            dve.wait_ge(y_turn, j - 1)
                    if k == 0:
                        dve.tensor_copy(n[:, :, 0:NB], rga[:, 2 * j:2 * j + 2, 0:NB])
                    for h in range(2):
                        ins = stt(n[:, h, NB:], rga[:, 2 * j + h, NB:], par[:, 2 * j + h, gain:gain + 1], sums[:, NB:], ALU.mult, ALU.mult)
                    ins.then_inc(nrm_ready, 1)
                    if k == 0:
                        dve.wait_ge(nrm_ready, j + 1)
                        dve.tensor_copy(outf[:, 2 * j:2 * j + 2, O_SHIFT:O_SHIFT + 1], n[:, :, NX - 1:NX])
                        dve.tensor_copy(outf[:, 2 * j:2 * j + 2, O_SHIFT + 1:O_SHIFT + 1 + NB], n[:, :, NB + SAMP - NB:NB + SAMP])
                    if split and j:
                        low_part(j - 1)
                if split:
                    low_part(7)

            norm(0, NX, GMIX, (xh, xl))

            head = Count(der_step, 0, 0)
            lam = par[:, :, LAM]
            w1, w2, w3, w4 = (der_work[:, :, k] for k in range(4))
            ts(w1, lam, -1.0).then_inc(head.sem, head.one())
            dve.wait_ge(head.sem, head.so_far())
            tt_(w1, w1, lam, ALU.max).then_inc(head.sem, head.one())
            dve.wait_ge(head.sem, head.so_far())
            dve.tensor_copy(w2, w1).then_inc(lam_abs, 1)
            dve.wait_ge(lam_exp, 1)
            ts(w3, w2, 2.0, op0=ALU.add).then_inc(head.sem, head.one())
            dve.wait_ge(head.sem, head.so_far())
            dve.reciprocal(w3, w3).then_inc(head.sem, head.one())
            dve.wait_ge(head.sem, head.so_far())
            tt_(w2, w2, w3, ALU.mult).then_inc(head.sem, head.one())
            dve.wait_ge(head.sem, head.so_far())
            tt_(w3, w2, w2, ALU.mult).then_inc(head.sem, head.one())
            dve.memset(w4, 1.0 / 19).then_inc(head.sem, head.one())
            dve.wait_ge(head.sem, head.so_far())
            for k in range(8, -1, -1):
                tt_(w4, w4, w3, ALU.mult).then_inc(head.sem, head.one())
                dve.wait_ge(head.sem, head.so_far())
                ts(w4, w4, 1.0 / (2 * k + 1), op0=ALU.add).then_inc(head.sem, head.one())
                dve.wait_ge(head.sem, head.so_far())
            tt_(w4, w4, w2, ALU.mult).then_inc(head.sem, head.one())
            ts(w1, lam, -1.0, 0.0, ALU.mult, ALU.max).then_inc(head.sem, head.one())
            dve.wait_ge(head.sem, head.so_far())
            stt(w4, w4, 2.0, w1, ALU.mult, ALU.add).then_inc(head.sem, head.one())
            dve.wait_ge(head.sem, head.so_far())
            ts(der[:, :, SP8], w4, 8.0).then_inc(head.sem, head.one())
            ts(der[:, :, NSP8], w4, -8.0).then_inc(head.sem, head.one())
            dve.wait_ge(head.sem, head.so_far())

            def shift_mix(mu, z, chain, done):
                tt_(dif[:, 0:SAMP], ex[:, 0:SAMP], ex[:, NB:NB + SAMP], ALU.subtract).then_inc(chain.sem, chain.one())
                ts(dif[:, SAMP:SAMP + 1], ex[:, NB + SAMP:NB + SAMP + 1], -1.0).then_inc(chain.sem, chain.one())
                tt_(dif[:, SAMP + 1:NT], ex[:, NB + SAMP:NX - 1], ex[:, NB + SAMP + 1:NX], ALU.subtract).then_inc(chain.sem, chain.one())
                dve.wait_ge(chain.sem, chain.so_far())
                stt(z, dif[:], mu, ex[:, NB:NX], ALU.mult, ALU.add).then_inc(done, 1)

            for n in range(4):
                dve.wait_ge(low_ex, n + 1)
                if n:
                    dve.wait_ge(low_mix, n)
                shift_mix(par[:, 0, MULOW + n:MULOW + n + 1], low[:, n, :], head, low_mix)
                if n < 3:
                    lo(n + 2, n % 2)

            def conv(it, chain):
                dve.wait_ge(unit_done, U_LOOP + it * LOOP_UNITS + 4)
                if isinstance(it, int) and it == 0:
                    dve.wait_ge(init_done, N_INIT)
                else:
                    dve.wait_ge(rgi_mm, it)
                dve.tensor_copy(ue[:, 24:24 + SAMP], bank[1][:, 0:SAMP]).then_inc(chain.sem, chain.one())
                dve.tensor_copy(ue[:, 59:315], bank[1][:, SAMP:NT]).then_inc(ue_ready, 1)
                dve.tensor_copy(ue[:, 0:24], ptu[:, CONV_STATE:CONV_STATE + 24]).then_inc(chain.sem, chain.one())
                dve.wait_ge(chain.sem, chain.so_far())
                dve.wait_ge(ue_ready, it + 1)
                parts = ((0, SAMP, 0, NB), (SAMP, NT, 56, 1))
                for x0, x1, o, by in parts:
                    ts(xc[:, x0:x1], ue[:, o:o + x1 - x0], ptu[:, CW:CW + 1], ptu[:, CB:CB + 1], ALU.mult, ALU.add).then_inc(chain.sem, chain.one())
                for j in range(1, 4):
                    dve.wait_ge(chain.sem, chain.so_far())
                    for x0, x1, o, by in parts:
                        ins = stt(xc[:, x0:x1], ue[:, o + j * by:o + j * by + x1 - x0], ptu[:, CW + j:CW + j + 1], xc[:, x0:x1], ALU.mult, ALU.add)
                        if j == 3 and x0:
                            ins.then_inc(conv_ready, 1)
                        else:
                            ins.then_inc(chain.sem, chain.one())
                dve.tensor_copy(outf[:, bass.ds(it, 1), O_CONV:O_CONV + 3].rearrange("p o t -> p (o t)"), ue[:, 312:315]).then_inc(chain.sem, chain.one())
                dve.tensor_copy(outf[:, bass.ds(it, 1), O_CONV + 3:NOUTF].rearrange("p o t -> p (o t)"), ue[:, 24 + NB:24 + SAMP]).then_inc(chain.sem, chain.one())

            def scalar(col):
                return ptc[:, col:col + 1]

            def early(name, it, rg):
                one = it + 1
                if name == "ad":
                    dve.wait_ge(sig_ready, 2 * it + 2)
                    ts(kp[:], siga[:], 1.0, ptu[:, KA:KA + 1], ALU.subtract, ALU.mult).then_inc(rg.sem, rg.one())
                    dve.wait_ge(rg.sem, rg.so_far())
                    stt(kp[:], kp[:], 1.0, zk[:], ALU.add, ALU.mult).then_inc(rg.sem, rg.one())
                elif name == "kk_sum":
                    dve.wait_ge(kk_mm, one)
                    ts(rn[:], bank[7][:, 0:NT], 1e-24, op0=ALU.max).then_inc(ss_ready, 1)
                elif name == "kk":
                    dve.wait_ge(kk_root, one)
                    dve.reciprocal(rn[:], rn[:]).then_inc(rg.sem, rg.one())
                    dve.wait_ge(rg.sem, rg.so_far())
                    stt(kkn[:], zk[:], ptu[:, KK:KK + 1], rn[:], ALU.mult, ALU.mult).then_inc(rg.sem, rg.one())
                elif name == "cum":
                    dve.wait_ge(decay_ready, one)
                    if not (isinstance(it, int) and it == 0):
                        dve.wait_ge(sexp_ready, it)
                    if isinstance(it, int) and it == 0:
                        dve.wait_ge(init_done, N_INIT)
                    for c in range(NCH):
                        o = 5 * NB + c * (CHUNK + 1) + 1
                        dve.tensor_tensor_scan(cum[:, o:o + CHUNK], sigw[:, SAMP + c * CHUNK:SAMP + (c + 1) * CHUNK], zeros[:], 1.0,
                                               ALU.mult, ALU.add).then_inc(rg.sem, rg.one())
                    for t in range(NS):
                        dve.wait_ge(rg.sem, rg.so_far())
                        tt_(cum[:, (t + 1) * NB:(t + 2) * NB], cum[:, t * NB:(t + 1) * NB], sigw[:, t * NB:(t + 1) * NB],
                            ALU.mult).then_inc(rg.sem, rg.one())
                    dve.wait_ge(rg.sem, rg.so_far())
                    at = cum_of("at")
                    dve.reciprocal(rn[:, samp_all], at[0]).then_inc(rg.sem, rg.one())
                    dve.reciprocal(chunks(rn[:]), at[1]).then_inc(rg.sem, rg.one())
                elif name == "tilde":
                    tt_(btl[:], kkn[:], siga[:], ALU.mult).then_inc(rg.sem, rg.one())
                    dve.wait_ge(rg.sem, rg.so_far())
                    tt_(btl[:], btl[:], rn[:], ALU.mult).then_inc(rg.sem, rg.one())
                    tt_(ktl[:], kp[:], rn[:], ALU.mult).then_inc(rg.sem, rg.one())
                    dve.wait_ge(rg.sem, rg.so_far())
                    last = cum[:, NS * NB:(NS + 1) * NB].unsqueeze(1).to_broadcast([P, NS, NB])
                    for k, src in enumerate((btl, ktl)):
                        tt_(bkh[:, k * SAMP:(k + 1) * SAMP].rearrange("p (t b) -> p t b", b=NB),
                            src[:, samp_all].rearrange("p (t b) -> p t b", b=NB), last, ALU.mult).then_inc(rg.sem, rg.one())
                elif name == "early_done":
                    dve.wait_ge(mixed, 3 * one)
                    dve.tensor_copy(vv[:, 0:SAMP], zv[:, samp_all]).then_inc(rg.sem, rg.one())
                    dve.tensor_copy(vv[:, SAMP:], zv[:, samp_all]).then_inc(early_end, 1)

            def stage(name, p, ch):
                one = p + 1
                later = not (isinstance(p, int) and p == 0)
                if name == "ar":
                    if later:
                        dve.wait_ge(rwo_ready, p)
                        dve.wait_ge(m_ready, NCH * p)
                    dve.wait_ge(early_end, one)
                    dve.tensor_copy(dtc[:], der[:, bass.ds(p, 1), :].rearrange("p o t -> p (o t)")).then_inc(ch.sem, ch.one())
                    dve.tensor_copy(ptc[:], par[:, bass.ds(p, 1), :].rearrange("p o t -> p (o t)")).then_inc(ptc_ready, 1)
                    dve.wait_ge(ptc_ready, one)
                    stt(bv[:], zr[:], scalar(RK), kp[:], ALU.mult, ALU.mult).then_inc(bt_ready, 1)
                    for c in range(NCH):
                        dve.tensor_copy(dl[:, c:c + 1], last_decay(c)).then_inc(ch.sem, ch.one())
                    before, at = cum_of("before"), cum_of("at")
                    for out, x, s, y in ((ar[:, 0, samp_all], kkn[:, samp_all], -1.0, before[0]),
                                         (chunks(ar[:, 0, :]), chunks(kkn[:]), -1.0, before[1]),
                                         (ar[:, 1, samp_all], zr[:, samp_all], 1.0, at[0])):
                        stt(out, x, s, y, ALU.mult, ALU.mult).then_inc(ch.sem, ch.one())
                    tt_(chunks(ar[:, 1, :]), chunks(zr[:]), at[1], ALU.mult).then_inc(ar_ready, 1)
                elif name == "rg_gates":
                    dve.wait_ge(rgi_sig, one)
                    dve.wait_ge(rgr_sig, one)
                    tt_(rgi[:], rgi[:], xc[:], ALU.mult).then_inc(ch.sem, ch.one())
                elif name == "bonus":
                    dve.wait_ge(bonus_mm, one)
                    tt_(bv[:], bank[5][:, 0:NT], zv[:], ALU.mult).then_inc(bonus_read, 1)
                elif name == "rg_decay":
                    dve.wait_ge(rg_exp, one)
                    tt_(m2[:], rgr[:], rgr[:], ALU.mult).then_inc(ch.sem, ch.one())
                    dve.wait_ge(ch.sem, ch.so_far())
                    stt(m2[:], m2[:], 1.0, th[:], ALU.add, ALU.mult).then_inc(m2_ready, 1)
                elif name == "rg_scan":
                    dve.wait_ge(m_root, one)
                    dve.memset(m2[:, SAMP:SAMP + 1], 1.0).then_inc(ch.sem, ch.one())
                    dve.wait_ge(ch.sem, ch.so_far())
                    tt_(m2[:], m2[:], rgi[:], ALU.mult).then_inc(ch.sem, ch.one())
                    dve.wait_ge(ch.sem, ch.so_far())
                    dve.tensor_tensor_scan(th[:, SAMP:NT], rgr[:, SAMP:NT], m2[:, SAMP:NT], 0.0, ALU.mult, ALU.add).then_inc(ch.sem, ch.one())
                    for t in range(NS):
                        now = slice(t * NB, (t + 1) * NB)
                        prev = ptc[:, H_STATE:H_STATE + NB] if t == 0 else th[:, (t - 1) * NB:t * NB]
                        tt_(th[:, now], rgr[:, now], prev, ALU.mult).then_inc(ch.sem, ch.one())
                        dve.wait_ge(ch.sem, ch.so_far())
                        tt_(th[:, now], th[:, now], m2[:, now], ALU.add).then_inc(ch.sem, ch.one())
                        dve.wait_ge(ch.sem, ch.so_far())
                    dve.tensor_copy(outf[:, bass.ds(p, 1), O_H:O_H + 1].rearrange("p o t -> p (o t)"), th[:, NT - 1:NT]).then_inc(ch.sem, ch.one())
                    dve.tensor_copy(outf[:, bass.ds(p, 1), O_H + 1:O_H + 1 + NB].rearrange("p o t -> p (o t)"), th[:, SAMP - NB:SAMP]).then_inc(ch.sem, ch.one())
                    dve.wait_ge(gelu_ready, one)
                    if not later:
                        dve.wait_ge(xt_saved, 16)
                    tt_(rga[:, bass.ds(p, 1), NB:].rearrange("p o t -> p (o t)"), th[:], gg[:], ALU.mult).then_inc(rga_ready, 1)
                elif name == "pairwise":
                    masks = cst[:, C_AM:C_AM + 256].unsqueeze(1).to_broadcast([P, 2, 256])
                    for h in range(2):
                        dve.wait_ge(pair_mm, 3 * p + h + 1)
                        tt_(ams[:, 2 * h:2 * h + 2, :], bank[4 + h][:].rearrange("p (g t) -> p g t", g=2), masks, ALU.mult).then_inc(pair_read, 1)
                    dve.wait_ge(ab_read, 2 * one)
                    tt_(tn, ab[:], cst[:, C_LM:C_LM + CHUNK].unsqueeze(1).to_broadcast([P, 4, CHUNK]), ALU.mult).then_inc(ch.sem, ch.one())
                    eye = cst[:, C_ID2:C_ID2 + HEAD].unsqueeze(1).to_broadcast([P, 4, CHUNK])
                    dve.wait_ge(pair_read, 2 * one)
                    tt_(tt, ams[:, :, 0:CHUNK], eye, ALU.add).then_inc(ch.sem, ch.one())
                    dve.wait_ge(ch.sem, ch.so_far())
                    tt_(tn, tn, eye, ALU.add).then_inc(tn_ready[0], 1)
                elif name[:6] == "invert" and name[7] == "b":
                    l = int(name[6])
                    dve.wait_ge(tn_mm, 5 * p + l)
                    dve.wait_ge(tn_ready[l - 1], one)
                    n = 512 if l < 5 else 256
                    tt_(inv[0:64, 0:n], inv[0:64, 0:n], bank[5][0:64, 0:n], ALU.add).then_inc(ch.sem, ch.one())
                    tt_(inv[64:128, 0:n], inv[64:128, 0:n], bank[6][64:128, 0:n], ALU.add).then_inc(tn_ready[l], 1)
                elif name == "samp_pair":
                    dve.wait_ge(spair_mm, one)
                    for h in range(2):
                        tt_(sam[:, h, :], bank[2 + h][0:SAMP, 0:128], cst[0:SAMP, C_SAM:C_SAM + 128], ALU.mult).then_inc(ch.sem, ch.one())
                        tt_(stn[:, h, :], bank[2 + h][0:SAMP, 128:160], cst[0:SAMP, C_SLM:C_SLM + SAMP], ALU.mult).then_inc(ch.sem, ch.one())
                        tt_(sa2[:, h, :], bank[2 + h][0:SAMP, 128:160], cst[0:SAMP, C_SLM + SAMP:C_SLM + 2 * SAMP], ALU.mult).then_inc(ch.sem, ch.one())
                    dve.wait_ge(ch.sem, ch.so_far())
                    eye = cst[0:SAMP, C_ID:C_ID + SAMP].unsqueeze(1).to_broadcast([SAMP, 2, SAMP])
                    tt_(stn[:], stn[:], eye, ALU.add).then_inc(ch.sem, ch.one())
                    tt_(stt_s[:], sam[:, :, 0:SAMP], eye, ALU.add).then_inc(sinv_ready, 1)
                    dve.wait_ge(sinv_ready, one)
                elif name == "samp_inv_b":
                    dve.wait_ge(stt_mm, one)
                    flat = "p a b -> p (a b)"
                    tt_(stt_s[:].rearrange(flat), stt_s[:].rearrange(flat), bank[3][0:SAMP, 0:2 * SAMP], ALU.add).then_inc(stt_ready, 1)
                elif name == "samp_u":
                    dve.wait_ge(su_mm, one)
                    dve.tensor_copy(suv[0:SAMP, :], bank[3][0:SAMP, 0:P]).then_inc(su_read, 1)
                elif name[0] == "u":
                    c = int(name[1:])
                    rc = slice((c % 2) * CHUNK, (c % 2 + 1) * CHUNK)
                    dve.wait_ge(u_mm, NCH * p + c + 1)
                    dve.tensor_copy(us[rc, :], bank[5][rc, 0:P]).then_inc(u_read, 1)
                elif name[:2] == "my":
                    c = int(name[2:])
                    dve.wait_ge(m_mm, NCH * p + c + 1)
                    new = mp[(c + 1) % 2]
                    if c:
                        if c == 1 and later:
                            dve.wait_ge(fin_saved, 32 * p)
                        dve.wait_ge(m_ready, NCH * p + c)
                        tt_(mtmp[:], mp[c % 2][:], bank[6][:, 0:P], ALU.add).then_inc(ch.sem, ch.one())
                        dve.wait_ge(ch.sem, ch.so_far())
                        stt(new[:], mtmp[:], dl[:, c:c + 1], bd, ALU.mult, ALU.mult).then_inc(m_ready, 1)
                    else:
                        stt(new[:], bank[6][:, 0:P], dl[:, c:c + 1], bd, ALU.mult, ALU.mult).then_inc(m_ready, 1)
                elif name == "mean":
                    dve.wait_ge(mean_mm, one)
                    stt(yc[:], bank[4][:, 0:NT], -1.0 / HEAD, yf[:], ALU.mult, ALU.add).then_inc(yc_ready, 1)
                elif name == "var":
                    dve.wait_ge(var_mm, one)
                    ts(sd[:], bank[5][:, 0:NT], 1.0 / HEAD, GN_EPS, ALU.mult, ALU.add).then_inc(var_ready, 1)
                    dve.wait_ge(y_root, one)
                    dve.reciprocal(sd[:], sd[:]).then_inc(ch.sem, ch.one())
                    dve.wait_ge(ch.sem, ch.so_far())
                    stt(yc[:], yc[:], scalar(GNW), sd[:], ALU.mult, ALU.mult).then_inc(ch.sem, ch.one())
                    dve.wait_ge(ch.sem, ch.so_far())
                    stt(yc[:], yc[:], scalar(GNB), bv[:], ALU.add, ALU.add).then_inc(ch.sem, ch.one())
                    dve.wait_ge(ch.sem, ch.so_far())
                    tt_(rwo[:, bass.ds(p, 1), :].rearrange("p o t -> p (o t)"), yc[:], gout[:], ALU.mult).then_inc(rwo_ready, 1)

            def lo_half(n, slot, part):
                dve.wait_ge((half_done, hi_done)[part], n - U_LOOP if part == 0 else n + 1)
                k = slice(part * KT // 2, (part + 1) * KT // 2)
                ins = dve.tensor_tensor(wl[slot][:, k, :], raw[slot][:, k, :], wh[slot][:, k, :].bitcast(F32), ALU.subtract)
                if part:
                    ins.then_inc(lo_done, 1)

            def step(it, units, chain):
                rg = Count(dve_rg, it, STEPS["dve_rg"])
                ch = Count(dve_ch, it - 1, STEPS["dve_ch"])
                for slot in range(SLOTS):
                    u, q = divmod(slot, PARTS)
                    if q == 0 and units == "loop":
                        if u == 0:
                            if chain:
                                dve.wait_ge(rg.sem, rg.so_far())
                                dve.wait_ge(conv_ready, it)
                            dve.tensor_copy(ptu[:], par[:, bass.ds(it, 1), :].rearrange("p o t -> p (o t)")).then_inc(rg.sem, rg.one())
                        elif u <= 3:
                            if chain:
                                dve.wait_ge(ch.sem, ch.so_far())
                            dve.wait_ge(ex_ready, 3 * it + u)
                            if not (isinstance(it, int) and it == 0 and u == 1):
                                dve.wait_ge(mixed, 3 * it + u - 1)
                            if u == 1:
                                dve.wait_ge(rg.sem, rg.so_far())
                            col = (MUK, MUR, MUV)[u - 1]
                            shift_mix(ptu[:, col:col + 1], (zk, zr, zv)[u - 1][:], rg, mixed)
                        elif u == 4:
                            if chain:
                                dve.wait_ge(ch.sem, ch.so_far())
                            conv(it, rg)
                    if q in LO_AT:
                        n = U_LOOP + it * LOOP_UNITS + u + 1 if units == "loop" else U_GB + u + 1
                        lo_half(n, (u + 1) % 2, LO_AT.index(q))
                    if chain:
                        for name in LATE.get(slot, []):
                            stage(name, it - 1, ch)
                    if units == "loop":
                        for name in EARLY.get(slot, []):
                            early(name, it, rg)
                if units == "loop":
                    rg.end()
                if chain:
                    ch.end()

            step(0, "loop", False)
            step(1, "loop", True)
            with dve.Fori(2, KT) as it:
                step(it, "loop", True)
            step(KT, "gb", True)
            lo(U_GB + 7, 1)

            def phase(base, evict=None, start=0, stop=KT, ahead=True):
                with dve.Fori(start // 2, (stop if ahead else stop - 2) // 2) as i:
                    for u in range(2):
                        if evict:
                            evict(2 * i + u, u, i)
                        lo(base + 2 * i + u + 2, u)
                if not ahead:
                    for u in range(2):
                        evict(KT - 2 + u, u, KT // 2 - 1)

            def tile(buf, k, first=0):
                return buf[:, bass.ds(k, 1), first:].rearrange("p o t -> p (o t)")

            def split_a(k, u, i):
                dve.wait_ge(split_hi, k - 5)
                two = bass.ds(2 * k - 12, 2)
                tt_(sbl[0][:, two, :], rga[:, two, NB:], sbh[0][:, two, :].bitcast(F32), ALU.subtract).then_inc(split_lo, 1)

            phase(U_GB, split_a, start=6, stop=14)
            phase(U_GB, start=14)

            def merge_a(k, u, i):
                dve.wait_ge(split_hi, 8 + k + 1)
                tt_(tile(sbl[1], k), tile(rwo, k), tile(sbh[1], k).bitcast(F32), ALU.subtract).then_inc(split_lo, 1)
                dve.wait_ge(split_lo, 8 + k + 1)
                dve.wait_ge(unit_done, U_RGO + k + 1)
                dve.wait_ge(g_in[u], 16 * i + 16)
                tt_(tile(rwo, k), bank[u][:, 0:NT], gt[u][:], ALU.mult).then_inc(merged, 1)

            def merge_b(k, u, i):
                dve.wait_ge(unit_done, U_RWO + k + 1)
                dve.wait_ge(g_in[u], 16 * (KT // 2) + 16 * i + 16)
                tt_(tmp[u][:], bank[u][:, 0:NT], gt[u][:], ALU.mult).then_inc(gated, 1)
                dve.wait_ge(gated, k + 1)
                tt_(tile(rwo, k), tile(rwo, k), tmp[u][:], ALU.add).then_inc(merged, 1)
                dve.wait_ge(merged_hi, k + 1)
                tt_(tile(sbl[0], k), tile(rwo, k), tile(sbh[0], k).bitcast(F32), ALU.subtract).then_inc(merged_lo, 1)

            def square_sum(k, u, n):
                dve.wait_ge(x_done, n)
                sq = nsq[u][:, 0, 0:NT]
                tt_(sq, tile(rga, k, NB), tile(rga, k, NB), ALU.mult).then_inc(sq_done, 1)

            def square_add(u, n):
                dve.wait_ge(sq_done, n)
                tt_(acc, acc, nsq[u][:, 0, 0:NT], ALU.add).then_inc(acc_ready, 1)

            def residual(base, squares=None):
                def evict(k, u, i):
                    dve.wait_ge(unit_done, base + k + 1)
                    tt_(tile(rga, k, NB), tile(rga, k, NB), bank[u][:, 0:NT], ALU.add).then_inc(x_done, 1)
                    if squares is not None:
                        square_sum(k, u, squares[0] + k + 1)
                        square_add(u, squares[1] + k + 1)
                return evict

            phase(U_RGO, merge_a)
            phase(U_RWO, merge_b)
            dve.wait_ge(x_back, 16)
            dve.wait_ge(merged_lo, KT)
            dve.memset(acc, 0.0)
            phase(U_WO, residual(U_WO, (0, 0)))
            norm(1, NT, GFFN, (xh, xl))
            n = 0
            for kind, g in FFN_PLAN:
                def hidden_lo(k, u, i, g=g):
                    dve.wait_ge(h_hi, KT * g + k + 1)
                    tt_(tile(sbl[g % 2], k), tmp[u][:], tile(sbh[g % 2], k).bitcast(F32), ALU.subtract).then_inc(h_lo, 1)

                base = U_FFN + n * KT
                if kind == "down":
                    dve.wait_ge(x_done, (g + 1) * KT)
                if n == 7:
                    dve.memset(acc, 0.0)
                phase(base, hidden_lo if kind == "up" else residual(base, (4 * KT, KT) if n == 7 else None))
                n += 1
            dve.wait_ge(pt_mm, 1)
            for k in range(2):
                dve.tensor_copy(pt[:, k, :], bank[4 + k][:, 0:NT]).then_inc(pt_ready, 1)
            dve.wait_ge(x_done, 5 * KT)
            norm(2, NT, GPLE, (xh, xl))

            def embed(k, u, i):
                dve.wait_ge(sg_ready, k + 1)
                dve.wait_ge(embed_mm, k + 1)
                tt_(tmp[u][:], tmp[u][:], bank[2 + u][:, 0:NT], ALU.mult).then_inc(tmp_ready, 1)
                dve.wait_ge(tmp_ready, k + 1)
                tt_(tile(rga, k, NB), tile(rga, k, NB), tmp[u][:], ALU.add).then_inc(x_done, 1)
                square_sum(k, u, 5 * KT + k + 1)
                square_add(u, 2 * KT + k + 1)

            dve.memset(acc, 0.0)
            phase(U_PLE, embed, ahead=False)
            dve.wait_ge(x_done, 6 * KT)
            norm(3, NT, GFIN, None)

        @block.gpsimd
        def _(pool):
            pool.memset(rows[0:NPAR, :], 0.0).then_inc(rows_zero, 1)
            pool.wait_ge(par_ready, 2)
            pool.wait_ge(nrm_lo, 8)
            for view, value in ((s0[:], 0.0), (cum[:], 1.0), (zeros[:], 0.0), (ue[:], 0.0)):
                pool.memset(view, value).then_inc(init_done, 1)

            def masked(p):
                pool.wait_ge(ab_read, 2 * (p + 1))
                if not (isinstance(p, int) and p == 0):
                    pool.wait_ge(yy_mm, 5 * p)
                masks = cst[:, C_LM + CHUNK:C_LM + 6 * CHUNK].rearrange("p (l t) -> p l t", l=5)
                pool.tensor_tensor(am, ab[:].unsqueeze(1).to_broadcast([P, 5, 4, CHUNK]),
                                   masks.unsqueeze(2).to_broadcast([P, 5, 4, CHUNK]), ALU.mult).then_inc(am_ready, 1)

            def samples(p):
                pool.wait_ge(ar_ready, p + 1)
                if not (isinstance(p, int) and p == 0):
                    pool.wait_ge(so_saved, 16 * p)
                pool.tensor_tensor(aex[:], ar[:, 0, samp_all].unsqueeze(1).to_broadcast([P, NB, SAMP]),
                                   cst[:, C_SEQ:C_SEQ + 256].rearrange("p (b t) -> p b t", b=NB), ALU.mult)
                pool.tensor_copy(dg[:, :, HEAD:], ar[:, 1, samp_all].rearrange("p (t b) -> p b t", b=NB))
                pool.tensor_tensor(dg[:, :, 0:HEAD], cst[:, C_ID2:C_ID2 + HEAD].unsqueeze(1).to_broadcast([P, NB, HEAD]),
                                   cum[:, NS * NB:(NS + 1) * NB].unsqueeze(2).to_broadcast([P, NB, HEAD]), ALU.mult)
                pool.wait_ge(turn_read, p + 1)
                own = cst[0:2 * SAMP, C_SQT:C_SQT + NB].unsqueeze(2).to_broadcast([2 * SAMP, NB, HEAD])
                for h in range(2):
                    ins = pool.tensor_tensor(bke[:, h, :].rearrange("p (b j) -> p b j", b=NB),
                                             sbk[:, h * HEAD:(h + 1) * HEAD].unsqueeze(1).to_broadcast([2 * SAMP, NB, HEAD]), own, ALU.mult)
                ins.then_inc(sexp_ready, 1)

            masked(0)
            samples(0)
            with pool.Fori(1, KT) as p:
                masked(p)
                samples(p)


_INS = ['x_prompt', 'x_sample', 'p_prompt', 'p_sample', 'state_rg_h', 'state_rg_conv', 'state_rwkv', 'state_shift',
        'norm_mix', 'w_in', 'conv_w', 'conv_b', 'rg_wa', 'rg_ba', 'rg_wx', 'rg_bx', 'rg_lam', 'w_rg_o', 'mu_shift',
        'rw_w0', 'rw_w2', 'rw_a0', 'rw_a2', 'rw_g2', 'rw_kk', 'rw_ka', 'rw_rk', 'rw_gn_w', 'rw_gn_b', 'w_rw_o', 'w_o',
        'norm_ffn', 'w_up', 'w_down', 'norm_ple', 'w_ple_gate', 'w_ple', 'norm_f']
_OUTS = [("o_y_p", (1, SEQ, D)), ("o_y_s", (NB, NS, D)), ("o_h_p", (1, 1, D)), ("o_conv_p", (1, 1, 3, D)),
         ("o_rwkv_p", (1, 1, D // HEAD, HEAD, HEAD)), ("o_shift_p", (1, 1, D)),
         ("o_h_s", (1, NB, D)), ("o_conv_s", (1, NB, 3, D)), ("o_rwkv_s", (1, NB, D // HEAD, HEAD, HEAD)),
         ("o_shift_s", (1, NB, D))]


def kernel(**inputs):
    import concourse.bacc as _bacc
    from concourse.bass_utils import run_bass_kernel_spmd as _run

    nc = _bacc.Bacc("TRN2", target_bir_lowering=False, num_devices=1, dynamic_dma_scratch_size=1024)
    arrays, aps = {}, {}
    for name in _INS:
        x = np.ascontiguousarray(inputs[name])
        arrays[name] = x
        aps[name] = nc.dram_tensor(name, x.shape, mybir.dt.from_np(x.dtype), kind="ExternalInput").ap()
    arrays["const"] = constants()
    aps["const"] = nc.dram_tensor("const", arrays["const"].shape, F32, kind="ExternalInput").ap()
    for name, shape in _OUTS:
        aps[name] = nc.dram_tensor(name, shape, F32, kind="ExternalOutput").ap()
    program(nc, aps)
    r = _run(nc, [arrays], core_ids=[0])
    return tuple(r.results[0][name] for name, _ in _OUTS)
```
